# Optimizing a Trainium2 kernel written in Bass

```python
import math
import jax
import jax.numpy as jnp
from jax import lax
import numpy as np

"""Hybrid decoder trunk: DEPTH layers of a causal hybrid residual block.

Each layer (sandwich RMSNorm around every sub-layer):
  h += 0.5 * post_norm(SwiGLU_1(pre_norm(h)))          macaron half-step FFN
  h += post_norm(mixer_i(pre_norm(h)))                  token mixing
  h += 0.5 * post_norm(SwiGLU_2(pre_norm(h)))          macaron half-step FFN
  h += post_norm(sigmoid(pre_norm(h) W_g) * (p[i] W_p)) per-layer input embedding
mixer_i for even i: one combined input projection split into
  A) chunked causal gMLP spatial gating (8 groups x 128 ch, chunk 128)
  B) Mamba-2 SSD (16 heads x 64, 2 B/C groups, state 128, conv 4, chunked scan)
  outputs concatenated -> one output projection.
mixer_i for odd i: C) multi-head latent attention (16 heads, low-rank q / kv,
  decoupled shared rotary key), causal, swept in 128-query blocks.
Inputs: x (BATCH, SEQ, D_MODEL) f32, p (DEPTH, BATCH, SEQ, 256) f32,
  positions (BATCH, SEQ) int32, plus per-layer weights.
Output: (BATCH, SEQ, D_MODEL).
"""

D_MODEL = 1024
BATCH = 1
SEQ = 256
DEPTH = 2

PLE_DIM = 256
N_EVEN = (DEPTH + 1) // 2
N_ODD = DEPTH // 2
D_FF = 2816
NORM_EPS = 1e-6
LN_EPS = 1e-5

GM_CHUNK = 128
GM_HEADS = 8
GM_HEAD_DIM = 128
GM_WIDTH = GM_HEADS * GM_HEAD_DIM

SSD_HEAD_DIM = 64
SSD_HEADS = 16
SSD_INNER = SSD_HEADS * SSD_HEAD_DIM
SSD_GROUPS = 2
SSD_STATE = 128
SSD_CONV = 4
SSD_CHUNK = 128
SSD_CONV_CH = SSD_INNER + 2 * SSD_GROUPS * SSD_STATE

HYB_IN = 2 * GM_WIDTH + SSD_INNER + SSD_CONV_CH + SSD_HEADS
HYB_OUT = GM_WIDTH + SSD_INNER

MLA_HEADS = 16
MLA_NOPE = 128
MLA_ROPE = 64
MLA_V = 128
MLA_Q_LORA = 256
MLA_KV_LORA = 128
MLA_QK = MLA_NOPE + MLA_ROPE
MLA_IN = MLA_Q_LORA + MLA_KV_LORA + MLA_ROPE
ROPE_BASE = 10000.0
ATTN_BLOCK = 128

kernel_name = "hybrid_gmlp_ssd_mla_macaron"

def rmsnorm(x, g):
    xf = x.astype(jnp.float32)
    y = xf * lax.rsqrt(jnp.mean(xf * xf, axis=-1, keepdims=True) + NORM_EPS)
    return (y * g.astype(jnp.float32)).astype(x.dtype)

def layernorm(x, g, b):
    xf = x.astype(jnp.float32)
    mu = jnp.mean(xf, axis=-1, keepdims=True)
    xc = xf - mu
    var = jnp.mean(xc * xc, axis=-1, keepdims=True)
    y = xc * lax.rsqrt(var + LN_EPS) * g.astype(jnp.float32) + b.astype(jnp.float32)
    return y.astype(x.dtype)

def swiglu(x, w_in, w_down):
    gate, up = jnp.split(x @ w_in, 2, axis=-1)
    return (jax.nn.silu(gate) * up) @ w_down

def rope_tables(positions):
    inv = 1.0 / (ROPE_BASE ** (jnp.arange(0, MLA_ROPE, 2, dtype=jnp.float32) / MLA_ROPE))
    ang = positions.astype(jnp.float32)[..., None] * inv
    return jnp.cos(ang), jnp.sin(ang)

def apply_rope(x, cos, sin):
    shape = cos.shape[:2] + (1,) * (x.ndim - 3) + cos.shape[2:]
    c = cos.reshape(shape)
    s = sin.reshape(shape)
    x1, x2 = jnp.split(x.astype(jnp.float32), 2, axis=-1)
    return jnp.concatenate([x1 * c - x2 * s, x2 * c + x1 * s], axis=-1).astype(x.dtype)

def gmlp_spatial_gating(uv, ln_g, ln_b, w_s, b_s):
    bsz, seq, _ = uv.shape
    u, v = jnp.split(jax.nn.gelu(uv), 2, axis=-1)
    v = v.reshape(bsz, seq // GM_CHUNK, GM_CHUNK, GM_HEADS, GM_HEAD_DIM)
    v = layernorm(v, ln_g.reshape(GM_HEADS, GM_HEAD_DIM), ln_b.reshape(GM_HEADS, GM_HEAD_DIM))
    causal = jnp.tril(jnp.ones((GM_CHUNK, GM_CHUNK), dtype=bool))
    w = jnp.where(causal[None], w_s, 0).astype(v.dtype)
    mixed = jnp.einsum('hts,bcshd->bcthd', w, v) + b_s.T[None, None, :, :, None]
    return u * mixed.reshape(bsz, seq, GM_WIDTH)

def ssd_chunked_scan(x, dt, a, bmat, cmat):
    bsz, seq, nh, hp = x.shape
    f32 = jnp.float32
    r = nh // SSD_GROUPS
    nc = seq // SSD_CHUNK
    L = SSD_CHUNK
    xd = (x.astype(f32) * dt[..., None]).reshape(bsz, nc, L, SSD_GROUPS, r, hp)
    da = (dt * a).reshape(bsz, nc, L, SSD_GROUPS, r)
    bc = bmat.astype(f32).reshape(bsz, nc, L, SSD_GROUPS, SSD_STATE)
    cc = cmat.astype(f32).reshape(bsz, nc, L, SSD_GROUPS, SSD_STATE)
    a_cs = jnp.cumsum(da, axis=2)
    seg = a_cs[:, :, :, None] - a_cs[:, :, None, :]
    causal = jnp.tril(jnp.ones((L, L), dtype=bool))[:, :, None, None]
    decay = jnp.exp(jnp.where(causal, seg, -jnp.inf))
    cb = jnp.einsum('bclgn,bcsgn->bclsg', cc, bc)
    y_diag = jnp.einsum('bclsgr,bcsgrp->bclgrp', cb[..., None] * decay, xd)
    decay_to_end = jnp.exp(a_cs[:, :, -1:] - a_cs)
    states = jnp.einsum('bclgn,bclgrp->bcgrpn', bc, xd * decay_to_end[..., None])
    chunk_decay = jnp.exp(a_cs[:, :, -1])

    def step(h, inp):
        st, dec = inp
        return h * dec[..., None, None] + st, h

    h0 = jnp.zeros((bsz, SSD_GROUPS, r, hp, SSD_STATE), f32)
    _, prev = lax.scan(step, h0, (jnp.moveaxis(states, 1, 0), jnp.moveaxis(chunk_decay, 1, 0)))
    prev = jnp.moveaxis(prev, 0, 1)
    y_off = jnp.einsum('bclgn,bcgrpn->bclgrp', cc, prev) * jnp.exp(a_cs)[..., None]
    return (y_diag + y_off).reshape(bsz, seq, nh, hp).astype(x.dtype)

def ssd_mixer(zxbcdt, conv_w, conv_b, dt_bias, a_log, d_skip, norm_g):
    bsz, seq, _ = zxbcdt.shape
    z, xbc, dt = jnp.split(zxbcdt, [SSD_INNER, SSD_INNER + SSD_CONV_CH], axis=-1)
    xbc = lax.conv_general_dilated(
        xbc, conv_w[:, None, :], window_strides=(1,), padding=[(SSD_CONV - 1, 0)],
        dimension_numbers=('NWC', 'WIO', 'NWC'), feature_group_count=SSD_CONV_CH) + conv_b
    xbc = jax.nn.silu(xbc)
    xs, bmat, cmat = jnp.split(xbc, [SSD_INNER, SSD_INNER + SSD_GROUPS * SSD_STATE], axis=-1)
    dt = jax.nn.softplus(dt.astype(jnp.float32) + dt_bias.astype(jnp.float32))
    a = -jnp.exp(a_log.astype(jnp.float32))
    xs = xs.reshape(bsz, seq, SSD_HEADS, SSD_HEAD_DIM)
    y = ssd_chunked_scan(xs, dt, a,
                         bmat.reshape(bsz, seq, SSD_GROUPS, SSD_STATE),
                         cmat.reshape(bsz, seq, SSD_GROUPS, SSD_STATE))
    y = (y + d_skip[:, None] * xs).reshape(bsz, seq, SSD_INNER)
    yg = (y * jax.nn.silu(z)).reshape(bsz, seq, SSD_GROUPS, SSD_INNER // SSD_GROUPS)
    yg = rmsnorm(yg, norm_g.reshape(SSD_GROUPS, SSD_INNER // SSD_GROUPS))
    return yg.reshape(bsz, seq, SSD_INNER)

def causal_attention_blocked(q, k, v):
    bsz, seq, nh, dk = q.shape
    nb = seq // ATTN_BLOCK
    scale = dk ** -0.5
    qb = jnp.moveaxis(q.reshape(bsz, nb, ATTN_BLOCK, nh, dk), 1, 0)
    k_pos = jnp.arange(seq)

    def one_block(args):
        qi, blk = args
        s = jnp.einsum('bthd,bshd->bhts', qi, k).astype(jnp.float32) * scale
        q_pos = blk * ATTN_BLOCK + jnp.arange(ATTN_BLOCK)
        s = jnp.where(k_pos[None, :] <= q_pos[:, None], s, -jnp.inf)
        pr = jax.nn.softmax(s, axis=-1).astype(v.dtype)
        return jnp.einsum('bhts,bshd->bthd', pr, v)

    out = lax.map(one_block, (qb, jnp.arange(nb)))
    return jnp.moveaxis(out, 0, 1).reshape(bsz, seq, nh, v.shape[-1])

def mla_attention(h, w_in, q_norm_g, kv_norm_g, w_uq, w_ukv, w_out, cos, sin):
    bsz, seq, _ = h.shape
    c_q, c_kv, k_rope = jnp.split(h @ w_in, [MLA_Q_LORA, MLA_Q_LORA + MLA_KV_LORA], axis=-1)
    q = (rmsnorm(c_q, q_norm_g) @ w_uq).reshape(bsz, seq, MLA_HEADS, MLA_QK)
    q_nope, q_rope = jnp.split(q, [MLA_NOPE], axis=-1)
    q = jnp.concatenate([q_nope, apply_rope(q_rope, cos, sin)], axis=-1)
    kv = (rmsnorm(c_kv, kv_norm_g) @ w_ukv).reshape(bsz, seq, MLA_HEADS, MLA_NOPE + MLA_V)
    k_nope, v = jnp.split(kv, [MLA_NOPE], axis=-1)
    k_rope = apply_rope(k_rope, cos, sin)
    k = jnp.concatenate(
        [k_nope, jnp.broadcast_to(k_rope[:, :, None, :], (bsz, seq, MLA_HEADS, MLA_ROPE))], axis=-1)
    o = causal_attention_blocked(q, k, v)
    return o.reshape(bsz, seq, MLA_HEADS * MLA_V) @ w_out

def setup_inputs(seed: int = 0) -> dict:
    key = jax.random.key(seed)
    ks = iter(jax.random.split(key, 48))
    f32 = jnp.float32

    def nrm(shape, scale):
        return jax.random.normal(next(ks), shape, f32) * scale

    def gain(shape):
        return 1.0 + nrm(shape, 0.02)

    x = nrm((BATCH, SEQ, D_MODEL), 1.0)
    p = nrm((DEPTH, BATCH, SEQ, PLE_DIM), 1.0)
    start = jax.random.randint(next(ks), (BATCH, 1), 0, 4096, dtype=jnp.int32)
    positions = start + jnp.arange(SEQ, dtype=jnp.int32)[None, :]

    ffn1_pre_g = gain((DEPTH, D_MODEL))
    ffn1_w_in = nrm((DEPTH, D_MODEL, 2 * D_FF), D_MODEL ** -0.5)
    ffn1_w_down = nrm((DEPTH, D_FF, D_MODEL), D_FF ** -0.5)
    ffn1_post_g = gain((DEPTH, D_MODEL))
    mix_pre_g = gain((DEPTH, D_MODEL))
    mix_post_g = gain((DEPTH, D_MODEL))
    ffn2_pre_g = gain((DEPTH, D_MODEL))
    ffn2_w_in = nrm((DEPTH, D_MODEL, 2 * D_FF), D_MODEL ** -0.5)
    ffn2_w_down = nrm((DEPTH, D_FF, D_MODEL), D_FF ** -0.5)
    ffn2_post_g = gain((DEPTH, D_MODEL))
    ple_pre_g = gain((DEPTH, D_MODEL))
    ple_w_gate = nrm((DEPTH, D_MODEL, D_MODEL), D_MODEL ** -0.5)
    ple_w_proj = nrm((DEPTH, PLE_DIM, D_MODEL), PLE_DIM ** -0.5)
    ple_post_g = gain((DEPTH, D_MODEL))

    hyb_w_in = nrm((N_EVEN, D_MODEL, HYB_IN), D_MODEL ** -0.5)
    gm_ln_g = gain((N_EVEN, GM_WIDTH))
    gm_ln_b = nrm((N_EVEN, GM_WIDTH), 0.02)
    gm_w_s = nrm((N_EVEN, GM_HEADS, GM_CHUNK, GM_CHUNK), GM_CHUNK ** -0.5)
    gm_b_s = gain((N_EVEN, GM_HEADS, GM_CHUNK))
    ssd_conv_w = nrm((N_EVEN, SSD_CONV, SSD_CONV_CH), SSD_CONV ** -0.5)
    ssd_conv_b = nrm((N_EVEN, SSD_CONV_CH), 0.02)
    dt0 = jnp.exp(jax.random.uniform(next(ks), (N_EVEN, SSD_HEADS), f32,
                                     math.log(1e-3), math.log(1e-1)))
    ssd_dt_bias = dt0 + jnp.log(-jnp.expm1(-dt0))
    ssd_a_log = jnp.log(jax.random.uniform(next(ks), (N_EVEN, SSD_HEADS), f32, 1.0, 16.0))
    ssd_d = gain((N_EVEN, SSD_HEADS))
    ssd_norm_g = gain((N_EVEN, SSD_INNER))
    hyb_w_out = nrm((N_EVEN, HYB_OUT, D_MODEL), HYB_OUT ** -0.5)

    mla_w_in = nrm((N_ODD, D_MODEL, MLA_IN), D_MODEL ** -0.5)
    mla_q_norm_g = gain((N_ODD, MLA_Q_LORA))
    mla_kv_norm_g = gain((N_ODD, MLA_KV_LORA))
    mla_w_uq = nrm((N_ODD, MLA_Q_LORA, MLA_HEADS * MLA_QK), MLA_Q_LORA ** -0.5)
    mla_w_ukv = nrm((N_ODD, MLA_KV_LORA, MLA_HEADS * (MLA_NOPE + MLA_V)), MLA_KV_LORA ** -0.5)
    mla_w_out = nrm((N_ODD, MLA_HEADS * MLA_V, D_MODEL), (MLA_HEADS * MLA_V) ** -0.5)

    return {
        "x": x, "p": p, "positions": positions,
        "ffn1_pre_g": ffn1_pre_g, "ffn1_w_in": ffn1_w_in, "ffn1_w_down": ffn1_w_down,
        "ffn1_post_g": ffn1_post_g, "mix_pre_g": mix_pre_g, "mix_post_g": mix_post_g,
        "ffn2_pre_g": ffn2_pre_g, "ffn2_w_in": ffn2_w_in, "ffn2_w_down": ffn2_w_down,
        "ffn2_post_g": ffn2_post_g, "ple_pre_g": ple_pre_g, "ple_w_gate": ple_w_gate,
        "ple_w_proj": ple_w_proj, "ple_post_g": ple_post_g,
        "hyb_w_in": hyb_w_in, "gm_ln_g": gm_ln_g, "gm_ln_b": gm_ln_b, "gm_w_s": gm_w_s,
        "gm_b_s": gm_b_s, "ssd_conv_w": ssd_conv_w, "ssd_conv_b": ssd_conv_b,
        "ssd_dt_bias": ssd_dt_bias, "ssd_a_log": ssd_a_log, "ssd_d": ssd_d,
        "ssd_norm_g": ssd_norm_g, "hyb_w_out": hyb_w_out,
        "mla_w_in": mla_w_in, "mla_q_norm_g": mla_q_norm_g, "mla_kv_norm_g": mla_kv_norm_g,
        "mla_w_uq": mla_w_uq, "mla_w_ukv": mla_w_ukv, "mla_w_out": mla_w_out,
    }

def reference(x, p, positions,
              ffn1_pre_g, ffn1_w_in, ffn1_w_down, ffn1_post_g, mix_pre_g, mix_post_g,
              ffn2_pre_g, ffn2_w_in, ffn2_w_down, ffn2_post_g,
              ple_pre_g, ple_w_gate, ple_w_proj, ple_post_g,
              hyb_w_in, gm_ln_g, gm_ln_b, gm_w_s, gm_b_s,
              ssd_conv_w, ssd_conv_b, ssd_dt_bias, ssd_a_log, ssd_d, ssd_norm_g, hyb_w_out,
              mla_w_in, mla_q_norm_g, mla_kv_norm_g, mla_w_uq, mla_w_ukv, mla_w_out):
    cos, sin = rope_tables(positions)
    h = x
    for i in range(DEPTH):
        j = i // 2
        f = swiglu(rmsnorm(h, ffn1_pre_g[i]), ffn1_w_in[i], ffn1_w_down[i])
        h = h + 0.5 * rmsnorm(f, ffn1_post_g[i])
        hn = rmsnorm(h, mix_pre_g[i])
        if i % 2 == 0:
            uv, zxbcdt = jnp.split(hn @ hyb_w_in[j], [2 * GM_WIDTH], axis=-1)
            ya = gmlp_spatial_gating(uv, gm_ln_g[j], gm_ln_b[j], gm_w_s[j], gm_b_s[j])
            yb = ssd_mixer(zxbcdt, ssd_conv_w[j], ssd_conv_b[j], ssd_dt_bias[j],
                           ssd_a_log[j], ssd_d[j], ssd_norm_g[j])
            mixed = jnp.concatenate([ya, yb], axis=-1) @ hyb_w_out[j]
        else:
            mixed = mla_attention(hn, mla_w_in[j], mla_q_norm_g[j], mla_kv_norm_g[j],
                                  mla_w_uq[j], mla_w_ukv[j], mla_w_out[j], cos, sin)
        h = h + rmsnorm(mixed, mix_post_g[i])
        f = swiglu(rmsnorm(h, ffn2_pre_g[i]), ffn2_w_in[i], ffn2_w_down[i])
        h = h + 0.5 * rmsnorm(f, ffn2_post_g[i])
        gate = jax.nn.sigmoid(rmsnorm(h, ple_pre_g[i]) @ ple_w_gate[i])
        h = h + rmsnorm(gate * (p[i] @ ple_w_proj[i]), ple_post_g[i])
    return h


_drawn_inputs = setup_inputs


def setup_inputs(seed=0):
    import zlib

    import numpy as np

    out = dict(_drawn_inputs(seed))
    spreads = {}
    factors = {'ffn1_pre_g': 3.554,
     'ffn1_post_g': 4.77,
     'mix_post_g': 3.463,
     'ffn2_pre_g': 5.514,
     'ffn2_post_g': 8.0,
     'ple_pre_g': 8.0,
     'ple_post_g': 4.179,
     'gm_ln_g': 8.0,
     'gm_ln_b': 8.0,
     'gm_b_s': 8.0,
     'ssd_conv_b': 3.652,
     'ssd_d': 21.427,
     'ssd_norm_g': 5.789,
     'mla_q_norm_g': 8.0,
     'mla_kv_norm_g': 4.808}
    for name, (base, spread) in spreads.items():
        noise = np.random.default_rng([zlib.crc32(name.encode()), seed]).standard_normal(out[name].shape)
        drawn = base * np.exp(spread * noise) if base else spread * noise
        out[name] = jnp.asarray(drawn.astype(out[name].dtype))
    for name, factor in factors.items():
        out[name] = (out[name] * factor).astype(out[name].dtype)
    return out
```

```python
from contextlib import ExitStack

import numpy as np

import concourse.bass as bass
from concourse import mybir

D = 1024
SEQ = 256
P = 128
D_FF = 2816
PLE = 256
BANK = 512
UNIT = 2048
RING = 3
KT = D // P
EPS = 1e-6
LN_EPS = 1e-5
CHUNK = 512
FULL = D_FF // CHUNK
FFN_UNITS = 33
GM_W = 1024
SSD_IN = 1024
CONV_CH = 1536
HEADS = 16
NOPE, ROPE, VD = 128, 64, 128
Q_LORA, KV_LORA = 256, 128
SCALE = float((NOPE + ROPE) ** -0.5)
ROPE_BASE = 10000.0
NEG = -1.0e30

STAGES = [("ffn", 0), ("hyb", 0), ("ffn", 1), ("ple", 0), ("ffn", 2), ("mla", 0), ("ffn", 3), ("ple", 1)]
N_UNITS = {"ffn": FFN_UNITS, "hyb": 26, "ple": 5, "mla": 15}


def hybrid_trunk(nc, stages, a, out):
    f32, f32r, bf16, i32 = mybir.dt.float32, mybir.dt.float32r, mybir.dt.bfloat16, mybir.dt.int32
    ALU = mybir.AluOpType
    ACT = mybir.ActivationFunctionType

    first = {}
    n_units = 0
    for s, (kind, _) in enumerate(stages):
        first[s] = n_units
        n_units += N_UNITS[kind]
    NS = len(stages)

    ctx = ExitStack()
    with ctx:
        base = 16512
        at = [base]

        def place(name, shape, dt=f32, offset=None):
            size = int(np.prod(shape[1:])) * (2 if dt == bf16 else 4)
            if offset is None:
                offset = at[0]
                at[0] += (size + 31) // 32 * 32
            return nc.alloc_sbuf_tensor_at(name, shape, dt, offset=offset)

        raw = place("raw", [P, RING, UNIT])
        WH = place("WH", [P, RING, UNIT], f32r)
        WL = place("WL", [P, RING, UNIT], f32r)
        x_at = at[0]
        XH = place("XH", [P, KT, SEQ], f32r)
        XL = place("XL", [P, KT, SEQ], f32r)
        c_at = at[0]
        CH = place("CH", [P, 16, SEQ], f32r)
        CL = place("CL", [P, 16, SEQ], f32r)
        h = place("h", [P, 2, D])
        PG = place("PG", [P, D])
        QG = place("QG", [P, D])
        hn_at = at[0]
        hn = place("hn", [P, 2, D])
        junk = place("junk", [P, 2, D])
        ident = place("ident", [P, P])
        zeros = place("zeros", [P, BANK], bf16)
        stat = place("stat", [P, 128])
        nhalf = place("nhalf", [P, 8])
        tri = place("tri", [P, P])
        cmask = place("cmask", [P, 2 * P])
        cosT = place("cosT", [P, 2, ROPE // 2])
        sinT = place("sinT", [P, 2, ROPE // 2])
        small = place("small", [P, 256])
        s_at = at[0]
        end = 229344

        sg = place("sg", [P, 2, CHUNK], offset=s_at)
        act_h = place("act_h", [P, 2, CHUNK], offset=s_at + 4096)
        HH = place("HH", [P, 4, SEQ], f32r, offset=c_at)
        HL = place("HL", [P, 4, SEQ], f32r, offset=c_at + 4096)
        gsb = place("gsb", [P, 2, D], offset=s_at + 8192)
        p_raw = place("p_raw", [P, 2, SEQ], offset=c_at + 8192)
        p_hi = place("p_hi", [P, 2, SEQ], f32r, offset=c_at + 8192 + 2048)
        p_lo = place("p_lo", [P, 2, SEQ], f32r, offset=c_at + 8192 + 4096)

        PS = ctx.enter_context(nc.psum_tensor("PS", [P, 8, BANK], f32))
        A, B, C, T = 0, 1, 2, 3

        def acc(t):
            return PS[:, 4 + 2 * t:6 + 2 * t, :]

        sems = {}

        def sem(name):
            if name not in sems:
                sems[name] = ctx.enter_context(nc.semaphore(name))
            return sems[name]

        for name in ("raw0", "raw1", "raw2", "w_hi", "w_lo", "w_used", "x_loaded", "consts", "pg", "qg",
                     "out_done", "ple_done", "post_sq", "post_rs", "h_new", "pre_sq", "pre_rs", "hn_done",
                     "x_tr", "x_hi", "x_lo", "gate", "silu", "up", "acted", "h_tr", "h_hi", "h_lo",
                     "act_chain", "dve_chain", "pool_chain", "stored"):
            sem(name)

        chains = {"dve_chain": 0, "pool_chain": 0}

        def link(eng, name, ins):
            chains[name] += 1
            ins.then_inc(sem(name), 1)
            eng.wait_ge(sem(name), chains[name])

        def unit_at(n, k, step):
            return n if k is None else k * step + n

        def load_unit(sp, n, k=None, step=0):
            if n >= RING:
                sp.wait_ge(sem("w_hi"), unit_at(n - RING + 1, k, step))
                sp.wait_ge(sem("w_lo"), unit_at(n - RING + 1, k, step))
            if k is None:
                src = a["stream"][n, :, :]
            else:
                src = a["stream"][bass.ds(k * step + n, 1), :, :].rearrange("a p n -> (a p) n")
            sp.dma_start(raw[:, n % RING, :], src).then_inc(sem(f"raw{n % RING}"), 16)

        def split_hi(act, n, k=None, step=0):
            if n >= n_units:
                return
            rounds = 16 * (n // RING + 1)
            act.wait_ge(sem(f"raw{n % RING}"), rounds if k is None else k * (16 * step // RING) + rounds)
            if n >= RING:
                act.wait_ge(sem("w_used"), unit_at(n - RING + 1, k, step))
            act.activation(WH[:, n % RING, :], raw[:, n % RING, :], ACT.Copy).then_inc(sem("w_hi"), 1)

        def split_lo(dve, n, k=None, step=0):
            if n >= n_units:
                return
            dve.wait_ge(sem("w_hi"), unit_at(n + 1, k, step))
            dve.tensor_tensor(WL[:, n % RING, :], raw[:, n % RING, :], WH[:, n % RING, :],
                              ALU.subtract).then_inc(sem("w_lo"), 1)

        def splitter(eng, split):
            done = [0]

            def split_to(n):
                while done[0] <= n:
                    split(eng, done[0])
                    done[0] += 1
            return done, split_to

        def whole(tile, n):
            return tile[:, n % RING, :]

        def product(pe, out_ap, xh, xl, wh, wl, start, stop):
            pe.matmul(out_ap, xh, wh, start=start, stop=False)
            pe.matmul(out_ap, xl, wh, start=False, stop=False)
            return pe.matmul(out_ap, xh, wl, start=False, stop=stop)

        def tok(t):
            return slice(t * P, (t + 1) * P)

        def col(s, t, what):
            c = (2 * s + t) * 4 + what
            return stat[:, c:c + 1]

        SQ, RS = 0, 1

        def source(s, t):
            if stages[s][0] == "ple":
                return gsb[:, t, :], sem("ple_done"), 2 * sum(k == "ple" for k, _ in stages[:s]) + t + 1
            if t:
                return acc(t), sem("w_used"), first[s] + N_UNITS[stages[s][0]]
            return acc(t), sem("out_done"), 1 + sum(k != "ple" for k, _ in stages[:s])

        def post_square(act, s, t):
            src, ready, value = source(s, t)
            act.wait_ge(ready, value)
            view = junk[:, t, :]
            if stages[s][0] != "ple":
                view = view.rearrange("p (a b) -> p a b", a=2)
            act.activation(view, src, ACT.Square, scale=1.0 / 32, accum_out=col(s, t, 2 + SQ))\
               .then_inc(sem("post_sq"), 1)

        def h_ready(eng, s, t):
            if s:
                eng.wait_ge(sem("h_new"), 2 * (s - 1) + t + 1)
            else:
                eng.wait_ge(sem("x_loaded"), 16)

        def pre_square(act, s, t):
            h_ready(act, s, t)
            act.activation(junk[:, t, :], h[:, t, :], ACT.Square, scale=1.0 / 32, accum_out=col(s, t, SQ))\
               .then_inc(sem("pre_sq"), 1)

        def inverse_rms(pool, s, t, what, factor, done):
            f = 1.0 / factor ** 2
            link(pool, "pool_chain", pool.tensor_scalar(col(s, t, what + RS), col(s, t, what + SQ), f, f * EPS,
                                                        ALU.mult, ALU.add))
            pool.tensor_tensor(col(s, t, what + RS), col(s, t, what + RS), nhalf[:, 0:1], ALU.pow)\
                .then_inc(sem(done), 1)

        def update_h(dve, s, t):
            src, ready, value = source(s, t)
            dve.wait_ge(sem("post_rs"), 2 * s + t + 1)
            if t == 0:
                dve.wait_ge(sem("pg"), 16 * (s + 1))
            y, g = hn[:, t, :], PG[:, :]
            if stages[s][0] != "ple":
                y, g = (v.rearrange("p (a b) -> p a b", a=2) for v in (y, g))
            link(dve, "dve_chain", dve.scalar_tensor_tensor(y, src, col(s, t, 2 + RS), g, ALU.mult, ALU.mult))
            dve.tensor_tensor(h[:, t, :], h[:, t, :], hn[:, t, :], ALU.add).then_inc(sem("h_new"), 1)

        def normed(dve, s, t):
            dve.wait_ge(sem("pre_rs"), 2 * s + t + 1)
            if t == 0:
                dve.wait_ge(sem("qg"), 16 * (s + 1))
            dve.scalar_tensor_tensor(hn[:, t, :], h[:, t, :], col(s, t, RS), QG[:, :], ALU.mult, ALU.mult)\
               .then_inc(sem("hn_done"), 1)

        def transpose_x(pe, s, t):
            pe.wait_ge(sem("hn_done"), 2 * s + t + 1)
            for kt in range(KT):
                ins = pe.transpose(PS[:, 2 * t + kt // 4, (kt % 4) * P:(kt % 4 + 1) * P],
                                   hn[:, t, kt * P:(kt + 1) * P], ident[:, :])
            ins.then_inc(sem("x_tr"), 1)

        def x_bank(t):
            return PS[:, 2 * t:2 * t + 2, :].rearrange("p a (k n) -> p (a k) n", n=P)

        def x_high(act, s, t):
            act.wait_ge(sem("x_tr"), 2 * s + t + 1)
            act.activation(XH[:, :, tok(t)], x_bank(t), ACT.Copy).then_inc(sem("x_hi"), 1)

        def x_low(dve, s, t):
            dve.wait_ge(sem("x_hi"), 2 * s + t + 1)
            dve.tensor_tensor(XL[:, :, tok(t)], x_bank(t), XH[:, :, tok(t)], ALU.subtract)\
               .then_inc(sem("x_lo"), 1)

        def boundary_act(act, s, split_to):
            for t in range(2):
                if s:
                    post_square(act, s - 1, t)
            if s == NS:
                return
            for t in range(2):
                pre_square(act, s, t)
            for t in range(2):
                x_high(act, s, t)

        def boundary_dve(dve, s, split_to):
            if s:
                for t in range(2):
                    update_h(dve, s - 1, t)
            if s == NS:
                return
            for t in range(2):
                normed(dve, s, t)
            for t in range(2):
                x_low(dve, s, t)

        def boundary_pool(pool, s):
            if s:
                factor = 0.5 if stages[s - 1][0] == "ffn" else 1.0
                for t in range(2):
                    pool.wait_ge(sem("post_sq"), 2 * (s - 1) + t + 1)
                    inverse_rms(pool, s - 1, t, 2, factor, "post_rs")
            if s == NS:
                return
            for t in range(2):
                pool.wait_ge(sem("pre_sq"), 2 * s + t + 1)
                inverse_rms(pool, s, t, 0, 1.0, "pre_rs")
            pool.dma_start(PG[:, :], a["post_g"][s, :].partition_broadcast(P)).then_inc(sem("pg"), 16)
            if s + 1 < NS:
                pool.wait_ge(sem("hn_done"), 2 * s + 2)
                pool.dma_start(QG[:, :], a["pre_g"][s + 1, :].partition_broadcast(P)).then_inc(sem("qg"), 16)

        def ffn_chunk_pe(pe, f, s, g, c, k=None, half=False):
            def n2(t):
                v = 12 * f + 2 * c + t + 1
                return v if k is None else k * 2 + v

            def n1(d=0):
                v = 6 * f + c + 1 - d
                return v if k is None else k + v

            width = CHUNK // 2 if half else CHUNK
            units = 1 if half else 2
            per = KT // units
            for which, banks, name in ((0, (A, B), "gate"), (1, (C, A), "up")):
                for j in range(units):
                    n = g + which * units + j
                    pe.wait_ge(sem("w_lo"), unit_at(n + 1, k, 6))
                    wh = whole(WH, n).rearrange("p (k n) -> p k n", k=per)
                    wl = whole(WL, n).rearrange("p (k n) -> p k n", k=per)
                    for t in range(2):
                        if which == 0 and j == 0 and c == 0 and k is None:
                            pe.wait_ge(sem("x_lo"), 2 * s + t + 1)
                        if which == 1 and j == 0 and t == 0:
                            if not (c == 0 and k is None):
                                pe.wait_ge(sem("h_lo"), n1(1))
                            pe.wait_ge(sem("silu"), n2(0))
                        for q in range(per):
                            kt = j * per + q
                            ins = product(pe, PS[:, banks[t], 0:width], XH[:, kt, tok(t)], XL[:, kt, tok(t)],
                                          wh[:, q, :], wl[:, q, :], kt == 0, kt == KT - 1)
                        if t == 1:
                            ins.then_inc(sem("w_used"), 1)
                        elif j == units - 1:
                            ins.then_inc(sem(name), 1)
            return n2, n1

        def ffn_down_pe(pe, s, g, k=None, kts=4, last=False):
            for j in range(kts // 2):
                n = g + j
                pe.wait_ge(sem("w_lo"), unit_at(n + 1, k, 6))
                wh = whole(WH, n).rearrange("p (k n) -> p k n", k=2)
                wl = whole(WL, n).rearrange("p (k n) -> p k n", k=2)
                for t in range(2):
                    for c in range(2):
                        for q in range(2):
                            kt = 2 * j + q
                            ins = product(pe, PS[:, 4 + 2 * t + c, :], HH[:, kt, tok(t)], HL[:, kt, tok(t)],
                                          wh[:, q, c * BANK:(c + 1) * BANK], wl[:, q, c * BANK:(c + 1) * BANK],
                                          False, last and q == 1)
                    if t == 1:
                        ins.then_inc(sem("w_used"), 1)
                    elif last:
                        ins.then_inc(sem("out_done"), 1)

        def ffn_transpose_pe(pe, n2, kts=4):
            for t in range(2):
                pe.wait_ge(sem("acted"), n2(t))
            for q in range(kts):
                for t in range(2):
                    ins = pe.transpose(PS[:, C + q // 2, (q % 2) * SEQ + t * P:(q % 2) * SEQ + (t + 1) * P],
                                       act_h[:, t, q * P:(q + 1) * P], ident[:, :])
            ins.then_inc(sem("h_tr"), 1)

        def ffn_pe(pe, s):
            f, u = stages[s][1], first[s]
            n2, n1 = ffn_chunk_pe(pe, f, s, u, 0)
            ffn_transpose_pe(pe, n2)
            for b in range(4, 8):
                pe.matmul(PS[:, b, :], zeros[:, 0:P], zeros[:, :], start=True, stop=False)
            with pe.Fori(0, FULL - 1) as k:
                n2, n1 = ffn_chunk_pe(pe, f, s, u + 4, 1, k)
                ffn_down_pe(pe, s, u + 8, k)
                ffn_transpose_pe(pe, n2)
            g = u + 4 + 6 * (FULL - 1)
            n2, n1 = ffn_chunk_pe(pe, f, s, g, FULL, half=True)
            ffn_down_pe(pe, s, g + 2)
            ffn_transpose_pe(pe, n2, 2)
            pe.wait_ge(sem("h_lo"), n1())
            ffn_down_pe(pe, s, g + 4, kts=2, last=True)

        def ffn_product_done(eng, name, f, c, t, n, k):
            if t == 0:
                eng.wait_ge(sem(name), unit_at(6 * f + c + 1, k, 1))
            else:
                eng.wait_ge(sem("w_used"), unit_at(n + 1, k, 6))

        def ffn_silu(act, f, c, n, k=None, width=CHUNK):
            for t in range(2):
                v = 12 * f + 2 * c + t + 1
                ffn_product_done(act, "gate", f, c, t, n, k)
                if v > 2:
                    act.wait_ge(sem("acted"), v - 2 if k is None else k * 2 + (v - 2))
                act.activation(sg[:, t, 0:width], PS[:, (A, B)[t], 0:width], ACT.Silu).then_inc(sem("silu"), 1)

        def h_bank(kts):
            return PS[:, C:C + (kts + 1) // 2, :]

        def h_tile(tile, kts):
            return tile[:, 0:kts, :].rearrange("p (a k) n -> p a (k n)", k=2)

        def ffn_high(act, f, c, k=None, kts=4):
            v = 6 * f + c + 1
            act.wait_ge(sem("h_tr"), v if k is None else k + v)
            act.activation(h_tile(HH, kts), h_bank(kts), ACT.Copy).then_inc(sem("h_hi"), 1)

        def ffn_low(dve, f, c, k=None, kts=4):
            v = 6 * f + c + 1
            dve.wait_ge(sem("h_hi"), v if k is None else k + v)
            dve.tensor_tensor(h_tile(HL, kts), h_bank(kts), h_tile(HH, kts), ALU.subtract)\
               .then_inc(sem("h_lo"), 1)

        def ffn_mult(dve, f, c, n, k=None, width=CHUNK):
            for t in range(2):
                ffn_product_done(dve, "up", f, c, t, n, k)
                if t == 0 and 6 * f + c > 0:
                    w = 6 * f + c
                    dve.wait_ge(sem("h_tr"), w if k is None else k + w)
                dve.tensor_tensor(act_h[:, t, 0:width], PS[:, (C, A)[t], 0:width], sg[:, t, 0:width],
                                  ALU.mult).then_inc(sem("acted"), 1)

        def ffn_act(act, s, done, split_to):
            f, u = stages[s][1], first[s]
            split_to(u + 3)
            ffn_silu(act, f, 0, u + 1)
            split_to(u + 5)
            ffn_high(act, f, 0)
            with act.Fori(0, FULL - 1) as k:
                g = u + 4
                split_hi(act, g + 2, k, 6)
                split_hi(act, g + 3, k, 6)
                ffn_silu(act, f, 1, g + 1, k)
                for j in range(4, 8):
                    split_hi(act, g + j, k, 6)
                ffn_high(act, f, 1, k)
            g = u + 4 + 6 * (FULL - 1)
            done[0] = g + 2
            split_to(g + 2)
            ffn_silu(act, f, FULL, g, width=CHUNK // 2)
            split_to(g + 4)
            if s + 1 < NS and stages[s + 1][0] == "ple":
                act.wait_ge(sem("p_loaded"), 16 * (stages[s + 1][1] + 1))
                act.activation(p_hi[:, :, :], p_raw[:, :, :], ACT.Copy).then_inc(sem("p_hi"), 1)
            split_to(g + 5)
            ffn_high(act, f, FULL, kts=2)
            split_to(g + 6)

        def ffn_dve(dve, s, done, split_to):
            f, u = stages[s][1], first[s]
            split_to(u + 4)
            ffn_mult(dve, f, 0, u + 3)
            split_to(u + 5)
            ffn_low(dve, f, 0)
            with dve.Fori(0, FULL - 1) as k:
                g = u + 4
                for j in range(2, 7):
                    split_lo(dve, g + j, k, 6)
                ffn_mult(dve, f, 1, g + 3, k)
                split_lo(dve, g + 7, k, 6)
                ffn_low(dve, f, 1, k)
            g = u + 4 + 6 * (FULL - 1)
            done[0] = g + 2
            split_to(g + 4)
            ffn_mult(dve, f, FULL, g + 1, width=CHUNK // 2)
            if s + 1 < NS and stages[s + 1][0] == "ple":
                dve.wait_ge(sem("p_hi"), stages[s + 1][1] + 1)
                dve.tensor_tensor(p_lo[:, :, :], p_raw[:, :, :], p_hi[:, :, :], ALU.subtract)\
                   .then_inc(sem("p_lo"), 1)
            split_to(g + 5)
            ffn_low(dve, f, FULL, kts=2)
            split_to(g + 6)

        def ffn_pool(pool, s):
            if s + 1 < NS and stages[s + 1][0] == "ple":
                h_ready(pool, s, 1)
                pool.dma_start(p_raw[:, :, :], a["p_t"][stages[s + 1][1]].rearrange("(k p) n -> p k n", p=P))\
                    .then_inc(sem("p_loaded"), 16)

        def ple_ahead_pe(pe, s):
            i, u = stages[s][1], first[s]
            pe.wait_ge(sem("p_lo"), i + 1)
            pe.wait_ge(sem("w_lo"), u + 1)
            wh = whole(WH, u).rearrange("p (k n) -> p k n", k=2)
            wl = whole(WL, u).rearrange("p (k n) -> p k n", k=2)
            for t in range(2):
                h_ready(pe, s, t)
                for c in range(2):
                    for q in range(2):
                        ins = product(pe, PS[:, 4 + 2 * t + c, :], p_hi[:, q, tok(t)], p_lo[:, q, tok(t)],
                                      wh[:, q, c * BANK:(c + 1) * BANK], wl[:, q, c * BANK:(c + 1) * BANK],
                                      q == 0, q == 1)
            ins.then_inc(sem("w_used"), 1)

        def ple_pe(pe, s):
            u = first[s] + 1
            for j in range(4):
                n = u + j
                pe.wait_ge(sem("w_lo"), n + 1)
                wh = whole(WH, n).rearrange("p (k n) -> p k n", k=2)
                wl = whole(WL, n).rearrange("p (k n) -> p k n", k=2)
                for t in range(2):
                    if j == 0:
                        pe.wait_ge(sem("x_lo"), 2 * s + t + 1)
                    for c in range(2):
                        for q in range(2):
                            kt = 2 * j + q
                            ins = product(pe, PS[:, 2 * t + c, :], XH[:, kt, tok(t)], XL[:, kt, tok(t)],
                                          wh[:, q, c * BANK:(c + 1) * BANK], wl[:, q, c * BANK:(c + 1) * BANK],
                                          kt == 0, kt == KT - 1)
                    if t == 1:
                        ins.then_inc(sem("w_used"), 1)
                    elif j == 3:
                        ins.then_inc(sem("ple_gate"), 1)

        def ple_act(act, s, done, split_to):
            i, u = stages[s][1], first[s]
            split_to(u + 6)
            for t in range(2):
                if t == 0:
                    act.wait_ge(sem("ple_gate"), i + 1)
                else:
                    act.wait_ge(sem("w_used"), u + 5)
                act.activation(gsb[:, t, :].rearrange("p (a b) -> p a b", a=2), PS[:, 2 * t:2 * t + 2, :],
                               ACT.Sigmoid).then_inc(sem("ple_sig"), 1)

        def ple_dve(dve, s, done, split_to):
            i, u = stages[s][1], first[s]
            split_to(u + 6)
            for t in range(2):
                dve.wait_ge(sem("ple_sig"), 2 * i + t + 1)
                g = gsb[:, t, :].rearrange("p (a b) -> p a b", a=2)
                dve.tensor_tensor(g, acc(t), g, ALU.mult).then_inc(sem("ple_done"), 1)

        for name in ("p_loaded", "p_hi", "p_lo", "ple_gate", "ple_sig"):
            sem(name)

        XBC, Z, V, UU = (0, 1, 2), (3, 4), (5, 6), (7, 8)
        P0, P1, P2, CT = 0, 4, 6, 2
        PAIR = [P0, P1, P2, P0, P2, P0, P1, P2, P0]
        NCH = CONV_CH // P
        GH = 8
        STATE = 128

        def pair(b):
            return PS[:, b:b + 2, :]

        def flat_pair(b):
            return pair(b).rearrange("p a n -> p (a n)")

        o = s_at
        cx = place("cx", [P, NCH, SEQ + 3], offset=o); o += NCH * (SEQ + 3) * 4 + 16
        xs = place("xs", [P, 2, SSD_IN], offset=o); o += 8192
        xd = place("xd", [P, 2, SSD_IN], offset=o); o += 8192
        zs = place("zs", [P, 2, SSD_IN], offset=o); o += 8192
        Eg = place("Eg", [P, 2, GH, P], offset=o); o += 8192
        cbm = place("cbm", [P, 4, P], offset=o); o += 2048
        sm_at = o
        sm = place("sm", [P, 512], offset=o); o += 2048
        Btok = place("Btok", [P, 2 * STATE], offset=o); o += 1024
        assert o <= end, o
        vt = hn
        gm_g = place("gm_g", [P, GM_W], offset=c_at)
        gm_b = place("gm_b", [P, GM_W], offset=c_at + 4096)
        dt_w = place("dt_w", [P, KT, HEADS], offset=c_at + 16384)
        dt_hi = place("dt_hi", [P, KT, HEADS], f32r, offset=c_at + 16384 + 512)
        dt_lo = place("dt_lo", [P, KT, HEADS], f32r, offset=c_at + 16384 + 1024)
        wsT = place("wsT", [P, 8, P], offset=c_at + 16384 + 4096)
        ca = place("ca", [P, 4, SEQ], offset=c_at + 8192)
        xde = place("xde", [P, SSD_IN], offset=c_at + 12288)
        ug = place("ug", [P, 2, 2, CHUNK], offset=c_at + 16384 + 8192)
        xt = place("xt", [P, 2, CHUNK], offset=c_at + 16384 + 12288)
        stT = place("stT", [P, 2, BANK], offset=x_at + 8192)
        yo = place("yo", [P, SSD_IN], offset=x_at + 12288)
        ng = place("ng", [P, SSD_IN], offset=x_at + 4096)

        def smc(lo, n):
            return sm[:, lo:lo + n]
        CW, CB, BS = smc(0, 48), smc(48, 12), smc(60, 8)
        DV, DTB, ALOG = smc(68, 16), smc(84, 16), smc(100, 16)
        X0 = sm[:, 116:148]
        NA, EX, S1, S2, PO, DT, DA = (smc(148 + 32 * i, 32) for i in range(7))
        ACS = smc(372, 48)
        DTE, EA, NEGA = smc(420, 16), smc(436, 16), smc(452, 16)
        BN = Eg[:, 1, 0:1, 0:96].rearrange("p a b -> p (a b)")
        MV = smc(468, 16)
        RV = smc(484, 8)
        GQ = smc(492, 8)

        for name in ("hy_small", "hy_dtw", "hy_gm", "hy_ws", "hy_wsm", "hy_ng", "hy_ev", "hy_trx", "hy_cx", "hy_pad",
                     "hy_ca", "hy_conv", "hy_dth", "hy_dtl", "hy_dtp", "hy_dtv", "hy_na", "hy_ex", "hy_al",
                     "hy_da", "hy_acs", "hy_acv", "hy_dea", "hy_dte", "hy_back", "hy_xs", "hy_xd", "hy_bc",
                     "hy_bt", "hy_cbm", "hy_abc", "hy_seg", "hy_exp", "hy_G", "hy_mv", "hy_rv", "hy_v",
                     "hy_mix", "hy_mixv", "hy_ya", "hy_trya", "hy_yahi", "hy_yalo", "hy_yd", "hy_st", "hy_stv",
                     "hy_yo", "hy_yoff", "hy_y", "hy_ysq", "hy_yrs", "hy_yn", "hy_try", "hy_yhi", "hy_ylo"):
            sem(name)

        def heads(ap, n=HEADS):
            return ap.rearrange("p (h q) -> p h q", h=n)

        def per_head(ap, n, width):
            return ap.unsqueeze(2).broadcast_to([P, n, width])

        def gemm_free(pe, idx):
            before = {3: 1, 4: 3, 5: 4, 7: 5, 8: 6}
            if idx in before:
                pe.wait_ge(sem("hy_ev"), before[idx])
            if idx == 6:
                pe.wait_ge(sem("hy_dtv"), 1)

        def hyb_pe(pe, s):
            u = first[s]

            def gemm(idx):
                gemm_free(pe, idx)
                for j in range(2):
                    n = u + 2 * idx + j
                    pe.wait_ge(sem("w_lo"), n + 1)
                    wh = whole(WH, n).rearrange("p (k n) -> p k n", k=4)
                    wl = whole(WL, n).rearrange("p (k n) -> p k n", k=4)
                    for t in range(2):
                        if idx == 0 and j == 0:
                            pe.wait_ge(sem("x_lo"), 2 * s + t + 1)
                        for q in range(4):
                            kt = 4 * j + q
                            ins = product(pe, PS[:, PAIR[idx] + t, :], XH[:, kt, tok(t)], XL[:, kt, tok(t)],
                                          wh[:, q, :], wl[:, q, :], kt == 0, kt == KT - 1)
                    ins.then_inc(sem("w_used"), 1)

            def transpose_conv_input(j):
                pe.wait_ge(sem("hy_ev"), j + 1)
                if j:
                    pe.wait_ge(sem("hy_cx"), j)
                for q in range(4):
                    for t in range(2):
                        ins = pe.transpose(PS[:, CT + q // 2, (q % 2) * SEQ + t * P:(q % 2) * SEQ + (t + 1) * P],
                                           xt[:, t, q * P:(q + 1) * P], ident[:, :])
                ins.then_inc(sem("hy_trx"), 1)

            def back(t):
                if t == 0:
                    pe.wait_ge(sem("hy_conv"), 2)
                    pe.wait_ge(sem("hy_acv"), 1)
                else:
                    pe.wait_ge(sem("hy_xd"), 1)
                for q in range(8):
                    ins = pe.transpose(PS[:, CT + q // 4, (q % 4) * P:(q % 4 + 1) * P],
                                       cx[:, q, 3 + t * P:3 + (t + 1) * P], ident[:, :])
                ins.then_inc(sem("hy_back"), 1)

            def cumulated(t, g):
                n = 2 * t + g
                if n == 0:
                    pe.wait_ge(sem("hy_cbm"), 1)
                    pe.wait_ge(sem("hy_bt"), 1)
                elif n == 2:
                    pe.wait_ge(sem("hy_yalo"), 2)
                else:
                    pe.wait_ge(sem("hy_seg"), n)
                for r in range(GH):
                    c = t * HEADS + g * GH + r
                    ins = pe.matmul(PS[:, CT + r // 4, (r % 4) * P:(r % 4 + 1) * P],
                                    DA[:, c:c + 1].broadcast_to([P, P]), tri[:, :], start=True, stop=True)
                ins.then_inc(sem("hy_abc"), 1)

            def mix(c):
                b = (P1, P2)[c]
                if c == 0:
                    pe.wait_ge(sem("hy_wsm"), 1)
                    pe.wait_ge(sem("hy_ev"), 7)
                else:
                    pe.wait_ge(sem("hy_ev"), 8)
                pe.wait_ge(sem("hy_v"), c + 1)
                for r in range(8):
                    ins = pe.matmul(PS[:, b + r // 4, (r % 4) * P:(r % 4 + 1) * P], wsT[:, r, :],
                                    vt[:, c, r * P:(r + 1) * P], start=True, stop=True)
                ins.then_inc(sem("hy_mix"), 1)

            def diagonal(t, g):
                pe.wait_ge(sem("hy_G"), 2 * t + g + 1)
                if g == 0:
                    if t == 0:
                        pe.wait_ge(sem("hy_ev"), 9)
                        pe.wait_ge(sem("hy_xd"), 2)
                    else:
                        pe.wait_ge(sem("hy_y"), 1)
                for r in range(GH):
                    ins = pe.matmul(PS[:, P0 + g, r * 64:(r + 1) * 64], Eg[:, g, r, :],
                                    xd[:, t, (g * GH + r) * 64:(g * GH + r + 1) * 64], start=True, stop=True)
                ins.then_inc(sem("hy_yd"), 1)

            def transpose_out(src, t, done):
                for q in range(8):
                    ins = pe.transpose(PS[:, CT + q // 4, (q % 4) * P:(q % 4 + 1) * P],
                                       src[:, t, q * P:(q + 1) * P], ident[:, :])
                ins.then_inc(sem(done), 1)

            def out_unit(j):
                n = u + 18 + j
                pe.wait_ge(sem("w_lo"), n + 1)
                if j == 0:
                    pe.wait_ge(sem("hy_mixv"), 2)
                if j == 4:
                    pe.wait_ge(sem("hy_ylo"), 2)
                wh = whole(WH, n).rearrange("p (k n) -> p k n", k=2)
                wl = whole(WL, n).rearrange("p (k n) -> p k n", k=2)
                for t in range(2):
                    for c in range(2):
                        for q in range(2):
                            kt = 2 * j + q
                            ins = product(pe, PS[:, 4 + 2 * t + c, :], CH[:, kt, tok(t)], CL[:, kt, tok(t)],
                                          wh[:, q, c * BANK:(c + 1) * BANK], wl[:, q, c * BANK:(c + 1) * BANK],
                                          kt == 0, kt == 15)
                    if t == 1:
                        ins.then_inc(sem("w_used"), 1)
                    elif j == 7:
                        ins.then_inc(sem("out_done"), 1)

            gemm(0)
            gemm(1)
            transpose_conv_input(0)
            gemm(2)
            transpose_conv_input(1)
            gemm(3)
            transpose_conv_input(2)
            pe.wait_ge(sem("hy_dtl"), 1)
            pe.wait_ge(sem("hy_ev"), 2)
            for t in range(2):
                for kt in range(KT):
                    ins = product(pe, PS[:, P1, t * HEADS:(t + 1) * HEADS], XH[:, kt, tok(t)], XL[:, kt, tok(t)],
                                  dt_hi[:, kt, :], dt_lo[:, kt, :], kt == 0, kt == KT - 1)
            ins.then_inc(sem("hy_dtp"), 1)
            gemm(4)
            pe.wait_ge(sem("hy_da"), 1)
            pe.wait_ge(sem("hy_cx"), 3)
            pe.matmul(PS[:, C, 0:32], tri[:, :], DA, start=True, stop=True)
            pe.matmul(PS[:, C, 32:48], tri[:, P - 1:P].broadcast_to([P, P]), DA[:, 0:HEADS], start=True, stop=True)\
              .then_inc(sem("hy_acs"), 1)
            gemm(5)
            back(0)
            gemm(6)
            back(1)
            gemm(7)
            pe.wait_ge(sem("hy_xd"), 2)
            pe.wait_ge(sem("hy_conv"), 3)
            for g in range(2):
                pe.transpose(PS[:, C, g * P:(g + 1) * P], cx[:, 8 + g, 3:3 + P], ident[:, :])
            for t in range(2):
                for g in range(2):
                    ins = pe.matmul(PS[:, T, (2 * t + g) * P:(2 * t + g + 1) * P], cx[:, 8 + g, 3 + t * P:3 + (t + 1) * P],
                                    cx[:, 10 + g, 3 + t * P:3 + (t + 1) * P], start=True, stop=True)
            ins.then_inc(sem("hy_bc"), 1)
            gemm(8)
            cumulated(0, 0)
            mix(0)
            cumulated(0, 1)
            mix(1)
            diagonal(0, 0)
            diagonal(0, 1)
            for t in range(2):
                pe.wait_ge(sem("hy_ya"), t + 1)
                if t == 0:
                    pe.wait_ge(sem("hy_seg"), 2)
                else:
                    pe.wait_ge(sem("hy_yalo"), 1)
                transpose_out(vt, t, "hy_trya")
            cumulated(1, 0)
            out_unit(0)
            cumulated(1, 1)
            out_unit(1)
            pe.wait_ge(sem("hy_seg"), 4)
            for g in range(2):
                ins = pe.matmul(PS[:, CT + g, :], Btok[:, g * P:(g + 1) * P], xde[:, g * BANK:(g + 1) * BANK],
                                start=True, stop=True)
            ins.then_inc(sem("hy_st"), 1)
            diagonal(1, 0)
            diagonal(1, 1)
            out_unit(2)
            pe.wait_ge(sem("hy_stv"), 1)
            for g in range(2):
                ins = pe.matmul(PS[:, CT + g, :], cx[:, 10 + g, 3 + P:3 + 2 * P], stT[:, g, :], start=True, stop=True)
            ins.then_inc(sem("hy_yo"), 1)
            out_unit(3)
            for t in range(2):
                pe.wait_ge(sem("hy_yn"), t + 1)
                pe.wait_ge(sem("hy_yoff" if t == 0 else "hy_ylo"), 1)
                transpose_out(xs, t, "hy_try")
            for j in range(4, 8):
                out_unit(j)

        def hyb_act(act, s, done, split_to):
            u = first[s]

            def evacuate(idx):
                act.wait_ge(sem("w_used"), u + 2 * idx + 2)
                if idx in XBC:
                    if idx:
                        act.wait_ge(sem("hy_trx"), idx)
                    dst, f = xt[:, :, :], ACT.Copy
                elif idx in Z:
                    dst, f = zs[:, :, (idx - 3) * BANK:(idx - 2) * BANK], ACT.Silu
                elif idx in V:
                    dst, f = vt[:, :, (idx - 5) * BANK:(idx - 4) * BANK], ACT.Gelu_apprx_tanh
                else:
                    if idx == 8:
                        act.wait_ge(sem("hy_trx"), 3)
                    dst, f = ug[:, idx - 7, :, :], ACT.Gelu_apprx_tanh
                act.activation(dst, pair(PAIR[idx]), f).then_inc(sem("hy_ev"), 1)

            def conv_silu(j):
                act.wait_ge(sem("hy_ca"), j + 1)
                act.activation(cx[:, 4 * j:4 * j + 4, 3:3 + SEQ], ca[:, :, :], ACT.Silu).then_inc(sem("hy_conv"), 1)

            def decay(n):
                act.wait_ge(sem("hy_seg"), n + 1)
                act.activation(Eg[:, n % 2, :, :], Eg[:, n % 2, :, :], ACT.Exp).then_inc(sem("hy_exp"), 1)

            def copy_xs(t):
                act.wait_ge(sem("hy_back"), t + 1)
                act.activation(xs[:, t, :], flat_pair(CT), ACT.Copy).then_inc(sem("hy_xs"), 1)

            def out_high(t, base, tr, hi):
                act.wait_ge(sem(tr), t + 1)
                act.activation(CH[:, base:base + 8, tok(t)],
                               pair(CT).rearrange("p a (k n) -> p (a k) n", n=P), ACT.Copy).then_inc(sem(hi), 1)

            split_to(u + 3)
            act.wait_ge(sem("hy_dtw"), 16)
            act.activation(dt_hi[:, :, :], dt_w[:, :, :], ACT.Copy).then_inc(sem("hy_dth"), 1)
            act.wait_ge(sem("hy_small"), 32)
            act.activation(NEGA, ALOG, ACT.Exp).then_inc(sem("hy_al"), 1)
            evacuate(0)
            split_to(u + 4)
            split_to(u + 5)
            evacuate(1)
            split_to(u + 7)
            conv_silu(0)
            evacuate(2)
            split_to(u + 9)
            conv_silu(1)
            evacuate(3)
            split_to(u + 10)
            act.wait_ge(sem("hy_na"), 1)
            act.activation(EX, NA, ACT.Exp).then_inc(sem("hy_ex"), 1)
            split_to(u + 11)
            evacuate(4)
            conv_silu(2)
            split_to(u + 12)
            act.wait_ge(sem("hy_dea"), 1)
            act.activation(DTE, DTE, ACT.Exp)
            act.activation(EA, ACS[:, HEADS:2 * HEADS], ACT.Exp).then_inc(sem("hy_dte"), 1)
            split_to(u + 13)
            evacuate(5)
            copy_xs(0)
            split_to(u + 15)
            evacuate(6)
            copy_xs(1)
            split_to(u + 17)
            evacuate(7)
            act.wait_ge(sem("hy_bc"), 1)
            act.activation(Btok[:, :], PS[:, C, 0:2 * P], ACT.Copy).then_inc(sem("hy_bt"), 1)
            split_to(u + 19)
            evacuate(8)
            split_to(u + 20)
            decay(0)
            decay(1)
            for t in range(2):
                out_high(t, 0, "hy_trya", "hy_yahi")
            decay(2)
            split_to(u + 21)
            decay(3)
            split_to(u + 22)
            act.wait_ge(sem("hy_st"), 1)
            act.activation(stT[:, :, :], pair(CT), ACT.Copy).then_inc(sem("hy_stv"), 1)
            split_to(u + 23)
            for t in range(2):
                act.wait_ge(sem("hy_y"), 2 * t + 2)
                for g in range(2):
                    act.activation(junk[:, t, g * BANK:(g + 1) * BANK], xs[:, t, g * BANK:(g + 1) * BANK], ACT.Square,
                                   accum_out=GQ[:, 2 * t + g:2 * t + g + 1]).then_inc(sem("hy_ysq"), 1)
            split_to(u + 24)
            for t in range(2):
                out_high(t, 8, "hy_try", "hy_yhi")
            split_to(u + 27)

        def hyb_dve(dve, s, done, split_to):
            u = first[s]

            def chain(ins):
                link(dve, "dve_chain", ins)

            def conv(j):
                dve.wait_ge(sem("hy_trx"), j + 1)
                if j == 0:
                    dve.wait_ge(sem("hy_small"), 32)
                dve.tensor_copy(cx[:, 4 * j:4 * j + 4, 3:3 + SEQ], PS[:, CT:CT + 2, :]
                                .rearrange("p a (k n) -> p (a k) n", n=SEQ)).then_inc(sem("hy_cx"), 1)
                dve.wait_ge(sem("hy_cx"), j + 1)
                if j == 0:
                    dve.wait_ge(sem("hy_pad"), 1)
                else:
                    dve.wait_ge(sem("hy_conv"), j)
                for tap in range(4):
                    for q in range(4):
                        c = 4 * j + q
                        x = cx[:, c, tap:tap + SEQ]
                        w = CW[:, 4 * c + tap:4 * c + tap + 1]
                        if tap == 0:
                            ins = dve.tensor_scalar(ca[:, q, :], x, w, CB[:, c:c + 1], ALU.mult, ALU.add)
                        else:
                            ins = dve.scalar_tensor_tensor(ca[:, q, :], x, w, ca[:, q, :], ALU.mult, ALU.add)
                    if tap < 3:
                        chain(ins)
                ins.then_inc(sem("hy_ca"), 1)

            def segment(t, g):
                n = 2 * t + g
                dve.wait_ge(sem("hy_abc"), n + 1)
                if n == 1:
                    dve.wait_ge(sem("hy_v"), 2)
                if n >= 2:
                    dve.wait_ge(sem("hy_yd"), n - 1)
                c = t * HEADS + g * GH
                chain(dve.tensor_tensor(Eg[:, g, :, :], flat_pair(CT).rearrange("p (h l) -> p h l", h=GH),
                                        per_head(ACS[:, c:c + GH], GH, P), ALU.subtract))
                dve.tensor_scalar(Eg[:, g, :, :], Eg[:, g, :, :], 0.0, None, ALU.min).then_inc(sem("hy_seg"), 1)

            def weigh(t, g):
                n = 2 * t + g
                dve.wait_ge(sem("hy_exp"), n + 1)
                dve.tensor_tensor(Eg[:, g, :, :], Eg[:, g, :, :],
                                  cbm[:, n, :].unsqueeze(1).broadcast_to([P, GH, P]), ALU.mult)\
                   .then_inc(sem("hy_G"), 1)

            def times_dt(t):
                dve.wait_ge(sem("hy_xs"), t + 1)
                dve.tensor_tensor(heads(xd[:, t, :]), heads(flat_pair(CT)),
                                  per_head(DT[:, t * HEADS:(t + 1) * HEADS], HEADS, 64), ALU.mult)\
                   .then_inc(sem("hy_xd"), 1)

            def skip(t):
                dve.tensor_tensor(heads(xs[:, t, :]), heads(xs[:, t, :]), per_head(DV, HEADS, 64), ALU.mult)

            def normalise(c):
                if c:
                    dve.wait_ge(sem("hy_v"), 1)
                for r in range(8):
                    ins = dve.bn_stats(BN[:, 6 * r:6 * r + 6], vt[:, c, r * P:(r + 1) * P])
                chain(ins)
                for r in range(8):
                    ins = dve.bn_aggr(MV[:, 2 * r:2 * r + 2], BN[:, 6 * r:6 * r + 6])
                ins.then_inc(sem("hy_mv"), 1)
                dve.wait_ge(sem("hy_mv"), c + 1)
                dve.wait_ge(sem("hy_rv"), c + 1)
                for r in range(8):
                    v = vt[:, c, r * P:(r + 1) * P]
                    ins = dve.tensor_scalar(v, v, MV[:, 2 * r:2 * r + 1], RV[:, r:r + 1], ALU.subtract, ALU.mult)
                chain(ins)
                if c == 0:
                    dve.wait_ge(sem("hy_gm"), 32)
                chain(dve.tensor_tensor(vt[:, c, :], vt[:, c, :], gm_g[:, :], ALU.mult))
                dve.tensor_tensor(vt[:, c, :], vt[:, c, :], gm_b[:, :], ALU.add).then_inc(sem("hy_v"), 1)

            def gate_v(c):
                dve.wait_ge(sem("hy_mix"), c + 1)
                b = (P1, P2)[c]
                dve.tensor_tensor(heads(vt[:, c, :], 8), heads(flat_pair(b), 8), per_head(BS, 8, P), ALU.add)\
                   .then_inc(sem("hy_mixv"), 1)
                dve.wait_ge(sem("hy_mixv"), c + 1)
                dve.wait_ge(sem("hy_ev"), 9)
                v = vt[:, c, :].rearrange("p (a n) -> p a n", a=2)
                dve.tensor_tensor(v, v, ug[:, :, c, :], ALU.mult).then_inc(sem("hy_ya"), 1)

            def out_low(t, base, hi, lo):
                dve.wait_ge(sem(hi), t + 1)
                dve.tensor_tensor(CL[:, base:base + 8, tok(t)], pair(CT).rearrange("p a (k n) -> p (a k) n", n=P),
                                  CH[:, base:base + 8, tok(t)], ALU.subtract).then_inc(sem(lo), 1)

            def gated(t):
                dve.wait_ge(sem("hy_yd"), 2 * t + 2)
                dve.tensor_tensor(xs[:, t, :], flat_pair(P0), xs[:, t, :], ALU.add).then_inc(sem("hy_y"), 1)
                if t:
                    dve.wait_ge(sem("hy_y"), 3)
                    chain(dve.tensor_tensor(xs[:, t, :], xs[:, t, :], yo[:, :], ALU.add))
                else:
                    dve.wait_ge(sem("hy_y"), 1)
                dve.tensor_tensor(xs[:, t, :], xs[:, t, :], zs[:, t, :], ALU.mult).then_inc(sem("hy_y"), 1)

            split_to(u + 3)
            dve.wait_ge(sem("hy_dth"), 1)
            dve.tensor_tensor(dt_lo[:, :, :], dt_w[:, :, :], dt_hi[:, :, :], ALU.subtract).then_inc(sem("hy_dtl"), 1)
            split_to(u + 6)
            conv(0)
            split_to(u + 8)
            conv(1)
            split_to(u + 10)
            dve.wait_ge(sem("hy_dtp"), 1)
            dve.tensor_tensor(X0.rearrange("p (t h) -> p t h", t=2), PS[:, P1, 0:32].rearrange("p (t h) -> p t h", t=2),
                              DTB.unsqueeze(1).broadcast_to([P, 2, HEADS]), ALU.add).then_inc(sem("hy_dtv"), 1)
            dve.wait_ge(sem("hy_dtv"), 1)
            dve.scalar_tensor_tensor(NA, X0, -1.0, X0, ALU.mult, ALU.min).then_inc(sem("hy_na"), 1)
            conv(2)
            dve.wait_ge(sem("hy_ex"), 1)
            chain(dve.tensor_scalar(S1, EX, 2.0, None, ALU.add))
            chain(dve.reciprocal(S1, S1))
            chain(dve.tensor_tensor(S1, S1, EX, ALU.mult))
            chain(dve.tensor_tensor(S2, S1, S1, ALU.mult))
            terms = [2.0 / (2 * i + 1) for i in range(9)]
            chain(dve.tensor_scalar(PO, S2, terms[8], terms[7], ALU.mult, ALU.add))
            for c in terms[6::-1]:
                chain(dve.tensor_tensor(PO, PO, S2, ALU.mult))
                chain(dve.tensor_scalar(PO, PO, c, None, ALU.add))
            chain(dve.tensor_tensor(PO, PO, S1, ALU.mult))
            chain(dve.scalar_tensor_tensor(DT, X0, 0.0, PO, ALU.max, ALU.add))
            dve.wait_ge(sem("hy_al"), 1)
            dve.scalar_tensor_tensor(DA.rearrange("p (t h) -> p t h", t=2), DT.rearrange("p (t h) -> p t h", t=2), -1.0,
                                     NEGA.unsqueeze(1).broadcast_to([P, 2, HEADS]), ALU.mult, ALU.mult)\
               .then_inc(sem("hy_da"), 1)
            split_to(u + 12)
            dve.wait_ge(sem("hy_acs"), 1)
            dve.tensor_copy(ACS, PS[:, C, 0:48]).then_inc(sem("hy_acv"), 1)
            dve.wait_ge(sem("hy_acv"), 1)
            dve.tensor_tensor(DTE, ACS[:, 32:48], ACS[:, 0:HEADS], ALU.subtract).then_inc(sem("hy_dea"), 1)
            split_to(u + 13)
            times_dt(0)
            dve.wait_ge(sem("hy_xd"), 1)
            dve.wait_ge(sem("hy_dte"), 1)
            dve.tensor_tensor(heads(xde[:, :]), heads(xd[:, 0, :]), per_head(DTE, HEADS, 64), ALU.mult)
            skip(0)
            split_to(u + 15)
            times_dt(1)
            skip(1)
            split_to(u + 16)
            dve.wait_ge(sem("hy_ev"), 7)
            normalise(0)
            split_to(u + 17)
            normalise(1)
            dve.wait_ge(sem("hy_bc"), 1)
            dve.tensor_tensor(cbm[:, :, :], PS[:, T, :].rearrange("p (n l) -> p n l", l=P),
                              tri[:, :].unsqueeze(1).broadcast_to([P, 4, P]), ALU.mult).then_inc(sem("hy_cbm"), 1)
            split_to(u + 20)
            segment(0, 0)
            gate_v(0)
            weigh(0, 0)
            segment(0, 1)
            gate_v(1)
            weigh(0, 1)
            for t in range(2):
                out_low(t, 0, "hy_yahi", "hy_yalo")
            segment(1, 0)
            weigh(1, 0)
            gated(0)
            split_to(u + 21)
            segment(1, 1)
            weigh(1, 1)
            split_to(u + 23)
            dve.wait_ge(sem("hy_yo"), 1)
            dve.tensor_tensor(heads(yo[:, :]), heads(flat_pair(CT)), per_head(EA, HEADS, 64), ALU.mult)\
               .then_inc(sem("hy_yoff"), 1)
            dve.wait_ge(sem("hy_yoff"), 1)
            gated(1)
            split_to(u + 24)
            dve.wait_ge(sem("hy_ng"), 16)
            for t in range(2):
                for g in range(2):
                    dve.wait_ge(sem("hy_yrs"), 1)
                    y = xs[:, t, g * BANK:(g + 1) * BANK]
                    ins = dve.scalar_tensor_tensor(y, y, GQ[:, 4 + 2 * t + g:5 + 2 * t + g], ng[:, g * BANK:(g + 1) * BANK],
                                                   ALU.mult, ALU.mult)
                ins.then_inc(sem("hy_yn"), 1)
            for t in range(2):
                out_low(t, 8, "hy_yhi", "hy_ylo")
            split_to(u + 27)

        def hyb_pool(pool, s):
            pool.memset(cx[:, :, 0:3], 0.0).then_inc(sem("hy_pad"), 1)
            pool.dma_start(dt_w[:, :, :], a["dt_w"]).then_inc(sem("hy_dtw"), 16)
            pool.dma_start(sm[:, 0:68], a["hy_cols"]).then_inc(sem("hy_small"), 16)
            pool.dma_start(sm[:, 68:116], a["hy_rows"].partition_broadcast(P)).then_inc(sem("hy_small"), 16)
            pool.dma_start(wsT[:, :, :], a["gm_w"]).then_inc(sem("hy_ws"), 16)
            pool.dma_start(gm_g[:, :], a["gm_g"].partition_broadcast(P)).then_inc(sem("hy_gm"), 16)
            pool.dma_start(gm_b[:, :], a["gm_b"].partition_broadcast(P)).then_inc(sem("hy_gm"), 16)
            pool.wait_ge(sem("hy_ws"), 16)
            pool.tensor_tensor(wsT[:, :, :], wsT[:, :, :], tri[:, :].unsqueeze(1).broadcast_to([P, 8, P]), ALU.mult)\
                .then_inc(sem("hy_wsm"), 1)
            for c in range(2):
                pool.wait_ge(sem("hy_mv"), c + 1)
                link(pool, "pool_chain", pool.tensor_scalar(RV, MV.rearrange("p (h q) -> p h q", q=2)[:, :, 1], LN_EPS, None,
                                                            ALU.add))
                pool.tensor_tensor(RV, RV, nhalf[:, :], ALU.pow).then_inc(sem("hy_rv"), 1)
                if c == 0:
                    pool.wait_ge(sem("hy_v"), 1)
            pool.wait_ge(sem("w_used"), first[s] + 18)
            pool.dma_start(ng[:, :], a["ssd_g"].partition_broadcast(P)).then_inc(sem("hy_ng"), 16)
            pool.wait_ge(sem("hy_ysq"), 4)
            link(pool, "pool_chain", pool.tensor_scalar(GQ[:, 4:8], GQ[:, 0:4], 1.0 / 512, EPS, ALU.mult, ALU.add))
            pool.tensor_tensor(GQ[:, 4:8], GQ[:, 4:8], nhalf[:, 0:4], ALU.pow).then_inc(sem("hy_yrs"), 1)


        HALF = ROPE // 2
        kT = place("kT", [P, HEADS, SEQ], offset=x_at)
        o = s_at
        qT = place("qT", [P, HEADS, SEQ], offset=o); o += 16384
        vv = place("vv", [P, 2, HEADS * VD], offset=o); o += 16384
        qrT = place("qrT", [P, 8, SEQ], offset=o); o += 8192
        krT = place("krT", [P, SEQ], offset=o); o += 1024
        pr = place("pr", [P, 2, 3 * P], offset=o); o += 3072
        pT = place("pT", [P, 2, 3 * P], offset=o); o += 3072
        msm = place("msm", [P, 256], offset=o); o += 1024
        assert o <= end, o
        qr = hn
        cn = place("cn", [P, 2, BANK], offset=c_at)
        cTH = place("cTH", [P, 3, SEQ], f32r, offset=c_at + 4096)
        cTL = place("cTL", [P, 3, SEQ], f32r, offset=c_at + 4096 + 3072)
        cg = place("cg", [P, Q_LORA + KV_LORA], offset=c_at + 10240)
        ra = place("ra", [P, HEADS, HALF], offset=c_at + 12288)
        rb = place("rb", [P, HEADS, HALF], offset=c_at + 14336)
        rc = place("rc", [P, HEADS, HALF], offset=c_at + 16384)
        rd = place("rd", [P, HEADS, HALF], offset=c_at + 18432)

        LSQ, LRS = msm[:, 0:4], msm[:, 4:8]
        NMX, SUM = msm[:, 8:72], msm[:, 72:136]
        MAXS = msm[:, 136:200]

        for name in ("ml_in", "ml_cg", "ml_sq", "ml_rs", "ml_cn", "ml_tr", "ml_chi", "ml_clo", "ml_krT", "ml_pa",
                     "ml_pv", "ml_S", "ml_mx", "ml_nm", "ml_exp", "ml_P", "ml_PT", "ml_PTe", "ml_O", "ml_Ohi", "ml_Olo",
                     "ml_qr", "ml_qrt", "rope_pos", "rope_arg", "rope_sin", "rope_done", "ml_X", "ml_XA", "ml_XD"):
            sem(name)

        def group_bank(n):
            return 4 * (n % 2)

        def group_free(pe, n):
            if n == 4:
                pe.wait_ge(sem("ml_qr"), 2)
            elif n >= 2:
                v = n - 1 if n < 4 else n - 2
                pe.wait_ge(sem("ml_XA"), v)
                pe.wait_ge(sem("ml_XD"), v)

        def mla_pe(pe, s):
            u = first[s]
            for j in range(2):
                pe.wait_ge(sem("w_lo"), u + j + 1)
                wh = whole(WH, u + j).rearrange("p (k n) -> p k n", k=4)
                wl = whole(WL, u + j).rearrange("p (k n) -> p k n", k=4)
                for t in range(2):
                    if j == 0:
                        pe.wait_ge(sem("x_lo"), 2 * s + t + 1)
                    for q in range(4):
                        kt = 4 * j + q
                        ins = product(pe, PS[:, t, 0:448], XH[:, kt, tok(t)], XL[:, kt, tok(t)],
                                      wh[:, q, 0:448], wl[:, q, 0:448], kt == 0, kt == KT - 1)
                ins.then_inc(sem("w_used"), 1)
            for t in range(2):
                pe.wait_ge(sem("ml_cn"), t + 1)
                for q in range(4):
                    ins = pe.transpose(PS[:, C + t, q * P:(q + 1) * P], cn[:, t, q * P:(q + 1) * P], ident[:, :])
                ins.then_inc(sem("ml_tr"), 1)

            def turned(n, b, h, unit, kts, wcol, base):
                wh = whole(WH, unit).rearrange("p (k n) -> p k n", k=kts)
                wl = whole(WL, unit).rearrange("p (k n) -> p k n", k=kts)
                out_ap = PS[:, b, (h % 2) * SEQ:(h % 2 + 1) * SEQ]
                for q in range(kts):
                    a_h, a_l = cTH[:, base + q, :], cTL[:, base + q, :]
                    w = slice(wcol * P, (wcol + 1) * P)
                    ins = product(pe, out_ap, wh[:, q, w], wl[:, q, w], a_h, a_l, q == 0, q == kts - 1)
                return ins

            pe.wait_ge(sem("ml_clo"), 2)
            pe.wait_ge(sem("ml_krT"), 2)
            pe.wait_ge(sem("w_lo"), u + 3)
            for g in range(2):
                group_free(pe, g)
                for r in range(8):
                    ins = turned(g, group_bank(g) + r // 2, r, u + 2, 1, 8 * g + r, 2)
                ins.then_inc(sem("ml_X" if g == 0 else "w_used"), 1)
            pe.wait_ge(sem("w_lo"), u + 4)
            group_free(pe, 2)
            wh = whole(WH, u + 3).rearrange("p (k n) -> p k n", k=2)
            wl = whole(WL, u + 3).rearrange("p (k n) -> p k n", k=2)
            for t in range(2):
                for c in range(2):
                    for q in range(2):
                        ins = product(pe, PS[:, 2 * t + c, :], cTH[:, q, tok(t)], cTL[:, q, tok(t)],
                                      wh[:, q, c * BANK:(c + 1) * BANK], wl[:, q, c * BANK:(c + 1) * BANK],
                                      q == 0, q == 1)
            ins.then_inc(sem("w_used"), 1)
            for g in range(2):
                pe.wait_ge(sem("w_lo"), u + 5 + g)
                group_free(pe, 3 + g)
                for r in range(8):
                    ins = turned(3 + g, group_bank(3 + g) + r // 2, r, u + 4 + g, 2, r, 0)
                ins.then_inc(sem("w_used"), 1)
            pe.wait_ge(sem("w_lo"), u + 7)
            for t in range(2):
                group_free(pe, 5 + t)
                for c in range(4):
                    ins = product(pe, PS[:, group_bank(5 + t) + c, :], cTH[:, 2, tok(t)], cTL[:, 2, tok(t)],
                                  whole(WH, u + 6)[:, c * BANK:(c + 1) * BANK], whole(WL, u + 6)[:, c * BANK:(c + 1) * BANK],
                                  True, True)
                ins.then_inc(sem("w_used" if t else "ml_X"), 1)
            group_free(pe, 7)
            pe.wait_ge(sem("ml_qr"), 2)
            for r in range(8):
                for t in range(2):
                    ins = pe.transpose(PS[:, 4 + r // 2, (r % 2) * SEQ + t * P:(r % 2) * SEQ + (t + 1) * P],
                                       qr[:, t, r * P:(r + 1) * P], ident[:, :])
            ins.then_inc(sem("ml_qrt"), 1)

            def scores(hd):
                if hd >= 2:
                    pe.wait_ge(sem("ml_mx"), hd - 1)
                lo = (hd % 2) * 64
                for t in range(2):
                    n = (t + 1) * P
                    dst = PS[:, hd % 2, t * P:t * P + n]
                    pe.matmul(dst, qT[:, hd, tok(t)], kT[:, hd, 0:n], start=True, stop=False)
                    ins = pe.matmul(dst, qrT[lo:lo + 64, hd // 2, tok(t)], krT[lo:lo + 64, 0:n], start=False, stop=True)
                ins.then_inc(sem("ml_S"), 1)

            def transpose_probabilities(hd):
                pe.wait_ge(sem("ml_P"), hd + 1)
                if hd:
                    pe.wait_ge(sem("ml_PTe"), hd)
                for q in range(3):
                    ins = pe.transpose(PS[:, C, q * P:(q + 1) * P], pr[:, hd % 2, q * P:(q + 1) * P], ident[:, :])
                ins.then_inc(sem("ml_PT"), 1)

            def weighted_values(hd):
                pe.wait_ge(sem("ml_PTe"), hd + 1)
                if hd % 2 == 0 and hd:
                    pe.wait_ge(sem("ml_Olo"), hd // 2)
                lo = (hd % 2) * SEQ
                w = slice(hd * VD, (hd + 1) * VD)
                pe.matmul(PS[:, T, lo:lo + SEQ], vv[:, 0, w], pT[:, hd % 2, 0:SEQ], start=True, stop=False)
                ins = pe.matmul(PS[:, T, lo + P:lo + SEQ], vv[:, 1, w], pT[:, hd % 2, SEQ:3 * P], start=False, stop=True)
                ins.then_inc(sem("ml_O"), 1)

            def out_unit(j):
                n = u + 7 + j
                pe.wait_ge(sem("w_lo"), n + 1)
                pe.wait_ge(sem("ml_Olo"), j + 1)
                wh = whole(WH, n).rearrange("p (k n) -> p k n", k=2)
                wl = whole(WL, n).rearrange("p (k n) -> p k n", k=2)
                for t in range(2):
                    for c in range(2):
                        for q in range(2):
                            kt = 2 * j + q
                            ins = product(pe, PS[:, 4 + 2 * t + c, :], CH[:, kt, tok(t)], CL[:, kt, tok(t)],
                                          wh[:, q, c * BANK:(c + 1) * BANK], wl[:, q, c * BANK:(c + 1) * BANK],
                                          kt == 0, kt == 15)
                    if t == 1:
                        ins.then_inc(sem("w_used"), 1)
                    elif j == 7:
                        ins.then_inc(sem("out_done"), 1)

            pe.wait_ge(sem("ml_XA"), 7)
            pe.wait_ge(sem("ml_XD"), 7)
            scores(0)
            scores(1)
            for j in range(8):
                transpose_probabilities(2 * j)
                if j < 7:
                    scores(2 * j + 2)
                transpose_probabilities(2 * j + 1)
                if j < 7:
                    scores(2 * j + 3)
                weighted_values(2 * j)
                weighted_values(2 * j + 1)
                if j:
                    out_unit(j - 1)
            out_unit(7)

        def group_ready(eng, s, n):
            u = first[s]
            if n == 0:
                eng.wait_ge(sem("ml_X"), 1)
            elif n == 5:
                eng.wait_ge(sem("ml_X"), 2)
            elif n == 7:
                eng.wait_ge(sem("ml_qrt"), 1)
            else:
                eng.wait_ge(sem("w_used"), u + {1: 3, 2: 4, 3: 5, 4: 6, 6: 7}[n])

        def group_part(n, part):
            b = group_bank(n) + 2 * part
            src = PS[:, b:b + 2, :]
            def four(tile, h0):
                return tile[:, h0 + 4 * part:h0 + 4 * part + 4, :].rearrange("p (a h) n -> p a (h n)", a=2)
            if n in (0, 1):
                return four(kT, 8 * n), src
            if n in (3, 4):
                return four(qT, 8 * (n - 3)), src
            if n == 7:
                return four(qrT, 0), src
            return vv[:, n - 5, part * 1024:(part + 1) * 1024].rearrange("p (a n) -> p a n", a=2), src

        def mla_act(act, s, done, split_to):
            u = first[s]
            split_to(u + 3)
            act.wait_ge(sem("w_used"), u + 2)
            for t in range(2):
                act.activation(junk[:, t, 0:Q_LORA], PS[:, t, 0:Q_LORA], ACT.Square, scale=1.0 / 16,
                               accum_out=LSQ[:, t:t + 1])
                act.activation(junk[:, t, Q_LORA:Q_LORA + KV_LORA], PS[:, t, Q_LORA:Q_LORA + KV_LORA], ACT.Square,
                               accum_out=LSQ[:, 2 + t:3 + t]).then_inc(sem("ml_sq"), 1)
            split_to(u + 4)
            for t in range(2):
                act.wait_ge(sem("ml_tr"), t + 1)
                act.activation(cTH[:, :, tok(t)], PS[:, C + t, 0:384].rearrange("p (k n) -> p k n", n=P), ACT.Copy)\
                   .then_inc(sem("ml_chi"), 1)

            def empty(n):
                group_ready(act, s, n)
                dst, src = group_part(n, 0)
                act.activation(dst, src, ACT.Copy).then_inc(sem("ml_XA"), 1)

            empty(0)
            empty(1)
            split_to(u + 5)
            split_to(u + 6)
            empty(3)
            split_to(u + 7)
            empty(4)
            empty(5)
            split_to(u + 8)
            empty(6)
            empty(7)
            split_to(u + 9)

            def exponentials(hd):
                act.wait_ge(sem("ml_nm"), hd + 1)
                for t in range(2):
                    p = pr[:, hd % 2, t * P:t * P + (t + 1) * P]
                    c = 2 * hd + t
                    ins = act.activation(p, p, ACT.Exp, bias=NMX[:, c:c + 1], scale=SCALE, accum_out=SUM[:, c:c + 1])
                ins.then_inc(sem("ml_exp"), 1)

            def copy_pT(hd):
                act.wait_ge(sem("ml_PT"), hd + 1)
                if hd >= 2:
                    act.wait_ge(sem("ml_O"), hd - 1)
                act.activation(pT[:, hd % 2, :], PS[:, C, 0:3 * P], ACT.Copy).then_inc(sem("ml_PTe"), 1)

            exponentials(0)
            exponentials(1)
            for j in range(8):
                copy_pT(2 * j)
                if j < 7:
                    exponentials(2 * j + 2)
                copy_pT(2 * j + 1)
                if j < 7:
                    exponentials(2 * j + 3)
                act.wait_ge(sem("ml_O"), 2 * j + 2)
                act.activation(CH[:, 2 * j:2 * j + 2, :], PS[:, T, :].rearrange("p (k n) -> p k n", n=SEQ), ACT.Copy)\
                   .then_inc(sem("ml_Ohi"), 1)
                if j:
                    split_to(u + 9 + j)
            split_to(u + 16)

        def mla_dve(dve, s, done, split_to):
            u = first[s]

            def rotate(x, y, t, n, tmp):
                c = cosT[:, t, :].unsqueeze(1).broadcast_to([P, n, HALF])
                sn = sinT[:, t, :].unsqueeze(1).broadcast_to([P, n, HALF])
                w, x_, y_, z_ = (m[:, 0:n, :] for m in tmp)
                dve.tensor_tensor(w, x[:, :, 0, :], c, ALU.mult)
                dve.tensor_tensor(x_, x[:, :, 1, :], sn, ALU.mult)
                dve.tensor_tensor(y_, x[:, :, 1, :], c, ALU.mult)
                link(dve, "dve_chain", dve.tensor_tensor(z_, x[:, :, 0, :], sn, ALU.mult))
                dve.tensor_tensor(y[:, :, 0, :], w, x_, ALU.subtract)
                return dve.tensor_tensor(y[:, :, 1, :], y_, z_, ALU.add)

            tmp = (ra, rb, rc, rd)
            split_to(u + 3)
            dve.wait_ge(sem("ml_cg"), 32)
            for t in range(2):
                dve.wait_ge(sem("ml_rs"), 1)
                q, kv = slice(0, Q_LORA), slice(Q_LORA, Q_LORA + KV_LORA)
                dve.scalar_tensor_tensor(cn[:, t, q], PS[:, t, q], LRS[:, t:t + 1], cg[:, q], ALU.mult, ALU.mult)
                dve.scalar_tensor_tensor(cn[:, t, kv], PS[:, t, kv], LRS[:, 2 + t:3 + t], cg[:, kv], ALU.mult, ALU.mult)
                link(dve, "dve_chain", rotate(PS[:, t, 384:448].rearrange("p (n a h) -> p n a h", n=1, a=2),
                                              cn[:, t, 384:448].rearrange("p (n a h) -> p n a h", n=1, a=2), t, 1, tmp))
                dve.tensor_copy(cn[:, t, 448:512], cn[:, t, 384:448]).then_inc(sem("ml_cn"), 1)
            split_to(u + 4)
            for t in range(2):
                dve.wait_ge(sem("ml_chi"), t + 1)
                dve.tensor_tensor(cTL[:, :, tok(t)], PS[:, C + t, 0:384].rearrange("p (k n) -> p k n", n=P),
                                  cTH[:, :, tok(t)], ALU.subtract).then_inc(sem("ml_clo"), 1)
                dve.tensor_copy(krT[:, tok(t)], PS[:, C + t, 384:512]).then_inc(sem("ml_krT"), 1)

            def empty(n):
                group_ready(dve, s, n)
                dst, src = group_part(n, 1)
                dve.tensor_copy(dst, src).then_inc(sem("ml_XD"), 1)

            empty(0)
            empty(1)
            split_to(u + 5)
            split_to(u + 6)
            group_ready(dve, s, 2)
            for t in range(2):
                rotate(PS[:, 2 * t:2 * t + 2, :].rearrange("p b (n a h) -> p (b n) a h", a=2, h=HALF),
                       qr[:, t, :].rearrange("p (n a h) -> p n a h", a=2, h=HALF), t, HEADS, tmp)\
                    .then_inc(sem("ml_qr"), 1)
                dve.wait_ge(sem("ml_qr"), t + 1)
            empty(3)
            split_to(u + 7)
            empty(4)
            empty(5)
            split_to(u + 8)
            empty(6)
            empty(7)
            split_to(u + 9)

            def maxima(hd):
                dve.wait_ge(sem("ml_S"), hd + 1)
                if hd >= 2:
                    dve.wait_ge(sem("ml_PT"), hd - 1)
                for t in range(2):
                    c = 2 * hd + t
                    n = (t + 1) * P
                    ins = dve.tensor_tensor_reduce(out=pr[:, hd % 2, t * P:t * P + n], in0=PS[:, hd % 2, t * P:t * P + n],
                                                   in1=cmask[:, 2 * P - n:2 * P], scale=1.0, scalar=-3.0e38, op0=ALU.add,
                                                   op1=ALU.max, accum_out=MAXS[:, c:c + 1])
                ins.then_inc(sem("ml_mx"), 1)
                dve.wait_ge(sem("ml_mx"), hd + 1)
                dve.tensor_scalar(NMX[:, 2 * hd:2 * hd + 2], MAXS[:, 2 * hd:2 * hd + 2], -SCALE, None, ALU.mult)\
                   .then_inc(sem("ml_nm"), 1)

            def normalise(hd):
                dve.wait_ge(sem("ml_exp"), hd + 1)
                r = SUM[:, 2 * hd:2 * hd + 2]
                link(dve, "dve_chain", dve.reciprocal(r, r))
                for t in range(2):
                    p = pr[:, hd % 2, t * P:t * P + (t + 1) * P]
                    c = 2 * hd + t
                    ins = dve.tensor_scalar(p, p, SUM[:, c:c + 1], None, ALU.mult)
                ins.then_inc(sem("ml_P"), 1)

            maxima(0)
            maxima(1)
            normalise(0)
            normalise(1)
            for j in range(8):
                if j < 7:
                    maxima(2 * j + 2)
                    maxima(2 * j + 3)
                    normalise(2 * j + 2)
                    normalise(2 * j + 3)
                dve.wait_ge(sem("ml_Ohi"), j + 1)
                dve.tensor_tensor(CL[:, 2 * j:2 * j + 2, :], PS[:, T, :].rearrange("p (k n) -> p k n", n=SEQ),
                                  CH[:, 2 * j:2 * j + 2, :], ALU.subtract).then_inc(sem("ml_Olo"), 1)
                if j:
                    split_to(u + 9 + j)
            split_to(u + 16)

        def mla_pool(pool, s):
            pool.dma_start(cg[:, 0:Q_LORA], a["q_g"].partition_broadcast(P)).then_inc(sem("ml_cg"), 16)
            pool.dma_start(cg[:, Q_LORA:Q_LORA + KV_LORA], a["kv_g"].partition_broadcast(P)).then_inc(sem("ml_cg"), 16)
            pool.wait_ge(sem("ml_sq"), 2)
            pool.tensor_scalar(LRS[:, 0:2], LSQ[:, 0:2], 1.0, EPS, ALU.mult, ALU.add)
            link(pool, "pool_chain", pool.tensor_scalar(LRS[:, 2:4], LSQ[:, 2:4], 1.0 / KV_LORA, EPS, ALU.mult, ALU.add))
            pool.tensor_tensor(LRS, LRS, nhalf[:, 0:4], ALU.pow).then_inc(sem("ml_rs"), 1)

        rp = place("rp", [P, 2], i32, offset=s_at)
        rf = place("rf", [P, 2], offset=s_at + 32)
        inv = place("inv", [P, HALF], offset=s_at + 64)
        ang = place("ang", [P, 2, HALF], offset=s_at + 256)
        turns = place("turns", [P, 2, HALF], offset=s_at + 512)
        sh = place("sh", [P, 2, HALF], offset=s_at + 768)
        parts, rest = [], 2 * np.pi
        for bits in (8, 8, 8):
            unit = 2.0 ** (np.floor(np.log2(rest)) - bits + 1)
            parts.append(float(np.floor(rest / unit) * unit))
            rest -= parts[-1]
        parts.append(float(rest))
        MAGIC = 1.5 * 2.0 ** 23
        LIMIT = 3.1415925

        def prelude_pool(pool):
            if not has_mla:
                return
            pool.dma_start(rp[:, :], a["positions"]).then_inc(sem("rope_pos"), 16)
            pool.dma_start(inv[:, :], a["inv"].partition_broadcast(P)).then_inc(sem("rope_pos"), 16)

        def prelude_act(act):
            if not has_mla:
                return
            act.wait_ge(sem("rope_arg"), 1)
            act.activation(sinT[:, :, :], ang[:, :, :], ACT.Sin)
            act.activation(sh[:, :, :], ang[:, :, :], ACT.Sin, scale=0.5).then_inc(sem("rope_sin"), 1)

        def prelude_dve(dve):
            if not has_mla:
                return

            def chain(ins):
                link(dve, "dve_chain", ins)

            dve.wait_ge(sem("rope_pos"), 32)
            chain(dve.tensor_copy(rf[:, :], rp[:, :]))
            for t in range(2):
                ins = dve.tensor_scalar(ang[:, t, :], inv[:, :], rf[:, t:t + 1], None, ALU.mult)
            chain(ins)
            chain(dve.tensor_scalar(turns[:, :, :], ang[:, :, :], float(1 / (2 * np.pi)), MAGIC, ALU.mult, ALU.add))
            chain(dve.tensor_scalar(turns[:, :, :], turns[:, :, :], MAGIC, None, ALU.subtract))
            for part in parts:
                chain(dve.scalar_tensor_tensor(ang[:, :, :], turns[:, :, :], -part, ang[:, :, :], ALU.mult, ALU.add))
            dve.tensor_scalar(ang[:, :, :], ang[:, :, :], LIMIT, -LIMIT, ALU.min, ALU.max).then_inc(sem("rope_arg"), 1)
            dve.wait_ge(sem("rope_sin"), 1)
            chain(dve.tensor_tensor(sh[:, :, :], sh[:, :, :], sh[:, :, :], ALU.mult))
            dve.tensor_scalar(cosT[:, :, :], sh[:, :, :], -2.0, 1.0, ALU.mult, ALU.add).then_inc(sem("rope_done"), 1)

        has_mla = any(kind == "mla" for kind, _ in stages)
        PES = {"ffn": ffn_pe, "ple": ple_pe, "hyb": hyb_pe, "mla": mla_pe}
        ACTS = {"ffn": ffn_act, "ple": ple_act, "hyb": hyb_act, "mla": mla_act}
        DVES = {"ffn": ffn_dve, "ple": ple_dve, "hyb": hyb_dve, "mla": mla_dve}
        POOL = {"ffn": ffn_pool, "ple": lambda pool, s: None, "hyb": hyb_pool, "mla": mla_pool}

        block = ctx.enter_context(nc.Block())

        @block.sync
        def _(sp):
            sp.dma_start(h[:, :, :], a["x"].rearrange("(t p) n -> p t n", p=P)).then_inc(sem("x_loaded"), 16)
            for n in range(2 * RING):
                load_unit(sp, n)
            rounds = (n_units - 2 * RING) // RING
            with sp.Fori(0, rounds) as k:
                for j in range(RING):
                    load_unit(sp, 2 * RING + j, k, RING)
            for n in range((2 + rounds) * RING, n_units):
                load_unit(sp, n)
            for t in range(2):
                h_ready(sp, NS, t)
                sp.dma_start(out[t * P:(t + 1) * P, :], h[:, t, :]).then_inc(sem("stored"), 16)
            sp.wait_ge(sem("stored"), 32)

        @block.gpsimd
        def _(pool):
            pool.dma_start(QG[:, :], a["pre_g"][0, :].partition_broadcast(P)).then_inc(sem("qg"), 16)
            pool.memset(ident[:, :], 0.0)
            pool.memset(tri[:, :], 1.0)
            pool.memset(cmask[:, :], 0.0)
            pool.memset(zeros[:, :], 0.0)
            link(pool, "pool_chain", pool.memset(nhalf[:, :], -0.5))
            pool.affine_select(out=ident[:, :], in_=ident[:, :], compare_op=ALU.not_equal, fill=1.0, base=0,
                               pattern=[[-1, P]], channel_multiplier=1)
            pool.affine_select(out=tri[:, :], in_=tri[:, :], compare_op=ALU.is_ge, fill=0.0, base=0,
                               pattern=[[1, P]], channel_multiplier=-1)
            pool.affine_select(out=cmask[:, P:2 * P], in_=cmask[:, P:2 * P], compare_op=ALU.is_ge, fill=NEG,
                               base=0, pattern=[[-1, P]], channel_multiplier=1).then_inc(sem("consts"), 1)
            prelude_pool(pool)
            for s, (kind, _) in enumerate(stages):
                boundary_pool(pool, s)
                POOL[kind](pool, s)
            boundary_pool(pool, NS)

        @block.scalar
        def _(act):
            done, split_to = splitter(act, split_hi)
            prelude_act(act)
            split_to(1)
            for s, (kind, _) in enumerate(stages):
                boundary_act(act, s, split_to)
                ACTS[kind](act, s, done, split_to)
            boundary_act(act, NS, split_to)

        @block.vector
        def _(dve):
            done, split_to = splitter(dve, split_lo)
            prelude_dve(dve)
            split_to(1)
            for s, (kind, _) in enumerate(stages):
                boundary_dve(dve, s, split_to)
                DVES[kind](dve, s, done, split_to)
            boundary_dve(dve, NS, split_to)

        @block.tensor
        def _(pe):
            pe.wait_ge(sem("consts"), 1)
            for s, (kind, _) in enumerate(stages):
                if kind == "ple":
                    ple_ahead_pe(pe, s)
                for t in range(2):
                    transpose_x(pe, s, t)
                PES[kind](pe, s)


def units_of(w, kts, cols):
    K, N = w.shape
    v = w.reshape(K // (kts * P), kts, P, N // cols, cols)
    return v.transpose(3, 0, 2, 1, 4).reshape(-1, P, kts * cols)


def ffn_units(w_in, w_down):
    gate, up = w_in[:, :D_FF], w_in[:, D_FF:]
    whole = FULL * CHUNK
    out, down = [], units_of(w_down, 2, D)
    for c in range(FULL):
        for w in (gate, up):
            out.append(units_of(w[:, c * CHUNK:(c + 1) * CHUNK], 4, CHUNK))
        if c:
            out.append(down[2 * (c - 1):2 * c])
    for w in (gate, up):
        out.append(units_of(w[:, whole:], 8, CHUNK // 2))
    out += [down[2 * (FULL - 1):2 * FULL], down[2 * FULL:]]
    return out


def hybrid_units(w_in, w_out):
    u, v = w_in[:, :GM_W], w_in[:, GM_W:2 * GM_W]
    z = w_in[:, 2 * GM_W:2 * GM_W + SSD_IN]
    xbc = w_in[:, 2 * GM_W + SSD_IN:2 * GM_W + SSD_IN + CONV_CH]
    return [units_of(c, 4, CHUNK) for c in (xbc, z, v, u)] + [units_of(w_out, 2, D)]


def mla_units(w_in, w_uq, w_ukv, w_out):
    pad = np.zeros((D, BANK - w_in.shape[1]), w_in.dtype)
    q = w_uq.reshape(Q_LORA, HEADS, NOPE + ROPE)
    kv = w_ukv.reshape(KV_LORA, HEADS, NOPE + VD)
    return [units_of(np.concatenate([w_in, pad], axis=1), 4, BANK),
            units_of(kv[:, :, :NOPE].reshape(KV_LORA, HEADS * NOPE), 1, UNIT),
            units_of(q[:, :, NOPE:].reshape(Q_LORA, HEADS * ROPE), 2, D),
            units_of(q[:, :, :NOPE].reshape(Q_LORA, HEADS * NOPE), 2, D),
            units_of(kv[:, :, NOPE:].reshape(KV_LORA, HEADS * VD), 1, UNIT),
            units_of(w_out, 2, D)]


def mixer_arrays(w):
    dt_w = w["hyb_w_in"][0][:, 2 * GM_W + SSD_IN + CONV_CH:]
    conv_w = w["ssd_conv_w"][0].T.reshape(CONV_CH // P, P, 4).transpose(1, 0, 2).reshape(P, -1)
    conv_b = w["ssd_conv_b"][0].reshape(CONV_CH // P, P).T
    inv = np.float32(1.0) / np.float32(ROPE_BASE) ** (np.arange(0, ROPE, 2, dtype=np.float32) / np.float32(ROPE))
    return {
        "dt_w": dt_w.reshape(KT, P, HEADS).transpose(1, 0, 2),
        "hy_cols": np.concatenate([conv_w, conv_b, w["gm_b_s"][0].T], axis=1),
        "hy_rows": np.concatenate([w["ssd_d"][0], w["ssd_dt_bias"][0], w["ssd_a_log"][0]]),
        "gm_w": w["gm_w_s"][0].transpose(2, 0, 1),
        "gm_g": w["gm_ln_g"][0],
        "gm_b": w["gm_ln_b"][0],
        "ssd_g": w["ssd_norm_g"][0],
        "q_g": w["mla_q_norm_g"][0],
        "kv_g": w["mla_kv_norm_g"][0],
        "positions": w["positions"][0].reshape(2, P).T,
        "inv": inv,
    }


def stream_of(stages, w):
    out = []
    for kind, i in stages:
        if kind == "ffn":
            name = "ffn1" if i % 2 == 0 else "ffn2"
            out += ffn_units(w[name + "_w_in"][i // 2], w[name + "_w_down"][i // 2])
        elif kind == "ple":
            out.append(units_of(w["ple_w_proj"][i], 2, D))
            out.append(units_of(w["ple_w_gate"][i], 2, D))
        elif kind == "hyb":
            out += hybrid_units(w["hyb_w_in"][0], w["hyb_w_out"][0])
        else:
            out += mla_units(w["mla_w_in"][0], w["mla_w_uq"][0], w["mla_w_ukv"][0], w["mla_w_out"][0])
    return np.concatenate(out, axis=0)


def gains_of(stages, w, side):
    out = []
    for n, (kind, i) in enumerate(stages):
        name = {"ffn": "ffn1" if i % 2 == 0 else "ffn2", "ple": "ple", "hyb": "mix", "mla": "mix"}[kind]
        layer = i // 2 if kind == "ffn" else 1 if kind == "mla" else i
        out.append(w[f"{name}_{side}_g"][layer])
    return np.stack(out)


def kernel(**inputs):
    import concourse.bacc as _bacc
    from concourse.bass_utils import run_bass_kernel_spmd as _run

    w = {n: np.asarray(v) for n, v in inputs.items()}
    arrays = {
        "x": w["x"][0],
        "stream": stream_of(STAGES, w),
        "pre_g": gains_of(STAGES, w, "pre"),
        "post_g": gains_of(STAGES, w, "post"),
        "p_t": w["p"][:, 0].transpose(0, 2, 1),
    }
    arrays.update(mixer_arrays(w))
    arrays = {n: np.ascontiguousarray(v) for n, v in arrays.items()}
    nc = _bacc.Bacc("TRN2", target_bir_lowering=False, num_devices=1)
    aps = {n: nc.dram_tensor(n, v.shape, mybir.dt.from_np(v.dtype), kind="ExternalInput").ap()
           for n, v in arrays.items()}
    out = nc.dram_tensor("out", (SEQ, D), mybir.dt.float32, kind="ExternalOutput").ap()
    hybrid_trunk(nc, STAGES, aps, out)
    r = _run(nc, [arrays], core_ids=[0])
    return r.results[0]["out"].reshape(1, SEQ, D)
```

```python
from contextlib import ExitStack

import numpy as np

import concourse.bass as bass
from concourse import mybir

D = 1024
SEQ = 256
P = 128
D_FF = 2816
PLE = 256
BANK = 512
UNIT = 2048
RING = 3
KT = D // P
EPS = 1e-6
LN_EPS = 1e-5
CHUNK = 512
FULL = D_FF // CHUNK
FFN_UNITS = 33
GM_W = 1024
SSD_IN = 1024
CONV_CH = 1536
HEADS = 16
NOPE, ROPE, VD = 128, 64, 128
Q_LORA, KV_LORA = 256, 128
SCALE = float((NOPE + ROPE) ** -0.5)
ROPE_BASE = 10000.0
NEG = -1.0e30

STAGES = [("ffn", 0), ("hyb", 0), ("ffn", 1), ("ple", 0), ("ffn", 2), ("mla", 0), ("ffn", 3), ("ple", 1)]
N_UNITS = {"ffn": FFN_UNITS, "hyb": 26, "ple": 5, "mla": 15}


def hybrid_trunk(nc, stages, a, out):
    f32, f32r, bf16, i32 = mybir.dt.float32, mybir.dt.float32r, mybir.dt.bfloat16, mybir.dt.int32
    ALU = mybir.AluOpType
    ACT = mybir.ActivationFunctionType

    first = {}
    n_units = 0
    for s, (kind, _) in enumerate(stages):
        first[s] = n_units
        n_units += N_UNITS[kind]
    NS = len(stages)

    ctx = ExitStack()
    with ctx:
        base = 16512
        at = [base]

        def place(name, shape, dt=f32, offset=None):
            size = int(np.prod(shape[1:])) * (2 if dt == bf16 else 4)
            if offset is None:
                offset = at[0]
                at[0] += (size + 31) // 32 * 32
            return nc.alloc_sbuf_tensor_at(name, shape, dt, offset=offset)

        raw = place("raw", [P, RING, UNIT])
        WH = place("WH", [P, RING, UNIT], f32r)
        WL = place("WL", [P, RING, UNIT], f32r)
        x_at = at[0]
        XH = place("XH", [P, KT, SEQ], f32r)
        XL = place("XL", [P, KT, SEQ], f32r)
        c_at = at[0]
        CH = place("CH", [P, 16, SEQ], f32r)
        CL = place("CL", [P, 16, SEQ], f32r)
        h = place("h", [P, 2, D])
        PG = place("PG", [P, D])
        QG = place("QG", [P, D])
        hn_at = at[0]
        hn = place("hn", [P, 2, D])
        junk = place("junk", [P, 2, D])
        ident = place("ident", [P, P])
        zeros = place("zeros", [P, BANK], bf16)
        stat = place("stat", [P, 128])
        nhalf = place("nhalf", [P, 8])
        tri = place("tri", [P, P])
        cmask = place("cmask", [P, 2 * P])
        cosT = place("cosT", [P, 2, ROPE // 2])
        sinT = place("sinT", [P, 2, ROPE // 2])
        mark = place("mark", [P, 8])
        s_at = at[0]
        end = 229344

        sg = place("sg", [P, 2, CHUNK], offset=s_at)
        act_h = place("act_h", [P, 2, CHUNK], offset=s_at + 4096)
        HH = place("HH", [P, 4, SEQ], f32r, offset=c_at)
        HL = place("HL", [P, 4, SEQ], f32r, offset=c_at + 4096)
        TH = place("TH", [P, 2, SEQ], f32r, offset=s_at + 8192)
        TL = place("TL", [P, 2, SEQ], f32r, offset=s_at + 8192 + 2048)
        gsb = place("gsb", [P, 2, D], offset=s_at + 8192)
        p_raw = place("p_raw", [P, 2, SEQ], offset=c_at + 8192)
        p_hi = place("p_hi", [P, 2, SEQ], f32r, offset=c_at + 8192 + 2048)
        p_lo = place("p_lo", [P, 2, SEQ], f32r, offset=c_at + 8192 + 4096)

        PS = ctx.enter_context(nc.psum_tensor("PS", [P, 8, BANK], f32))
        A, B, C, T = 0, 1, 2, 3

        def acc(t):
            return PS[:, 4 + 2 * t:6 + 2 * t, :]

        sems = {}

        def sem(name):
            if name not in sems:
                sems[name] = ctx.enter_context(nc.semaphore(name))
            return sems[name]

        for name in ("raw0", "raw1", "raw2", "w_hi", "w_lo", "w_used", "x_loaded0", "x_loaded1", "consts", "pg", "qg",
                     "out_done", "ple_done", "post_sq", "post_y", "post_rs", "w_lo_pool", "h_new", "pre_sq", "pre_rs", "hn_done",
                     "x_tr", "x_hi", "x_lo", "gate", "silu", "up", "acted", "h_tr", "h_hi", "h_lo",
                     "act_chain", "dve_chain", "pool_chain", "stored"):
            sem(name)

        chains = {"dve_chain": 0, "pool_chain": 0}

        def link(eng, name, ins):
            chains[name] += 1
            ins.then_inc(sem(name), 1)
            eng.wait_ge(sem(name), chains[name])

        def unit_at(n, k, step):
            return n if k is None else k * step + n

        def load_unit(sp, n, k=None, step=0):
            if n >= RING:
                sp.wait_ge(sem("w_hi"), unit_at(n - RING + 1, k, step))
                sp.wait_ge(sem("w_lo"), unit_at(n - RING + 1, k, step))
            if k is None:
                src = a["stream"][n, :, :]
            else:
                src = a["stream"][bass.ds(k * step + n, 1), :, :].rearrange("a p n -> (a p) n")
            sp.dma_start(raw[:, n % RING, :], src).then_inc(sem(f"raw{n % RING}"), 16)

        def split_hi(act, n, k=None, step=0):
            if n >= n_units:
                return
            rounds = 16 * (n // RING + 1)
            act.wait_ge(sem(f"raw{n % RING}"), rounds if k is None else k * (16 * step // RING) + rounds)
            if n >= RING:
                act.wait_ge(sem("w_used"), unit_at(n - RING + 1, k, step))
            act.activation(WH[:, n % RING, :], raw[:, n % RING, :], ACT.Copy).then_inc(sem("w_hi"), 1)

        def split_lo(dve, n, k=None, step=0):
            if n >= n_units:
                return
            dve.wait_ge(sem("w_hi"), unit_at(n + 1, k, step))
            dve.tensor_tensor(WL[:, n % RING, :], raw[:, n % RING, :], WH[:, n % RING, :],
                              ALU.subtract).then_inc(sem("w_lo"), 1)

        def splitter(eng, split):
            done = [0]

            def split_to(n):
                while done[0] <= n:
                    split(eng, done[0])
                    done[0] += 1
            return done, split_to

        def whole(tile, n):
            return tile[:, n % RING, :]

        def product(pe, out_ap, xh, xl, wh, wl, start, stop):
            pe.matmul(out_ap, xh, wh, start=start, stop=False)
            pe.matmul(out_ap, xl, wh, start=False, stop=False)
            return pe.matmul(out_ap, xh, wl, start=False, stop=stop)

        def tok(t):
            return slice(t * P, (t + 1) * P)

        def lagged(units):
            units = list(units)
            order = [(units[0], 0)]
            for j in range(1, len(units)):
                order += [(units[j], 0), (units[j - 1], 1)]
            return order + [(units[-1], 1)]

        def wide(pe, n, t, bank, xh, xl, kt, start, stop, done=None, k=None, step=0):
            pe.wait_ge(sem("w_lo"), unit_at(n + 1, k, step))
            wh = whole(WH, n).rearrange("p (k n) -> p k n", k=2)
            wl = whole(WL, n).rearrange("p (k n) -> p k n", k=2)
            for c in range(2):
                for q in range(2):
                    ins = product(pe, PS[:, bank + c, :], xh[:, kt + q, tok(t)], xl[:, kt + q, tok(t)],
                                  wh[:, q, c * BANK:(c + 1) * BANK], wl[:, q, c * BANK:(c + 1) * BANK],
                                  start and q == 0, stop and q == 1)
                if (t, c) == (1, 1):
                    ins.then_inc(sem("w_used"), 1)
                elif done:
                    ins.then_inc(sem(done), 1)

        def col(s, t, what):
            c = (2 * s + t) * 8 + what
            return stat[:, c:c + 1]

        SQ, RS = 0, 1
        POST_RS, POST_SQ = 2, 3

        def post_factor(s):
            return 0.5 if stages[s][0] == "ffn" else 1.0

        def half(a_):
            return slice(a_ * BANK, (a_ + 1) * BANK)

        def source(s, t, b):
            n = 2 * t + b
            if stages[s][0] == "ple":
                return gsb[:, t, half(b)], sem("ple_done"), 4 * sum(k == "ple" for k, _ in stages[:s]) + n + 1
            if n == 3:
                return PS[:, 7, :], sem("w_used"), first[s] + N_UNITS[stages[s][0]]
            return PS[:, 4 + n, :], sem("out_done"), 3 * sum(k != "ple" for k, _ in stages[:s]) + n + 1

        def post_square(act, s, t):
            for b in range(2):
                if stages[s][0] == "ple":
                    ple_sigmoid(act, s, t, b)
            for b in range(2):
                src, ready, value = source(s, t, b)
                act.wait_ge(ready, value)
                act.activation(junk[:, t, half(b)], src, ACT.Square, scale=1.0 / 32 / post_factor(s),
                               accum_out=col(s, t, POST_SQ + b)).then_inc(sem("post_sq"), 1)

        def h_ready(eng, s, t, b=1):
            if s:
                eng.wait_ge(sem("h_new"), 4 * (s - 1) + 2 * t + b + 1)
            else:
                eng.wait_ge(sem(f"x_loaded{t}"), 16)

        def pre_square(act, s, t):
            h_ready(act, s, t)
            act.activation(junk[:, t, :], h[:, t, :], ACT.Square, scale=1.0 / 32, accum_out=col(s, t, SQ))\
               .then_inc(sem("pre_sq"), 1)

        def inverse_rms(pool, s, t):
            link(pool, "pool_chain", pool.tensor_scalar(col(s, t, RS), col(s, t, SQ), 1.0, EPS, ALU.mult, ALU.add))
            pool.tensor_tensor(col(s, t, RS), col(s, t, RS), nhalf[:, 0:1], ALU.pow).then_inc(sem("pre_rs"), 1)

        def gained(dve, s, t, b):
            src, ready, value = source(s, t, b)
            dve.wait_ge(ready, value)
            dve.wait_ge(sem("post_sq"), 4 * s + 2 * t + b + 1)
            if (t, b) == (0, 0):
                dve.wait_ge(sem("pg"), 16 * (s + 1))
            dve.tensor_tensor(hn[:, t, half(b)], src, PG[:, half(b)], ALU.mult).then_inc(sem("post_y"), 1)

        def post_inverse_rms(pool, s, t):
            pool.wait_ge(sem("post_sq"), 4 * s + 2 * t + 2)
            link(pool, "pool_chain", pool.tensor_scalar(col(s, t, POST_RS), col(s, t, POST_SQ), col(s, t, POST_SQ + 1),
                                                        EPS / post_factor(s) ** 2, ALU.add, ALU.add))
            pool.tensor_tensor(col(s, t, POST_RS), col(s, t, POST_RS), nhalf[:, 0:1], ALU.pow)\
                .then_inc(sem("post_rs"), 1)

        def update_h(dve, s, t, b):
            dve.wait_ge(sem("post_y"), 4 * s + 2 * t + b + 1)
            dve.scalar_tensor_tensor(h[:, t, half(b)], hn[:, t, half(b)], col(s, t, POST_RS), h[:, t, half(b)],
                                     ALU.mult, ALU.add).then_inc(sem("h_new"), 1)

        def behind(dve, s, t):
            if s >= 0:
                if stages[s][0] == "ple":
                    ple_product(dve, s, t, 0)
                    ple_product(dve, s, t, 1)
                for b in range(2):
                    gained(dve, s, t, b)
                dve.wait_ge(sem("post_rs"), 2 * s + t + 1)
                if t == 1 and s + 1 < NS:
                    dve.wait_ge(sem("w_lo_pool"), s + 1)
                    dve.memset(mark[:, :], 0.0).then_inc(sem("w_lo"), 1)
            for b in range(2):
                if s >= 0:
                    update_h(dve, s, t, b)
                if s + 1 < NS:
                    normed(dve, s + 1, t, b)

        def normed(dve, s, t, b):
            h_ready(dve, s, t, b)
            if (t, b) == (0, 0):
                dve.wait_ge(sem("qg"), 16 * (s + 1))
            dve.tensor_tensor(hn[:, t, half(b)], h[:, t, half(b)], QG[:, half(b)], ALU.mult)\
               .then_inc(sem("hn_done"), 1)

        def x_bank(s, t, a_):
            return (2 * t if t == 0 or stages[s][0] != "ffn" else 4) + a_

        def transpose_x(pe, s, t):
            for a_ in range(2):
                pe.wait_ge(sem("hn_done"), 4 * s + 2 * t + a_ + 1)
                for q in range(4):
                    kt = 4 * a_ + q
                    ins = pe.transpose(PS[:, x_bank(s, t, a_), q * P:(q + 1) * P], hn[:, t, kt * P:(kt + 1) * P],
                                       ident[:, :])
                ins.then_inc(sem("x_tr"), 1)

        def x_there(pe, s, t, a_):
            pe.wait_ge(sem("x_lo"), 4 * s + 2 * t + a_ + 1)

        def x_half(tile, t, a_):
            return tile[:, 4 * a_:4 * a_ + 4, tok(t)]

        def x_psum(s, t, a_):
            return PS[:, x_bank(s, t, a_), :].rearrange("p (k n) -> p k n", n=P)

        def x_high(act, s, t):
            for a_ in range(2):
                act.wait_ge(sem("x_tr"), 4 * s + 2 * t + a_ + 1)
                act.activation(x_half(XH, t, a_), x_psum(s, t, a_), ACT.Copy).then_inc(sem("x_hi"), 1)

        def x_low(dve, s, t):
            for a_ in range(2):
                dve.wait_ge(sem("x_hi"), 4 * s + 2 * t + a_ + 1)
                dve.tensor_tensor(x_half(XL, t, a_), x_psum(s, t, a_), x_half(XH, t, a_), ALU.subtract)\
                   .then_inc(sem("x_lo"), 1)

        def boundary_act(act, s, split_to):
            m = first[s] if s < NS else n_units
            if s:
                post_square(act, s - 1, 0)
            if s == NS:
                post_square(act, s - 1, 1)
                return
            split_to(m + 1)
            x_high(act, s, 0)
            if s:
                post_square(act, s - 1, 1)
            pre_square(act, s, 0)
            split_to(m + 2)
            x_high(act, s, 1)
            pre_square(act, s, 1)

        def boundary_dve(dve, s, done, split_to):
            m = first[s] if s < NS else n_units
            behind(dve, s - 1, 0)
            if s == NS:
                behind(dve, s - 1, 1)
                return
            x_low(dve, s, 0)
            if s:
                done[0] = m + 2
            behind(dve, s - 1, 1)
            split_to(m + 2)
            x_low(dve, s, 1)

        def boundary_pool(pool, s):
            if s:
                post_inverse_rms(pool, s - 1, 0)
                if s < NS:
                    n = first[s] + 1
                    pool.wait_ge(sem("w_hi"), n + 1)
                    pool.tensor_tensor(whole(WL, n), whole(raw, n), whole(WH, n), ALU.subtract)\
                        .then_inc(sem("w_lo_pool"), 1)
                post_inverse_rms(pool, s - 1, 1)
            if s == NS:
                return
            for t in range(2):
                pool.wait_ge(sem("pre_sq"), 2 * s + t + 1)
                inverse_rms(pool, s, t)
            if s:
                pool.wait_ge(sem("post_y"), 4 * s)
            pool.dma_start(PG[:, :], a["post_g"][s, :].partition_broadcast(P)).then_inc(sem("pg"), 16)
            if s + 1 < NS:
                pool.wait_ge(sem("hn_done"), 4 * s + 4)
                pool.dma_start(QG[:, :], a["pre_g"][s + 1, :].partition_broadcast(P)).then_inc(sem("qg"), 16)

        def ffn_chunk_pe(pe, f, s, g, c, k=None, half=False):
            def n2(t):
                v = 12 * f + 2 * c + t + 1
                return v if k is None else k * 2 + v

            def n1(d=0):
                v = 6 * f + c + 1 - d
                return v if k is None else k + v

            start = c == 0 and k is None
            width = CHUNK // 2 if half else CHUNK
            units = 1 if half else 2
            per = KT // units
            pairs = [(j, t) for j in range(2 * units) for t in range(2)]
            for j, t in lagged(range(4)) if start else pairs:
                up, part = j // units, j % units
                if start and (j, t) == (0, 1):
                    transpose_x(pe, s, 1)
                n = g + j
                pe.wait_ge(sem("w_lo"), unit_at(n + 1, k, 6))
                wh = whole(WH, n).rearrange("p (k n) -> p k n", k=per)
                wl = whole(WL, n).rearrange("p (k n) -> p k n", k=per)
                if start and not up:
                    x_there(pe, s, t, part)
                if up and part == 0 and t == 0 and not start:
                    pe.wait_ge(sem("h_lo"), n1(1))
                if up and part == 0 and t == 1:
                    pe.wait_ge(sem("silu"), n2(0))
                bank = (C, A)[t] if up else (A, B)[t]
                for q in range(per):
                    kt = part * per + q
                    ins = product(pe, PS[:, bank, 0:width], XH[:, kt, tok(t)], XL[:, kt, tok(t)],
                                  wh[:, q, :], wl[:, q, :], kt == 0, kt == KT - 1)
                if t == 1:
                    ins.then_inc(sem("w_used"), 1)
                elif part == units - 1:
                    ins.then_inc(sem("up" if up else "gate"), 1)
            return n2, n1

        def ffn_down_pe(pe, g, j, t, k=None):
            wide(pe, g + j, t, 4 + 2 * t, HH, HL, 2 * j, False, False, None, k, 6)

        def ffn_transpose_pe(pe, n2, kts=4):
            for t in range(2):
                pe.wait_ge(sem("acted"), n2(t))
            for q in range(kts):
                for t in range(2):
                    ins = pe.transpose(PS[:, C + q // 2, (q % 2) * SEQ + t * P:(q % 2) * SEQ + (t + 1) * P],
                                       act_h[:, t, q * P:(q + 1) * P], ident[:, :])
            ins.then_inc(sem("h_tr"), 1)

        def ffn_pe(pe, s):
            f, u = stages[s][1], first[s]
            n2, n1 = ffn_chunk_pe(pe, f, s, u, 0)
            for b in range(4, 8):
                pe.matmul(PS[:, b, :], zeros[:, 0:P], zeros[:, :], start=True, stop=False)
            ffn_transpose_pe(pe, n2)
            with pe.Fori(0, FULL - 1) as k:
                n2, n1 = ffn_chunk_pe(pe, f, s, u + 4, 1, k)
                for j in range(2):
                    for t in range(2):
                        ffn_down_pe(pe, u + 8, j, t, k)
                ffn_transpose_pe(pe, n2)
            g = u + 4 + 6 * (FULL - 1)
            n2, n1 = ffn_chunk_pe(pe, f, s, g, FULL, half=True)
            ffn_down_pe(pe, g + 2, 0, 0)
            ffn_down_pe(pe, g + 2, 1, 0)
            ffn_transpose_pe(pe, n2, 2)
            ffn_down_pe(pe, g + 2, 0, 1)
            pe.wait_ge(sem("h_lo"), n1())
            wide(pe, g + 4, 0, 4, TH, TL, 0, False, True, "out_done")
            ffn_down_pe(pe, g + 2, 1, 1)
            wide(pe, g + 4, 1, 6, TH, TL, 0, False, True, "out_done")

        def ffn_product_done(eng, name, f, c, t, n, k):
            if t == 0:
                eng.wait_ge(sem(name), unit_at(6 * f + c + 1, k, 1))
            else:
                eng.wait_ge(sem("w_used"), unit_at(n + 1, k, 6))

        def ffn_silu(act, s, f, c, n, k=None, width=CHUNK):
            for t in range(2):
                v = 12 * f + 2 * c + t + 1
                ffn_product_done(act, "gate", f, c, t, n, k)
                if c == 0:
                    act.wait_ge(sem("pre_rs"), 2 * s + t + 1)
                if v > 2:
                    act.wait_ge(sem("acted"), v - 2 if k is None else k * 2 + (v - 2))
                act.activation(sg[:, t, 0:width], PS[:, (A, B)[t], 0:width], ACT.Silu, scale=col(s, t, RS))\
                   .then_inc(sem("silu"), 1)

        def h_bank(kts):
            return PS[:, C:C + (kts + 1) // 2, :]

        def h_tile(tile, kts):
            return tile[:, 0:kts, :].rearrange("p (a k) n -> p a (k n)", k=2)

        def ffn_high(act, f, c, k=None, kts=4, high=HH):
            v = 6 * f + c + 1
            act.wait_ge(sem("h_tr"), v if k is None else k + v)
            act.activation(h_tile(high, kts), h_bank(kts), ACT.Copy).then_inc(sem("h_hi"), 1)

        def ffn_low(dve, f, c, k=None, kts=4, high=HH, low=HL):
            v = 6 * f + c + 1
            dve.wait_ge(sem("h_hi"), v if k is None else k + v)
            dve.tensor_tensor(h_tile(low, kts), h_bank(kts), h_tile(high, kts), ALU.subtract)\
               .then_inc(sem("h_lo"), 1)

        def ffn_mult(dve, s, f, c, n, k=None, width=CHUNK):
            for t in range(2):
                ffn_product_done(dve, "up", f, c, t, n, k)
                if c == 0:
                    dve.wait_ge(sem("silu"), 12 * f + t + 1)
                if t == 0 and 6 * f + c > 0:
                    w = 6 * f + c
                    dve.wait_ge(sem("h_tr"), w if k is None else k + w)
                dve.scalar_tensor_tensor(act_h[:, t, 0:width], PS[:, (C, A)[t], 0:width], col(s, t, RS),
                                         sg[:, t, 0:width], ALU.mult, ALU.mult).then_inc(sem("acted"), 1)

        def ffn_act(act, s, done, split_to):
            f, u = stages[s][1], first[s]
            split_to(u + 3)
            ffn_silu(act, s, f, 0, u + 1)
            if s == 0:
                prelude_act(act)
            split_to(u + 5)
            ffn_high(act, f, 0)
            with act.Fori(0, FULL - 1) as k:
                g = u + 4
                split_hi(act, g + 2, k, 6)
                split_hi(act, g + 3, k, 6)
                ffn_silu(act, s, f, 1, g + 1, k)
                for j in range(4, 8):
                    split_hi(act, g + j, k, 6)
                ffn_high(act, f, 1, k)
            g = u + 4 + 6 * (FULL - 1)
            done[0] = g + 2
            split_to(g + 2)
            ffn_silu(act, s, f, FULL, g, width=CHUNK // 2)
            split_to(g + 4)
            if s + 1 < NS and stages[s + 1][0] == "ple":
                act.wait_ge(sem("p_loaded"), 16 * (stages[s + 1][1] + 1))
                act.activation(p_hi[:, :, :], p_raw[:, :, :], ACT.Copy).then_inc(sem("p_hi"), 1)
            ffn_high(act, f, FULL, kts=2, high=TH)
            split_to(g + 5)

        def ffn_dve(dve, s, done, split_to):
            f, u = stages[s][1], first[s]
            if s == 0:
                prelude_dve(dve)
            split_to(u + 4)
            ffn_mult(dve, s, f, 0, u + 3)
            split_to(u + 5)
            ffn_low(dve, f, 0)
            if s == 0:
                prelude_dve_end(dve)
            with dve.Fori(0, FULL - 1) as k:
                g = u + 4
                for j in range(2, 7):
                    split_lo(dve, g + j, k, 6)
                ffn_mult(dve, s, f, 1, g + 3, k)
                split_lo(dve, g + 7, k, 6)
                ffn_low(dve, f, 1, k)
            g = u + 4 + 6 * (FULL - 1)
            done[0] = g + 2
            split_to(g + 4)
            ffn_mult(dve, s, f, FULL, g + 1, width=CHUNK // 2)
            if s + 1 < NS and stages[s + 1][0] == "ple":
                dve.wait_ge(sem("p_hi"), stages[s + 1][1] + 1)
                dve.tensor_tensor(p_lo[:, :, :], p_raw[:, :, :], p_hi[:, :, :], ALU.subtract)\
                   .then_inc(sem("p_lo"), 1)
            ffn_low(dve, f, FULL, kts=2, high=TH, low=TL)
            split_to(g + 5)

        def ffn_pool(pool, s):
            if s + 1 < NS and stages[s + 1][0] == "hyb":
                hyb_early(pool)
            if s + 1 < NS and stages[s + 1][0] == "mla":
                h_ready(pool, s, 1)
                mla_early(pool)
            if s + 1 < NS and stages[s + 1][0] == "ple":
                h_ready(pool, s, 1)
                pool.dma_start(p_raw[:, :, :], a["p_t"][stages[s + 1][1]].rearrange("(k p) n -> p k n", p=P))\
                    .then_inc(sem("p_loaded"), 16)

        def ple_pe(pe, s):
            i, u = stages[s][1], first[s]
            pe.wait_ge(sem("p_lo"), i + 1)
            for t in range(2):
                pe.wait_ge(sem("post_sq"), 4 * (s - 1) + 2 * t + 2)
                pe.wait_ge(sem("post_y"), 4 * (s - 1) + 2 * t + 2)
                wide(pe, u, t, 4 + 2 * t, p_hi, p_lo, 0, True, True)
            for j, t in lagged(range(4)):
                if (j, t) == (0, 1):
                    transpose_x(pe, s, 1)
                if j == 0:
                    x_there(pe, s, t, 1)
                wide(pe, u + 1 + j, t, 2 * t, XH, XL, 2 * j, j == 0, j == 3, "ple_gate" if j == 3 else None)

        def ple_sigmoid(act, s, t, b):
            i, n = stages[s][1], 2 * t + b
            if n < 3:
                act.wait_ge(sem("ple_gate"), 3 * i + n + 1)
            else:
                act.wait_ge(sem("w_used"), first[s] + 5)
            act.wait_ge(sem("pre_rs"), 2 * s + t + 1)
            act.activation(gsb[:, t, half(b)], PS[:, n, :], ACT.Sigmoid, scale=col(s, t, RS)).then_inc(sem("ple_sig"), 1)

        def ple_product(dve, s, t, b):
            n = 2 * t + b
            dve.wait_ge(sem("ple_sig"), 4 * stages[s][1] + n + 1)
            dve.tensor_tensor(gsb[:, t, half(b)], PS[:, 4 + n, :], gsb[:, t, half(b)], ALU.mult)\
               .then_inc(sem("ple_done"), 1)

        def ple_act(act, s, done, split_to):
            split_to(first[s] + 5)

        def ple_dve(dve, s, done, split_to):
            split_to(first[s] + 5)

        for name in ("p_loaded", "p_hi", "p_lo", "ple_gate", "ple_sig"):
            sem(name)

        XBC, Z, V, UU = (0, 1, 2), (3, 4), (5, 6), (7, 8)
        P0, P1, P2, CT = 0, 4, 6, 2
        PAIR = [P0, P1, P2, P0, P2, P0, P1, P2, P0]
        NCH = CONV_CH // P
        GH = 8
        STATE = 128

        def pair(b):
            return PS[:, b:b + 2, :]

        def flat_pair(b):
            return pair(b).rearrange("p a n -> p (a n)")

        o = s_at
        cx = place("cx", [P, NCH, SEQ + 3], offset=o); o += NCH * (SEQ + 3) * 4 + 16
        xs = place("xs", [P, 2, SSD_IN], offset=o); o += 8192
        xd = place("xd", [P, 2, SSD_IN], offset=o); o += 8192
        zs = place("zs", [P, 2, SSD_IN], offset=o); o += 8192
        Eg = place("Eg", [P, 2, GH, P], offset=o); o += 8192
        cbm = place("cbm", [P, 4, P], offset=o); o += 2048
        sm_at = o
        sm = place("sm", [P, 512], offset=o); o += 2048
        Btok = place("Btok", [P, 2 * STATE], offset=o); o += 1024
        assert o <= end, o
        vt = hn
        gm_g = place("gm_g", [P, GM_W], offset=c_at)
        gm_b = place("gm_b", [P, GM_W], offset=c_at + 4096)
        dt_w = place("dt_w", [P, KT, HEADS], offset=c_at + 16384)
        dt_hi = place("dt_hi", [P, KT, HEADS], f32r, offset=c_at + 16384 + 512)
        dt_lo = place("dt_lo", [P, KT, HEADS], f32r, offset=c_at + 16384 + 1024)
        wsT = place("wsT", [P, 8, P], offset=c_at + 16384 + 4096)
        ca = place("ca", [P, 4, SEQ], offset=c_at + 8192)
        xde = place("xde", [P, SSD_IN], offset=c_at + 12288)
        ug = place("ug", [P, 2, 2, CHUNK], offset=c_at + 16384 + 8192)
        xt = place("xt", [P, 2, CHUNK], offset=c_at + 16384 + 12288)
        stT = place("stT", [P, 2, BANK], offset=x_at + 8192)
        yo = place("yo", [P, SSD_IN], offset=x_at + 12288)
        ng = place("ng", [P, SSD_IN], offset=x_at + 4096)

        def smc(lo, n):
            return sm[:, lo:lo + n]
        CW, CB, BS = smc(0, 48), smc(48, 12), smc(60, 8)
        DV, DTB, ALOG = smc(68, 16), smc(84, 16), smc(100, 16)
        X0 = sm[:, 116:148]
        NA, EX, S1, S2, PO, DT, DA = (smc(148 + 32 * i, 32) for i in range(7))
        ACS = smc(372, 48)
        DTE, EA, NEGA = smc(420, 16), smc(436, 16), smc(452, 16)
        BN = Eg[:, 1, 0:1, 0:96].rearrange("p a b -> p (a b)")
        MV = smc(468, 16)
        RV = smc(484, 8)
        GQ = smc(492, 8)

        for name in ("hy_small", "hy_dtw", "hy_gm", "hy_ws", "hy_wsm", "hy_ng", "hy_ev", "hy_trx", "hy_cx", "hy_pad",
                     "hy_ca", "hy_conv", "hy_dth", "hy_dtl", "hy_dtp", "hy_dtv", "hy_na", "hy_ex", "hy_al",
                     "hy_da", "hy_acs", "hy_acv", "hy_dea", "hy_dte", "hy_back", "hy_xs", "hy_xd", "hy_bc",
                     "hy_bt", "hy_cbm", "hy_abc", "hy_seg", "hy_exp", "hy_G", "hy_mv", "hy_rv", "hy_vn", "hy_v", "hy_t0",
                     "hy_mix", "hy_mixv", "hy_ya", "hy_trya", "hy_yahi", "hy_yalo", "hy_yd", "hy_st", "hy_stv",
                     "hy_yo", "hy_yoff", "hy_y", "hy_ysq", "hy_yrs", "hy_yn", "hy_try", "hy_yhi", "hy_ylo"):
            sem(name)

        def heads(ap, n=HEADS):
            return ap.rearrange("p (h q) -> p h q", h=n)

        def per_head(ap, n, width):
            return ap.unsqueeze(2).broadcast_to([P, n, width])

        def gemm_free(pe, idx):
            before = {3: 1, 4: 3, 5: 4, 7: 5, 8: 6}
            if idx in before:
                pe.wait_ge(sem("hy_ev"), before[idx])
            if idx == 6:
                pe.wait_ge(sem("hy_dtv"), 1)

        def hyb_pe(pe, s):
            u = first[s]

            def gemm(idx, parts=(0, 1)):
                if parts[0] == 0:
                    gemm_free(pe, idx)
                order = lagged(range(2)) if idx == 0 else [(j, t) for j in parts for t in range(2)]
                for j, t in order:
                    if idx == 0:
                        if (j, t) == (0, 1):
                            transpose_x(pe, s, 1)
                        x_there(pe, s, t, j)
                    n = u + 2 * idx + j
                    pe.wait_ge(sem("w_lo"), n + 1)
                    wh = whole(WH, n).rearrange("p (k n) -> p k n", k=4)
                    wl = whole(WL, n).rearrange("p (k n) -> p k n", k=4)
                    for q in range(4):
                        kt = 4 * j + q
                        ins = product(pe, PS[:, PAIR[idx] + t, :], XH[:, kt, tok(t)], XL[:, kt, tok(t)],
                                      wh[:, q, :], wl[:, q, :], kt == 0, kt == KT - 1)
                    if t == 1:
                        ins.then_inc(sem("w_used"), 1)

            def transpose_conv_input(j):
                pe.wait_ge(sem("hy_ev"), j + 1)
                if j:
                    pe.wait_ge(sem("hy_cx"), j)
                for q in range(4):
                    for t in range(2):
                        ins = pe.transpose(PS[:, CT + q // 2, (q % 2) * SEQ + t * P:(q % 2) * SEQ + (t + 1) * P],
                                           xt[:, t, q * P:(q + 1) * P], ident[:, :])
                ins.then_inc(sem("hy_trx"), 1)

            def back(t):
                if t == 0:
                    pe.wait_ge(sem("hy_conv"), 2)
                    pe.wait_ge(sem("hy_acv"), 1)
                else:
                    pe.wait_ge(sem("hy_xd"), 1)
                for q in range(8):
                    ins = pe.transpose(PS[:, CT + q // 4, (q % 4) * P:(q % 4 + 1) * P],
                                       cx[:, q, 3 + t * P:3 + (t + 1) * P], ident[:, :])
                ins.then_inc(sem("hy_back"), 1)

            def cumulated(t, g):
                n = 2 * t + g
                if n == 0:
                    pe.wait_ge(sem("hy_cbm"), 1)
                    pe.wait_ge(sem("hy_bt"), 1)
                elif n == 2:
                    pe.wait_ge(sem("hy_yalo"), 2)
                else:
                    pe.wait_ge(sem("hy_seg"), n)
                for r in range(GH):
                    c = t * HEADS + g * GH + r
                    ins = pe.matmul(PS[:, CT + r // 4, (r % 4) * P:(r % 4 + 1) * P],
                                    DA[:, c:c + 1].broadcast_to([P, P]), tri[:, :], start=True, stop=True)
                ins.then_inc(sem("hy_abc"), 1)

            def mix(c):
                b = (P1, P2)[c]
                if c == 0:
                    pe.wait_ge(sem("hy_wsm"), 1)
                    pe.wait_ge(sem("hy_ev"), 7)
                else:
                    pe.wait_ge(sem("hy_ev"), 8)
                pe.wait_ge(sem("hy_v"), c + 1)
                for r in range(8):
                    ins = pe.matmul(PS[:, b + r // 4, (r % 4) * P:(r % 4 + 1) * P], wsT[:, r, :],
                                    vt[:, c, r * P:(r + 1) * P], start=True, stop=True)
                ins.then_inc(sem("hy_mix"), 1)

            def diagonal(t, g):
                pe.wait_ge(sem("hy_G"), 2 * t + g + 1)
                if g == 0:
                    if t == 0:
                        pe.wait_ge(sem("hy_ev"), 9)
                        pe.wait_ge(sem("hy_xd"), 2)
                    else:
                        pe.wait_ge(sem("hy_y"), 1)
                for r in range(GH):
                    ins = pe.matmul(PS[:, P0 + g, r * 64:(r + 1) * 64], Eg[:, g, r, :],
                                    xd[:, t, (g * GH + r) * 64:(g * GH + r + 1) * 64], start=True, stop=True)
                ins.then_inc(sem("hy_yd"), 1)

            def transpose_out(src, t, done):
                for q in range(8):
                    ins = pe.transpose(PS[:, CT + q // 4, (q % 4) * P:(q % 4 + 1) * P],
                                       src[:, t, q * P:(q + 1) * P], ident[:, :])
                ins.then_inc(sem(done), 1)

            def out_unit(j, t):
                if j == 0:
                    pe.wait_ge(sem("hy_mixv"), t + 1)
                    pe.wait_ge(sem("hy_yalo"), t + 1)
                if j == 4:
                    pe.wait_ge(sem("hy_ylo"), t + 1)
                wide(pe, u + 18 + j, t, 4 + 2 * t, CH, CL, 2 * j, j == 0, j == 7, "out_done" if j == 7 else None)

            gemm(0)
            gemm(1)
            transpose_conv_input(0)
            gemm(2)
            transpose_conv_input(1)
            gemm(3)
            transpose_conv_input(2)
            pe.wait_ge(sem("hy_dtl"), 1)
            pe.wait_ge(sem("hy_ev"), 2)
            for t in range(2):
                for kt in range(KT):
                    ins = product(pe, PS[:, P1, t * HEADS:(t + 1) * HEADS], XH[:, kt, tok(t)], XL[:, kt, tok(t)],
                                  dt_hi[:, kt, :], dt_lo[:, kt, :], kt == 0, kt == KT - 1)
            ins.then_inc(sem("hy_dtp"), 1)
            gemm(4)
            gemm(5)
            pe.wait_ge(sem("hy_da"), 1)
            pe.wait_ge(sem("hy_cx"), 3)
            pe.matmul(PS[:, C, 0:32], tri[:, :], DA, start=True, stop=True)
            pe.matmul(PS[:, C, 32:48], tri[:, P - 1:P].broadcast_to([P, P]), DA[:, 0:HEADS], start=True, stop=True)\
              .then_inc(sem("hy_acs"), 1)
            gemm(6, (0,))
            back(0)
            gemm(6, (1,))
            gemm(7, (0,))
            back(1)
            gemm(7, (1,))
            pe.wait_ge(sem("hy_xd"), 2)
            pe.wait_ge(sem("hy_conv"), 3)
            for g in range(2):
                pe.transpose(PS[:, C, g * P:(g + 1) * P], cx[:, 8 + g, 3:3 + P], ident[:, :])
            for t in range(2):
                for g in range(2):
                    ins = pe.matmul(PS[:, T, (2 * t + g) * P:(2 * t + g + 1) * P], cx[:, 8 + g, 3 + t * P:3 + (t + 1) * P],
                                    cx[:, 10 + g, 3 + t * P:3 + (t + 1) * P], start=True, stop=True)
            ins.then_inc(sem("hy_bc"), 1)
            gemm(8, (0,))
            cumulated(0, 0)
            gemm(8, (1,))
            mix(0)
            cumulated(0, 1)
            mix(1)

            def transpose_ya(t):
                pe.wait_ge(sem("hy_ya"), t + 1)
                if t == 0:
                    pe.wait_ge(sem("hy_seg"), 2)
                else:
                    pe.wait_ge(sem("hy_yalo"), 1)
                transpose_out(vt, t, "hy_trya")

            def transpose_y(t):
                pe.wait_ge(sem("hy_yn"), t + 1)
                pe.wait_ge(sem("hy_yoff" if t == 0 else "hy_ylo"), 1)
                transpose_out(xs, t, "hy_try")

            transpose_ya(0)
            diagonal(0, 0)
            diagonal(0, 1)
            out_unit(0, 0)
            transpose_ya(1)
            out_unit(1, 0)
            out_unit(0, 1)
            cumulated(1, 0)
            out_unit(1, 1)
            cumulated(1, 1)
            out_unit(2, 0)
            diagonal(1, 0)
            pe.wait_ge(sem("hy_seg"), 4)
            for g in range(2):
                ins = pe.matmul(PS[:, CT + g, :], Btok[:, g * P:(g + 1) * P], xde[:, g * BANK:(g + 1) * BANK],
                                start=True, stop=True)
            ins.then_inc(sem("hy_st"), 1)
            diagonal(1, 1)
            pe.wait_ge(sem("hy_stv"), 1)
            for g in range(2):
                ins = pe.matmul(PS[:, CT + g, :], cx[:, 10 + g, 3 + P:3 + 2 * P], stT[:, g, :], start=True, stop=True)
            ins.then_inc(sem("hy_yo"), 1)
            out_unit(2, 1)
            transpose_y(0)
            out_unit(3, 0)
            out_unit(3, 1)
            transpose_y(1)
            for j, t in lagged(range(4, 8)):
                out_unit(j, t)

        def hyb_act(act, s, done, split_to):
            u = first[s]

            def evacuate(idx):
                act.wait_ge(sem("w_used"), u + 2 * idx + 2)
                if idx in XBC:
                    if idx:
                        act.wait_ge(sem("hy_trx"), idx)
                    dst, f = xt[:, :, :], ACT.Copy
                elif idx in Z:
                    dst, f = zs[:, :, (idx - 3) * BANK:(idx - 2) * BANK], ACT.Silu
                elif idx in V:
                    dst, f = vt[:, :, (idx - 5) * BANK:(idx - 4) * BANK], ACT.Gelu_apprx_tanh
                else:
                    if idx == 8:
                        act.wait_ge(sem("hy_trx"), 3)
                    dst, f = ug[:, idx - 7, :, :], ACT.Gelu_apprx_tanh
                if idx == 0:
                    act.wait_ge(sem("pre_rs"), 2 * s + 2)
                for t in range(2):
                    ins = act.activation(dst[:, t, :], PS[:, PAIR[idx] + t, :], f, scale=col(s, t, RS))
                ins.then_inc(sem("hy_ev"), 1)

            def first_tap(j):
                act.wait_ge(sem("hy_cx"), j + 1)
                if j == 0:
                    act.wait_ge(sem("hy_pad"), 1)
                else:
                    act.wait_ge(sem("hy_conv"), j)
                for q in range(4):
                    c = 4 * j + q
                    ins = act.activation(ca[:, q, :], cx[:, c, 0:SEQ], ACT.Identity, bias=CB[:, c:c + 1],
                                         scale=CW[:, 4 * c:4 * c + 1])
                ins.then_inc(sem("hy_t0"), 1)

            def conv_silu(j):
                act.wait_ge(sem("hy_ca"), j + 1)
                act.activation(cx[:, 4 * j:4 * j + 4, 3:3 + SEQ], ca[:, :, :], ACT.Silu).then_inc(sem("hy_conv"), 1)

            def decay(n):
                act.wait_ge(sem("hy_seg"), n + 1)
                act.activation(Eg[:, n % 2, :, :], Eg[:, n % 2, :, :], ACT.Exp).then_inc(sem("hy_exp"), 1)

            def copy_xs(t):
                act.wait_ge(sem("hy_back"), t + 1)
                act.activation(xs[:, t, :], flat_pair(CT), ACT.Copy).then_inc(sem("hy_xs"), 1)

            def out_high(t, base, tr, hi):
                act.wait_ge(sem(tr), t + 1)
                act.activation(CH[:, base:base + 8, tok(t)],
                               pair(CT).rearrange("p a (k n) -> p (a k) n", n=P), ACT.Copy).then_inc(sem(hi), 1)

            split_to(u + 2)
            act.wait_ge(sem("hy_dtw"), 16)
            act.activation(dt_hi[:, :, :], dt_w[:, :, :], ACT.Copy).then_inc(sem("hy_dth"), 1)
            act.wait_ge(sem("hy_small"), 32)
            act.activation(NEGA, ALOG, ACT.Exp).then_inc(sem("hy_al"), 1)
            split_to(u + 3)
            evacuate(0)
            split_to(u + 5)
            evacuate(1)
            split_to(u + 6)
            first_tap(0)
            split_to(u + 7)
            evacuate(2)
            split_to(u + 8)
            conv_silu(0)
            first_tap(1)
            split_to(u + 9)
            evacuate(3)
            split_to(u + 10)
            conv_silu(1)
            first_tap(2)
            act.wait_ge(sem("hy_na"), 1)
            act.activation(EX, NA, ACT.Exp).then_inc(sem("hy_ex"), 1)
            split_to(u + 11)
            evacuate(4)
            split_to(u + 12)
            conv_silu(2)
            split_to(u + 13)
            evacuate(5)
            act.wait_ge(sem("hy_dea"), 1)
            act.activation(DTE, DTE, ACT.Exp)
            act.activation(EA, ACS[:, HEADS:2 * HEADS], ACT.Exp).then_inc(sem("hy_dte"), 1)
            split_to(u + 14)
            copy_xs(0)
            split_to(u + 15)
            evacuate(6)
            split_to(u + 16)
            copy_xs(1)
            split_to(u + 17)
            evacuate(7)
            act.wait_ge(sem("hy_bc"), 1)
            act.activation(Btok[:, :], PS[:, C, 0:2 * P], ACT.Copy).then_inc(sem("hy_bt"), 1)
            split_to(u + 19)
            decay(0)
            evacuate(8)
            split_to(u + 20)

            def squares(t):
                act.wait_ge(sem("hy_y"), 2 * t + 2)
                for g in range(2):
                    act.activation(junk[:, t, g * BANK:(g + 1) * BANK], xs[:, t, g * BANK:(g + 1) * BANK], ACT.Square,
                                   accum_out=GQ[:, 2 * t + g:2 * t + g + 1]).then_inc(sem("hy_ysq"), 1)

            out_high(0, 0, "hy_trya", "hy_yahi")
            decay(1)
            out_high(1, 0, "hy_trya", "hy_yahi")
            squares(0)
            split_to(u + 21)
            decay(2)
            decay(3)
            act.wait_ge(sem("hy_st"), 1)
            act.activation(stT[:, :, :], pair(CT), ACT.Copy).then_inc(sem("hy_stv"), 1)
            split_to(u + 22)
            squares(1)
            out_high(0, 8, "hy_try", "hy_yhi")
            split_to(u + 24)
            out_high(1, 8, "hy_try", "hy_yhi")
            split_to(u + 26)

        def hyb_dve(dve, s, done, split_to):
            u = first[s]

            def chain(ins):
                link(dve, "dve_chain", ins)

            def conv_input(j):
                dve.wait_ge(sem("hy_trx"), j + 1)
                dve.tensor_copy(cx[:, 4 * j:4 * j + 4, 3:3 + SEQ], PS[:, CT:CT + 2, :]
                                .rearrange("p a (k n) -> p (a k) n", n=SEQ)).then_inc(sem("hy_cx"), 1)

            def taps(j, which):
                if which[0] == 1:
                    dve.wait_ge(sem("hy_t0"), j + 1)
                    dve.wait_ge(sem("hy_cx"), j + 1)
                    dve.wait_ge(sem("hy_pad"), 1)
                for tap in which:
                    for q in range(4):
                        c = 4 * j + q
                        ins = dve.scalar_tensor_tensor(ca[:, q, :], cx[:, c, tap:tap + SEQ], CW[:, 4 * c + tap:4 * c + tap + 1],
                                                       ca[:, q, :], ALU.mult, ALU.add)
                    if tap < 3:
                        chain(ins)
                    else:
                        ins.then_inc(sem("hy_ca"), 1)

            def segment(t, g):
                n = 2 * t + g
                dve.wait_ge(sem("hy_abc"), n + 1)
                if n == 1:
                    dve.wait_ge(sem("hy_mv"), 2)
                if n >= 2:
                    dve.wait_ge(sem("hy_yd"), n - 1)
                c = t * HEADS + g * GH
                chain(dve.tensor_tensor(Eg[:, g, :, :], flat_pair(CT).rearrange("p (h l) -> p h l", h=GH),
                                        per_head(ACS[:, c:c + GH], GH, P), ALU.subtract))
                dve.tensor_scalar(Eg[:, g, :, :], Eg[:, g, :, :], 0.0, None, ALU.min).then_inc(sem("hy_seg"), 1)

            def weigh(t, g):
                n = 2 * t + g
                dve.wait_ge(sem("hy_exp"), n + 1)
                dve.tensor_tensor(Eg[:, g, :, :], Eg[:, g, :, :],
                                  cbm[:, n, :].unsqueeze(1).broadcast_to([P, GH, P]), ALU.mult)\
                   .then_inc(sem("hy_G"), 1)

            def times_dt(t):
                dve.wait_ge(sem("hy_xs"), t + 1)
                dve.tensor_tensor(heads(xd[:, t, :]), heads(flat_pair(CT)),
                                  per_head(DT[:, t * HEADS:(t + 1) * HEADS], HEADS, 64), ALU.mult)\
                   .then_inc(sem("hy_xd"), 1)

            def skip(t):
                dve.tensor_tensor(heads(xs[:, t, :]), heads(xs[:, t, :]), per_head(DV, HEADS, 64), ALU.mult)

            def normalise(c):
                if c:
                    dve.wait_ge(sem("hy_vn"), 1)
                for r in range(8):
                    ins = dve.bn_stats(BN[:, 6 * r:6 * r + 6], vt[:, c, r * P:(r + 1) * P])
                chain(ins)
                for r in range(8):
                    ins = dve.bn_aggr(MV[:, 2 * r:2 * r + 2], BN[:, 6 * r:6 * r + 6])
                ins.then_inc(sem("hy_mv"), 1)
                dve.wait_ge(sem("hy_mv"), c + 1)
                dve.wait_ge(sem("hy_rv"), c + 1)
                for r in range(8):
                    v = vt[:, c, r * P:(r + 1) * P]
                    ins = dve.tensor_scalar(v, v, MV[:, 2 * r:2 * r + 1], RV[:, r:r + 1], ALU.subtract, ALU.mult)
                ins.then_inc(sem("hy_vn"), 1)

            def gate_v(c):
                dve.wait_ge(sem("hy_mix"), c + 1)
                b = (P1, P2)[c]
                dve.tensor_tensor(heads(vt[:, c, :], 8), heads(flat_pair(b), 8), per_head(BS, 8, P), ALU.add)\
                   .then_inc(sem("hy_mixv"), 1)
                dve.wait_ge(sem("hy_mixv"), c + 1)
                dve.wait_ge(sem("hy_ev"), 9)
                v = vt[:, c, :].rearrange("p (a n) -> p a n", a=2)
                dve.tensor_tensor(v, v, ug[:, :, c, :], ALU.mult).then_inc(sem("hy_ya"), 1)

            def out_low(t, base, hi, lo):
                dve.wait_ge(sem(hi), t + 1)
                dve.tensor_tensor(CL[:, base:base + 8, tok(t)], pair(CT).rearrange("p a (k n) -> p (a k) n", n=P),
                                  CH[:, base:base + 8, tok(t)], ALU.subtract).then_inc(sem(lo), 1)

            def gated(t):
                dve.wait_ge(sem("hy_yd"), 2 * t + 2)
                dve.tensor_tensor(xs[:, t, :], flat_pair(P0), xs[:, t, :], ALU.add).then_inc(sem("hy_y"), 1)
                if t:
                    dve.wait_ge(sem("hy_y"), 3)
                    chain(dve.tensor_tensor(xs[:, t, :], xs[:, t, :], yo[:, :], ALU.add))
                else:
                    dve.wait_ge(sem("hy_y"), 1)
                dve.tensor_tensor(xs[:, t, :], xs[:, t, :], zs[:, t, :], ALU.mult).then_inc(sem("hy_y"), 1)

            split_to(u + 2)
            dve.wait_ge(sem("hy_dth"), 1)
            dve.tensor_tensor(dt_lo[:, :, :], dt_w[:, :, :], dt_hi[:, :, :], ALU.subtract).then_inc(sem("hy_dtl"), 1)
            split_to(u + 6)
            conv_input(0)
            taps(0, (1,))
            split_to(u + 7)
            taps(0, (2, 3))
            split_to(u + 8)
            conv_input(1)
            taps(1, (1,))
            split_to(u + 9)
            taps(1, (2, 3))
            split_to(u + 10)
            conv_input(2)
            dve.wait_ge(sem("hy_dtp"), 1)
            dve.wait_ge(sem("pre_rs"), 2 * s + 2)
            for t in range(2):
                hs = slice(t * HEADS, (t + 1) * HEADS)
                ins = dve.scalar_tensor_tensor(X0[:, hs], PS[:, P1, hs], col(s, t, RS), DTB, ALU.mult, ALU.add)
            ins.then_inc(sem("hy_dtv"), 1)
            dve.wait_ge(sem("hy_dtv"), 1)
            dve.scalar_tensor_tensor(NA, X0, -1.0, X0, ALU.mult, ALU.min).then_inc(sem("hy_na"), 1)
            taps(2, (1,))
            split_to(u + 11)
            dve.wait_ge(sem("hy_ex"), 1)
            chain(dve.tensor_scalar(S1, EX, 2.0, None, ALU.add))
            chain(dve.reciprocal(S1, S1))
            chain(dve.tensor_tensor(S1, S1, EX, ALU.mult))
            chain(dve.tensor_tensor(S2, S1, S1, ALU.mult))
            terms = [2.0 / (2 * i + 1) for i in range(9)]
            chain(dve.tensor_scalar(PO, S2, terms[8], None, ALU.mult))
            for c in terms[7:0:-1]:
                chain(dve.scalar_tensor_tensor(PO, PO, c, S2, ALU.add, ALU.mult))
            chain(dve.scalar_tensor_tensor(PO, PO, terms[0], S1, ALU.add, ALU.mult))
            chain(dve.scalar_tensor_tensor(DT, X0, 0.0, PO, ALU.max, ALU.add))
            dve.wait_ge(sem("hy_al"), 1)
            dve.scalar_tensor_tensor(DA.rearrange("p (t h) -> p t h", t=2), DT.rearrange("p (t h) -> p t h", t=2), -1.0,
                                     NEGA.unsqueeze(1).broadcast_to([P, 2, HEADS]), ALU.mult, ALU.mult)\
               .then_inc(sem("hy_da"), 1)
            split_to(u + 12)
            taps(2, (2, 3))
            split_to(u + 13)
            dve.wait_ge(sem("hy_acs"), 1)
            dve.tensor_copy(ACS, PS[:, C, 0:48]).then_inc(sem("hy_acv"), 1)
            dve.wait_ge(sem("hy_acv"), 1)
            dve.tensor_tensor(DTE, ACS[:, 32:48], ACS[:, 0:HEADS], ALU.subtract).then_inc(sem("hy_dea"), 1)
            split_to(u + 14)
            times_dt(0)
            dve.wait_ge(sem("hy_xd"), 1)
            dve.wait_ge(sem("hy_dte"), 1)
            dve.tensor_tensor(heads(xde[:, :]), heads(xd[:, 0, :]), per_head(DTE, HEADS, 64), ALU.mult)
            skip(0)
            split_to(u + 15)
            split_to(u + 16)
            times_dt(1)
            skip(1)
            dve.wait_ge(sem("hy_ev"), 7)
            normalise(0)
            split_to(u + 17)
            dve.wait_ge(sem("hy_bc"), 1)
            dve.tensor_tensor(cbm[:, :, :], PS[:, T, :].rearrange("p (n l) -> p n l", l=P),
                              tri[:, :].unsqueeze(1).broadcast_to([P, 4, P]), ALU.mult).then_inc(sem("hy_cbm"), 1)
            normalise(1)
            segment(0, 0)
            split_to(u + 18)
            gate_v(0)
            segment(0, 1)
            weigh(0, 0)
            out_low(0, 0, "hy_yahi", "hy_yalo")
            gate_v(1)
            weigh(0, 1)
            split_to(u + 19)
            out_low(1, 0, "hy_yahi", "hy_yalo")
            gated(0)
            split_to(u + 20)
            segment(1, 0)
            split_to(u + 21)
            weigh(1, 0)
            segment(1, 1)
            weigh(1, 1)

            def normalise_y(t):
                if t == 0:
                    dve.wait_ge(sem("hy_ng"), 16)
                dve.wait_ge(sem("hy_yrs"), t + 1)
                for g in range(2):
                    y = xs[:, t, g * BANK:(g + 1) * BANK]
                    ins = dve.scalar_tensor_tensor(y, y, GQ[:, 4 + 2 * t + g:5 + 2 * t + g], ng[:, g * BANK:(g + 1) * BANK],
                                                   ALU.mult, ALU.mult)
                ins.then_inc(sem("hy_yn"), 1)

            normalise_y(0)
            dve.wait_ge(sem("hy_yo"), 1)
            dve.tensor_tensor(heads(yo[:, :]), heads(flat_pair(CT)), per_head(EA, HEADS, 64), ALU.mult)\
               .then_inc(sem("hy_yoff"), 1)
            dve.wait_ge(sem("hy_yoff"), 1)
            gated(1)
            split_to(u + 22)
            out_low(0, 8, "hy_yhi", "hy_ylo")
            normalise_y(1)
            split_to(u + 23)
            split_to(u + 24)
            out_low(1, 8, "hy_yhi", "hy_ylo")
            split_to(u + 26)

        def hyb_early(pool):
            pool.dma_start(dt_w[:, :, :], a["dt_w"]).then_inc(sem("hy_dtw"), 16)
            pool.dma_start(sm[:, 0:68], a["hy_cols"]).then_inc(sem("hy_small"), 16)
            pool.dma_start(sm[:, 68:116], a["hy_rows"].partition_broadcast(P)).then_inc(sem("hy_small"), 16)
            pool.dma_start(wsT[:, :, :], a["gm_w"]).then_inc(sem("hy_ws"), 16)
            pool.wait_ge(sem("hy_ws"), 16)
            pool.tensor_tensor(wsT[:, :, :], wsT[:, :, :], tri[:, :].unsqueeze(1).broadcast_to([P, 8, P]), ALU.mult)\
                .then_inc(sem("hy_wsm"), 1)

        def hyb_pool(pool, s):
            if s == 0:
                hyb_early(pool)
            pool.memset(cx[:, :, 0:3], 0.0).then_inc(sem("hy_pad"), 1)
            pool.dma_start(gm_g[:, :], a["gm_g"].partition_broadcast(P)).then_inc(sem("hy_gm"), 16)
            pool.dma_start(gm_b[:, :], a["gm_b"].partition_broadcast(P)).then_inc(sem("hy_gm"), 16)
            for c in range(2):
                pool.wait_ge(sem("hy_mv"), c + 1)
                if c:
                    pool.wait_ge(sem("hy_vn"), 1)
                link(pool, "pool_chain", pool.tensor_scalar(RV, MV.rearrange("p (h q) -> p h q", q=2)[:, :, 1], LN_EPS, None,
                                                            ALU.add))
                pool.tensor_tensor(RV, RV, nhalf[:, :], ALU.pow).then_inc(sem("hy_rv"), 1)
                if c == 0:
                    pool.wait_ge(sem("hy_gm"), 32)
                pool.wait_ge(sem("hy_vn"), c + 1)
                link(pool, "pool_chain", pool.tensor_tensor(vt[:, c, :], vt[:, c, :], gm_g[:, :], ALU.mult))
                pool.tensor_tensor(vt[:, c, :], vt[:, c, :], gm_b[:, :], ALU.add).then_inc(sem("hy_v"), 1)
            pool.wait_ge(sem("w_used"), first[s] + 18)
            pool.dma_start(ng[:, :], a["ssd_g"].partition_broadcast(P)).then_inc(sem("hy_ng"), 16)
            for t in range(2):
                pool.wait_ge(sem("hy_ysq"), 2 * t + 2)
                ms, rs = GQ[:, 2 * t:2 * t + 2], GQ[:, 4 + 2 * t:6 + 2 * t]
                link(pool, "pool_chain", pool.tensor_scalar(rs, ms, 1.0 / 512, EPS, ALU.mult, ALU.add))
                pool.tensor_tensor(rs, rs, nhalf[:, 0:2], ALU.pow).then_inc(sem("hy_yrs"), 1)


        HALF = ROPE // 2
        kT = place("kT", [P, HEADS, SEQ], offset=x_at)
        o = s_at
        qT = place("qT", [P, HEADS, SEQ], offset=o); o += 16384
        vv = place("vv", [P, 2, HEADS * VD], offset=o); o += 16384
        qrT = place("qrT", [P, 8, SEQ], offset=o); o += 8192
        krT = place("krT", [P, SEQ], offset=o); o += 1024
        pr = place("pr", [P, 2, 3 * P], offset=o); o += 3072
        pT = place("pT", [P, 2, 3 * P], offset=o); o += 3072
        msm = place("msm", [P, 256], offset=o); o += 1024
        assert o <= end, o
        qr = hn
        cn = place("cn", [P, 2, BANK], offset=c_at)
        cTH = place("cTH", [P, 3, SEQ], f32r, offset=c_at + 4096)
        cTL = place("cTL", [P, 3, SEQ], f32r, offset=c_at + 4096 + 3072)
        cg = place("cg", [P, Q_LORA + KV_LORA], offset=c_at + 10240)
        ra = place("ra", [P, HEADS, HALF], offset=c_at + 12288)
        rb = place("rb", [P, HEADS, HALF], offset=c_at + 14336)
        rc = place("rc", [P, HEADS, HALF], offset=c_at + 16384)
        rd = place("rd", [P, HEADS, HALF], offset=c_at + 18432)

        LSQ, LRS = msm[:, 0:4], msm[:, 4:8]
        NMX, SUM = msm[:, 8:72], msm[:, 72:136]
        MAXS = msm[:, 136:200]

        for name in ("ml_in", "ml_cg", "ml_sq", "ml_rs", "ml_cn", "ml_tr", "ml_chi", "ml_clo", "ml_krT", "ml_pa",
                     "ml_pv", "ml_S", "ml_mx", "ml_nm", "ml_exp", "ml_P", "ml_PT", "ml_PTe", "ml_O", "ml_Ohi", "ml_Olo",
                     "ml_qr", "ml_qrt", "rope_pos", "rope_arg", "rope_sin", "rope_done", "ml_X", "ml_XA", "ml_XD"):
            sem(name)

        def group_bank(n):
            return 4 * (n % 2)

        def group_free(pe, n):
            if n == 4:
                pe.wait_ge(sem("ml_qr"), 2)
            elif n >= 2:
                v = n - 1 if n < 4 else n - 2
                pe.wait_ge(sem("ml_XA"), v)
                pe.wait_ge(sem("ml_XD"), v)

        def mla_pe(pe, s):
            u = first[s]
            for j, t in lagged(range(2)):
                if (j, t) == (0, 1):
                    transpose_x(pe, s, 1)
                pe.wait_ge(sem("w_lo"), u + j + 1)
                wh = whole(WH, u + j).rearrange("p (k n) -> p k n", k=4)
                wl = whole(WL, u + j).rearrange("p (k n) -> p k n", k=4)
                x_there(pe, s, t, j)
                for q in range(4):
                    kt = 4 * j + q
                    ins = product(pe, PS[:, t, 0:448], XH[:, kt, tok(t)], XL[:, kt, tok(t)],
                                  wh[:, q, 0:448], wl[:, q, 0:448], kt == 0, kt == KT - 1)
                if t == 1:
                    ins.then_inc(sem("w_used"), 1)
                elif j == 1:
                    ins.then_inc(sem("ml_in"), 1)
            for t in range(2):
                pe.wait_ge(sem("ml_cn"), t + 1)
                for q in range(4):
                    ins = pe.transpose(PS[:, C + t, q * P:(q + 1) * P], cn[:, t, q * P:(q + 1) * P], ident[:, :])
                ins.then_inc(sem("ml_tr"), 1)

            def turned(n, b, h, unit, kts, wcol, base):
                wh = whole(WH, unit).rearrange("p (k n) -> p k n", k=kts)
                wl = whole(WL, unit).rearrange("p (k n) -> p k n", k=kts)
                out_ap = PS[:, b, (h % 2) * SEQ:(h % 2 + 1) * SEQ]
                for q in range(kts):
                    a_h, a_l = cTH[:, base + q, :], cTL[:, base + q, :]
                    w = slice(wcol * P, (wcol + 1) * P)
                    ins = product(pe, out_ap, wh[:, q, w], wl[:, q, w], a_h, a_l, q == 0, q == kts - 1)
                return ins

            pe.wait_ge(sem("ml_clo"), 2)
            pe.wait_ge(sem("ml_krT"), 2)
            pe.wait_ge(sem("w_lo"), u + 3)
            for g in range(2):
                group_free(pe, g)
                for r in range(8):
                    ins = turned(g, group_bank(g) + r // 2, r, u + 2, 1, 8 * g + r, 2)
                ins.then_inc(sem("ml_X" if g == 0 else "w_used"), 1)
            pe.wait_ge(sem("w_lo"), u + 4)
            group_free(pe, 2)
            wh = whole(WH, u + 3).rearrange("p (k n) -> p k n", k=2)
            wl = whole(WL, u + 3).rearrange("p (k n) -> p k n", k=2)
            for t in range(2):
                for c in range(2):
                    for q in range(2):
                        ins = product(pe, PS[:, 2 * t + c, :], cTH[:, q, tok(t)], cTL[:, q, tok(t)],
                                      wh[:, q, c * BANK:(c + 1) * BANK], wl[:, q, c * BANK:(c + 1) * BANK],
                                      q == 0, q == 1)
            ins.then_inc(sem("w_used"), 1)
            for g in range(2):
                pe.wait_ge(sem("w_lo"), u + 5 + g)
                group_free(pe, 3 + g)
                for r in range(8):
                    ins = turned(3 + g, group_bank(3 + g) + r // 2, r, u + 4 + g, 2, r, 0)
                ins.then_inc(sem("w_used"), 1)
            pe.wait_ge(sem("w_lo"), u + 7)
            for t in range(2):
                group_free(pe, 5 + t)
                for c in range(4):
                    ins = product(pe, PS[:, group_bank(5 + t) + c, :], cTH[:, 2, tok(t)], cTL[:, 2, tok(t)],
                                  whole(WH, u + 6)[:, c * BANK:(c + 1) * BANK], whole(WL, u + 6)[:, c * BANK:(c + 1) * BANK],
                                  True, True)
                ins.then_inc(sem("w_used" if t else "ml_X"), 1)
            group_free(pe, 7)
            pe.wait_ge(sem("ml_qr"), 2)
            for r in range(8):
                for t in range(2):
                    ins = pe.transpose(PS[:, 4 + r // 2, (r % 2) * SEQ + t * P:(r % 2) * SEQ + (t + 1) * P],
                                       qr[:, t, r * P:(r + 1) * P], ident[:, :])
            ins.then_inc(sem("ml_qrt"), 1)

            def scores(hd):
                if hd >= 2:
                    pe.wait_ge(sem("ml_mx"), hd - 1)
                lo = (hd % 2) * 64
                for t in range(2):
                    n = (t + 1) * P
                    dst = PS[:, hd % 2, t * P:t * P + n]
                    pe.matmul(dst, qT[:, hd, tok(t)], kT[:, hd, 0:n], start=True, stop=False)
                    ins = pe.matmul(dst, qrT[lo:lo + 64, hd // 2, tok(t)], krT[lo:lo + 64, 0:n], start=False, stop=True)
                ins.then_inc(sem("ml_S"), 1)

            def transpose_probabilities(hd):
                pe.wait_ge(sem("ml_P"), hd + 1)
                if hd:
                    pe.wait_ge(sem("ml_PTe"), hd)
                for q in range(3):
                    ins = pe.transpose(PS[:, C, q * P:(q + 1) * P], pr[:, hd % 2, q * P:(q + 1) * P], ident[:, :])
                ins.then_inc(sem("ml_PT"), 1)

            def weighted_values(hd):
                pe.wait_ge(sem("ml_PTe"), hd + 1)
                if hd % 2 == 0 and hd:
                    pe.wait_ge(sem("ml_Olo"), hd // 2)
                lo = (hd % 2) * SEQ
                w = slice(hd * VD, (hd + 1) * VD)
                pe.matmul(PS[:, T, lo:lo + SEQ], vv[:, 0, w], pT[:, hd % 2, 0:SEQ], start=True, stop=False)
                ins = pe.matmul(PS[:, T, lo + P:lo + SEQ], vv[:, 1, w], pT[:, hd % 2, SEQ:3 * P], start=False, stop=True)
                ins.then_inc(sem("ml_O"), 1)

            def out_unit(j, t):
                pe.wait_ge(sem("ml_Olo"), j + 1)
                wide(pe, u + 7 + j, t, 4 + 2 * t, CH, CL, 2 * j, j == 0, j == 7, "out_done" if j == 7 else None)

            pe.wait_ge(sem("ml_XA"), 7)
            pe.wait_ge(sem("ml_XD"), 7)
            scores(0)
            scores(1)
            for j in range(8):
                transpose_probabilities(2 * j)
                if j < 7:
                    scores(2 * j + 2)
                transpose_probabilities(2 * j + 1)
                if j < 7:
                    scores(2 * j + 3)
                weighted_values(2 * j)
                weighted_values(2 * j + 1)
                if 0 < j < 7:
                    for t in range(2):
                        out_unit(j - 1, t)
            for j, t in lagged((6, 7)):
                out_unit(j, t)

        def group_ready(eng, s, n):
            u = first[s]
            if n == 0:
                eng.wait_ge(sem("ml_X"), 1)
            elif n == 5:
                eng.wait_ge(sem("ml_X"), 2)
            elif n == 7:
                eng.wait_ge(sem("ml_qrt"), 1)
            else:
                eng.wait_ge(sem("w_used"), u + {1: 3, 2: 4, 3: 5, 4: 6, 6: 7}[n])

        def group_part(n, part):
            b = group_bank(n) + 2 * part
            src = PS[:, b:b + 2, :]
            def four(tile, h0):
                return tile[:, h0 + 4 * part:h0 + 4 * part + 4, :].rearrange("p (a h) n -> p a (h n)", a=2)
            if n in (0, 1):
                return four(kT, 8 * n), src
            if n in (3, 4):
                return four(qT, 8 * (n - 3)), src
            if n == 7:
                return four(qrT, 0), src
            return vv[:, n - 5, part * 1024:(part + 1) * 1024].rearrange("p (a n) -> p a n", a=2), src

        def mla_act(act, s, done, split_to):
            u = first[s]
            split_to(u + 2)
            for t in range(2):
                if t == 0:
                    act.wait_ge(sem("ml_in"), 1)
                else:
                    act.wait_ge(sem("w_used"), u + 2)
                act.wait_ge(sem("pre_rs"), 2 * s + t + 1)
                act.activation(junk[:, t, 0:Q_LORA], PS[:, t, 0:Q_LORA], ACT.Square, scale=col(s, t, RS),
                               accum_out=LSQ[:, t:t + 1])
                act.activation(junk[:, t, Q_LORA:Q_LORA + KV_LORA], PS[:, t, Q_LORA:Q_LORA + KV_LORA], ACT.Square,
                               scale=col(s, t, RS), accum_out=LSQ[:, 2 + t:3 + t]).then_inc(sem("ml_sq"), 1)
            split_to(u + 3)
            split_to(u + 4)
            for t in range(2):
                act.wait_ge(sem("ml_tr"), t + 1)
                act.activation(cTH[:, :, tok(t)], PS[:, C + t, 0:384].rearrange("p (k n) -> p k n", n=P), ACT.Copy)\
                   .then_inc(sem("ml_chi"), 1)

            def empty(n):
                group_ready(act, s, n)
                dst, src = group_part(n, 0)
                act.activation(dst, src, ACT.Copy).then_inc(sem("ml_XA"), 1)

            empty(0)
            empty(1)
            split_to(u + 5)
            split_to(u + 6)
            empty(3)
            split_to(u + 7)
            empty(4)
            empty(5)
            split_to(u + 8)
            empty(6)
            empty(7)
            split_to(u + 9)

            def exponentials(hd):
                act.wait_ge(sem("ml_nm"), hd + 1)
                for t in range(2):
                    p = pr[:, hd % 2, t * P:t * P + (t + 1) * P]
                    c = 2 * hd + t
                    ins = act.activation(p, p, ACT.Exp, bias=NMX[:, c:c + 1], scale=SCALE, accum_out=SUM[:, c:c + 1])
                ins.then_inc(sem("ml_exp"), 1)

            def copy_pT(hd):
                act.wait_ge(sem("ml_PT"), hd + 1)
                if hd >= 2:
                    act.wait_ge(sem("ml_O"), hd - 1)
                act.activation(pT[:, hd % 2, :], PS[:, C, 0:3 * P], ACT.Copy).then_inc(sem("ml_PTe"), 1)

            exponentials(0)
            exponentials(1)
            for j in range(8):
                copy_pT(2 * j)
                if j < 7:
                    exponentials(2 * j + 2)
                copy_pT(2 * j + 1)
                if j < 7:
                    exponentials(2 * j + 3)
                act.wait_ge(sem("ml_O"), 2 * j + 2)
                act.activation(CH[:, 2 * j:2 * j + 2, :], PS[:, T, :].rearrange("p (k n) -> p k n", n=SEQ), ACT.Copy)\
                   .then_inc(sem("ml_Ohi"), 1)
                if j:
                    split_to(min(u + 9 + j, u + 15))
            split_to(u + 15)

        def mla_dve(dve, s, done, split_to):
            u = first[s]

            def rotate(x, y, t, n, tmp):
                c = cosT[:, t, :].unsqueeze(1).broadcast_to([P, n, HALF])
                sn = sinT[:, t, :].unsqueeze(1).broadcast_to([P, n, HALF])
                w, x_, y_, z_ = (m[:, 0:n, :] for m in tmp)
                dve.tensor_tensor(w, x[:, :, 0, :], c, ALU.mult)
                dve.tensor_tensor(x_, x[:, :, 1, :], sn, ALU.mult)
                dve.tensor_tensor(y_, x[:, :, 1, :], c, ALU.mult)
                link(dve, "dve_chain", dve.tensor_tensor(z_, x[:, :, 0, :], sn, ALU.mult))
                dve.tensor_tensor(y[:, :, 0, :], w, x_, ALU.subtract)
                return dve.tensor_tensor(y[:, :, 1, :], y_, z_, ALU.add)

            tmp = (ra, rb, rc, rd)
            split_to(u + 2)
            dve.wait_ge(sem("ml_cg"), 32)
            for t in range(2):
                dve.wait_ge(sem("ml_rs"), 1)
                q, kv = slice(0, Q_LORA), slice(Q_LORA, Q_LORA + KV_LORA)
                dve.scalar_tensor_tensor(cn[:, t, q], PS[:, t, q], LRS[:, t:t + 1], cg[:, q], ALU.mult, ALU.mult)
                dve.scalar_tensor_tensor(cn[:, t, kv], PS[:, t, kv], LRS[:, 2 + t:3 + t], cg[:, kv], ALU.mult, ALU.mult)
                kr = ra[:, 2 + 2 * t:4 + 2 * t, :]
                link(dve, "dve_chain", rotate(PS[:, t, 384:448].rearrange("p (n a h) -> p n a h", n=1, a=2),
                                              kr.unsqueeze(1), t, 1, tmp))
                for twice in range(2):
                    lo = 384 + 64 * twice
                    ins = dve.tensor_scalar(cn[:, t, lo:lo + 64], kr.rearrange("p a h -> p (a h)"), col(s, t, RS), None,
                                            ALU.mult)
                ins.then_inc(sem("ml_cn"), 1)
            split_to(u + 4)
            for t in range(2):
                dve.wait_ge(sem("ml_chi"), t + 1)
                dve.tensor_tensor(cTL[:, :, tok(t)], PS[:, C + t, 0:384].rearrange("p (k n) -> p k n", n=P),
                                  cTH[:, :, tok(t)], ALU.subtract).then_inc(sem("ml_clo"), 1)
                dve.tensor_copy(krT[:, tok(t)], PS[:, C + t, 384:512]).then_inc(sem("ml_krT"), 1)

            def empty(n):
                group_ready(dve, s, n)
                dst, src = group_part(n, 1)
                dve.tensor_copy(dst, src).then_inc(sem("ml_XD"), 1)

            empty(0)
            empty(1)
            split_to(u + 5)
            split_to(u + 6)
            group_ready(dve, s, 2)
            for t in range(2):
                rotate(PS[:, 2 * t:2 * t + 2, :].rearrange("p b (n a h) -> p (b n) a h", a=2, h=HALF),
                       qr[:, t, :].rearrange("p (n a h) -> p n a h", a=2, h=HALF), t, HEADS, tmp)\
                    .then_inc(sem("ml_qr"), 1)
                dve.wait_ge(sem("ml_qr"), t + 1)
            empty(3)
            split_to(u + 7)
            empty(4)
            empty(5)
            split_to(u + 8)
            empty(6)
            empty(7)
            split_to(u + 9)

            def maxima(hd):
                dve.wait_ge(sem("ml_S"), hd + 1)
                if hd >= 2:
                    dve.wait_ge(sem("ml_PT"), hd - 1)
                for t in range(2):
                    c = 2 * hd + t
                    n = (t + 1) * P
                    ins = dve.tensor_tensor_reduce(out=pr[:, hd % 2, t * P:t * P + n], in0=PS[:, hd % 2, t * P:t * P + n],
                                                   in1=cmask[:, 2 * P - n:2 * P], scale=1.0, scalar=-3.0e38, op0=ALU.add,
                                                   op1=ALU.max, accum_out=MAXS[:, c:c + 1])
                ins.then_inc(sem("ml_mx"), 1)
                dve.wait_ge(sem("ml_mx"), hd + 1)
                dve.tensor_scalar(NMX[:, 2 * hd:2 * hd + 2], MAXS[:, 2 * hd:2 * hd + 2], -SCALE, None, ALU.mult)\
                   .then_inc(sem("ml_nm"), 1)

            def normalise(hd):
                dve.wait_ge(sem("ml_exp"), hd + 1)
                r = SUM[:, 2 * hd:2 * hd + 2]
                link(dve, "dve_chain", dve.reciprocal(r, r))
                for t in range(2):
                    p = pr[:, hd % 2, t * P:t * P + (t + 1) * P]
                    c = 2 * hd + t
                    ins = dve.tensor_scalar(p, p, SUM[:, c:c + 1], None, ALU.mult)
                ins.then_inc(sem("ml_P"), 1)

            maxima(0)
            maxima(1)
            normalise(0)
            normalise(1)
            for j in range(8):
                if j < 7:
                    maxima(2 * j + 2)
                    maxima(2 * j + 3)
                    normalise(2 * j + 2)
                    normalise(2 * j + 3)
                dve.wait_ge(sem("ml_Ohi"), j + 1)
                dve.tensor_tensor(CL[:, 2 * j:2 * j + 2, :], PS[:, T, :].rearrange("p (k n) -> p k n", n=SEQ),
                                  CH[:, 2 * j:2 * j + 2, :], ALU.subtract).then_inc(sem("ml_Olo"), 1)
                if j:
                    split_to(min(u + 9 + j, u + 15))
            split_to(u + 15)

        def mla_early(pool):
            pool.dma_start(cg[:, 0:Q_LORA], a["q_g"].partition_broadcast(P)).then_inc(sem("ml_cg"), 16)
            pool.dma_start(cg[:, Q_LORA:Q_LORA + KV_LORA], a["kv_g"].partition_broadcast(P)).then_inc(sem("ml_cg"), 16)

        def mla_pool(pool, s):
            if s == 0:
                mla_early(pool)
            pool.wait_ge(sem("ml_sq"), 2)
            pool.tensor_scalar(LRS[:, 0:2], LSQ[:, 0:2], 1.0 / Q_LORA, EPS, ALU.mult, ALU.add)
            link(pool, "pool_chain", pool.tensor_scalar(LRS[:, 2:4], LSQ[:, 2:4], 1.0 / KV_LORA, EPS, ALU.mult, ALU.add))
            link(pool, "pool_chain", pool.tensor_tensor(LRS, LRS, nhalf[:, 0:4], ALU.pow))
            for g in range(2):
                for t in range(2):
                    c = 2 * g + t
                    ins = pool.tensor_scalar(LRS[:, c:c + 1], LRS[:, c:c + 1], col(s, t, RS), None, ALU.mult)
            ins.then_inc(sem("ml_rs"), 1)

        r_at = s_at + 16384
        rp = place("rp", [P, 2], i32, offset=r_at)
        rf = place("rf", [P, 2], offset=r_at + 32)
        inv = place("inv", [P, HALF], offset=r_at + 64)
        ang = place("ang", [P, 2, HALF], offset=r_at + 256)
        turns = place("turns", [P, 2, HALF], offset=r_at + 512)
        sh = place("sh", [P, 2, HALF], offset=r_at + 768)
        parts, rest = [], 2 * np.pi
        for bits in (8, 8, 8):
            unit = 2.0 ** (np.floor(np.log2(rest)) - bits + 1)
            parts.append(float(np.floor(rest / unit) * unit))
            rest -= parts[-1]
        parts.append(float(rest))
        MAGIC = 1.5 * 2.0 ** 23
        LIMIT = 3.1415925

        def prelude_pool(pool):
            if not has_mla:
                return
            pool.dma_start(rp[:, :], a["positions"]).then_inc(sem("rope_pos"), 16)
            pool.dma_start(inv[:, :], a["inv"].partition_broadcast(P)).then_inc(sem("rope_pos"), 16)

        def prelude_act(act):
            if not has_mla:
                return
            act.wait_ge(sem("rope_arg"), 1)
            act.activation(sinT[:, :, :], ang[:, :, :], ACT.Sin)
            act.activation(sh[:, :, :], ang[:, :, :], ACT.Sin, scale=0.5).then_inc(sem("rope_sin"), 1)

        def prelude_dve(dve):
            if not has_mla:
                return

            def chain(ins):
                link(dve, "dve_chain", ins)

            dve.wait_ge(sem("rope_pos"), 32)
            chain(dve.tensor_copy(rf[:, :], rp[:, :]))
            for t in range(2):
                ins = dve.tensor_scalar(ang[:, t, :], inv[:, :], rf[:, t:t + 1], None, ALU.mult)
            chain(ins)
            chain(dve.tensor_scalar(turns[:, :, :], ang[:, :, :], float(1 / (2 * np.pi)), MAGIC, ALU.mult, ALU.add))
            chain(dve.tensor_scalar(turns[:, :, :], turns[:, :, :], MAGIC, None, ALU.subtract))
            for part in parts:
                chain(dve.scalar_tensor_tensor(ang[:, :, :], turns[:, :, :], -part, ang[:, :, :], ALU.mult, ALU.add))
            dve.tensor_scalar(ang[:, :, :], ang[:, :, :], LIMIT, -LIMIT, ALU.min, ALU.max).then_inc(sem("rope_arg"), 1)

        def prelude_dve_end(dve):
            if not has_mla:
                return
            dve.wait_ge(sem("rope_sin"), 1)
            link(dve, "dve_chain", dve.tensor_tensor(sh[:, :, :], sh[:, :, :], sh[:, :, :], ALU.mult))
            dve.tensor_scalar(cosT[:, :, :], sh[:, :, :], -2.0, 1.0, ALU.mult, ALU.add).then_inc(sem("rope_done"), 1)

        has_mla = any(kind == "mla" for kind, _ in stages)
        PES = {"ffn": ffn_pe, "ple": ple_pe, "hyb": hyb_pe, "mla": mla_pe}
        ACTS = {"ffn": ffn_act, "ple": ple_act, "hyb": hyb_act, "mla": mla_act}
        DVES = {"ffn": ffn_dve, "ple": ple_dve, "hyb": hyb_dve, "mla": mla_dve}
        POOL = {"ffn": ffn_pool, "ple": lambda pool, s: None, "hyb": hyb_pool, "mla": mla_pool}

        block = ctx.enter_context(nc.Block())

        @block.sync
        def _(sp):
            for t in range(2):
                sp.dma_start(h[:, t, :], a["x"][tok(t), :]).then_inc(sem(f"x_loaded{t}"), 16)
                load_unit(sp, t)
            for n in range(2, 2 * RING):
                load_unit(sp, n)
            rounds = (n_units - 2 * RING) // RING
            with sp.Fori(0, rounds) as k:
                for j in range(RING):
                    load_unit(sp, 2 * RING + j, k, RING)
            for n in range((2 + rounds) * RING, n_units):
                load_unit(sp, n)
            for t in range(2):
                for b in range(2):
                    h_ready(sp, NS, t, b)
                    sp.dma_start(out[tok(t), half(b)], h[:, t, half(b)]).then_inc(sem("stored"), 16)
            sp.wait_ge(sem("stored"), 64)

        @block.gpsimd
        def _(pool):
            pool.dma_start(QG[:, :], a["pre_g"][0, :].partition_broadcast(P)).then_inc(sem("qg"), 16)
            pool.memset(ident[:, :], 0.0)
            pool.memset(tri[:, :], 1.0)
            pool.memset(cmask[:, :], 0.0)
            pool.memset(zeros[:, :], 0.0)
            link(pool, "pool_chain", pool.memset(nhalf[:, :], -0.5))
            pool.affine_select(out=ident[:, :], in_=ident[:, :], compare_op=ALU.not_equal, fill=1.0, base=0,
                               pattern=[[-1, P]], channel_multiplier=1)
            pool.affine_select(out=tri[:, :], in_=tri[:, :], compare_op=ALU.is_ge, fill=0.0, base=0,
                               pattern=[[1, P]], channel_multiplier=-1)
            pool.affine_select(out=cmask[:, P:2 * P], in_=cmask[:, P:2 * P], compare_op=ALU.is_ge, fill=NEG,
                               base=0, pattern=[[-1, P]], channel_multiplier=1).then_inc(sem("consts"), 1)
            prelude_pool(pool)
            for s, (kind, _) in enumerate(stages):
                boundary_pool(pool, s)
                POOL[kind](pool, s)
            boundary_pool(pool, NS)

        @block.scalar
        def _(act):
            done, split_to = splitter(act, split_hi)
            split_to(0)
            for s, (kind, _) in enumerate(stages):
                boundary_act(act, s, split_to)
                ACTS[kind](act, s, done, split_to)
            boundary_act(act, NS, split_to)

        @block.vector
        def _(dve):
            done, split_to = splitter(dve, split_lo)
            split_to(0)
            for s, (kind, _) in enumerate(stages):
                boundary_dve(dve, s, done, split_to)
                DVES[kind](dve, s, done, split_to)
            boundary_dve(dve, NS, done, split_to)

        @block.tensor
        def _(pe):
            pe.wait_ge(sem("consts"), 1)
            for s, (kind, _) in enumerate(stages):
                transpose_x(pe, s, 0)
                PES[kind](pe, s)


def units_of(w, kts, cols):
    K, N = w.shape
    v = w.reshape(K // (kts * P), kts, P, N // cols, cols)
    return v.transpose(3, 0, 2, 1, 4).reshape(-1, P, kts * cols)


def ffn_units(w_in, w_down):
    gate, up = w_in[:, :D_FF], w_in[:, D_FF:]
    whole = FULL * CHUNK
    out, down = [], units_of(w_down, 2, D)
    for c in range(FULL):
        for w in (gate, up):
            out.append(units_of(w[:, c * CHUNK:(c + 1) * CHUNK], 4, CHUNK))
        if c:
            out.append(down[2 * (c - 1):2 * c])
    for w in (gate, up):
        out.append(units_of(w[:, whole:], 8, CHUNK // 2))
    out += [down[2 * (FULL - 1):2 * FULL], down[2 * FULL:]]
    return out


def hybrid_units(w_in, w_out):
    u, v = w_in[:, :GM_W], w_in[:, GM_W:2 * GM_W]
    z = w_in[:, 2 * GM_W:2 * GM_W + SSD_IN]
    xbc = w_in[:, 2 * GM_W + SSD_IN:2 * GM_W + SSD_IN + CONV_CH]
    return [units_of(c, 4, CHUNK) for c in (xbc, z, v, u)] + [units_of(w_out, 2, D)]


def mla_units(w_in, w_uq, w_ukv, w_out):
    pad = np.zeros((D, BANK - w_in.shape[1]), w_in.dtype)
    q = w_uq.reshape(Q_LORA, HEADS, NOPE + ROPE)
    kv = w_ukv.reshape(KV_LORA, HEADS, NOPE + VD)
    return [units_of(np.concatenate([w_in, pad], axis=1), 4, BANK),
            units_of(kv[:, :, :NOPE].reshape(KV_LORA, HEADS * NOPE), 1, UNIT),
            units_of(q[:, :, NOPE:].reshape(Q_LORA, HEADS * ROPE), 2, D),
            units_of(q[:, :, :NOPE].reshape(Q_LORA, HEADS * NOPE), 2, D),
            units_of(kv[:, :, NOPE:].reshape(KV_LORA, HEADS * VD), 1, UNIT),
            units_of(w_out, 2, D)]


def mixer_arrays(w):
    dt_w = w["hyb_w_in"][0][:, 2 * GM_W + SSD_IN + CONV_CH:]
    conv_w = w["ssd_conv_w"][0].T.reshape(CONV_CH // P, P, 4).transpose(1, 0, 2).reshape(P, -1)
    conv_b = w["ssd_conv_b"][0].reshape(CONV_CH // P, P).T
    inv = np.float32(1.0) / np.float32(ROPE_BASE) ** (np.arange(0, ROPE, 2, dtype=np.float32) / np.float32(ROPE))
    return {
        "dt_w": dt_w.reshape(KT, P, HEADS).transpose(1, 0, 2),
        "hy_cols": np.concatenate([conv_w, conv_b, w["gm_b_s"][0].T], axis=1),
        "hy_rows": np.concatenate([w["ssd_d"][0], w["ssd_dt_bias"][0], w["ssd_a_log"][0]]),
        "gm_w": w["gm_w_s"][0].transpose(2, 0, 1),
        "gm_g": w["gm_ln_g"][0],
        "gm_b": w["gm_ln_b"][0],
        "ssd_g": w["ssd_norm_g"][0],
        "q_g": w["mla_q_norm_g"][0],
        "kv_g": w["mla_kv_norm_g"][0],
        "positions": w["positions"][0].reshape(2, P).T,
        "inv": inv,
    }


def stream_of(stages, w):
    out = []
    for kind, i in stages:
        if kind == "ffn":
            name = "ffn1" if i % 2 == 0 else "ffn2"
            out += ffn_units(w[name + "_w_in"][i // 2], w[name + "_w_down"][i // 2])
        elif kind == "ple":
            out.append(units_of(w["ple_w_proj"][i], 2, D))
            out.append(units_of(w["ple_w_gate"][i], 2, D))
        elif kind == "hyb":
            out += hybrid_units(w["hyb_w_in"][0], w["hyb_w_out"][0])
        else:
            out += mla_units(w["mla_w_in"][0], w["mla_w_uq"][0], w["mla_w_ukv"][0], w["mla_w_out"][0])
    return np.concatenate(out, axis=0)


def gains_of(stages, w, side):
    out = []
    for n, (kind, i) in enumerate(stages):
        name = {"ffn": "ffn1" if i % 2 == 0 else "ffn2", "ple": "ple", "hyb": "mix", "mla": "mix"}[kind]
        layer = i // 2 if kind == "ffn" else 1 if kind == "mla" else i
        out.append(w[f"{name}_{side}_g"][layer])
    return np.stack(out)


def kernel(**inputs):
    import concourse.bacc as _bacc
    from concourse.bass_utils import run_bass_kernel_spmd as _run

    w = {n: np.asarray(v) for n, v in inputs.items()}
    arrays = {
        "x": w["x"][0],
        "stream": stream_of(STAGES, w),
        "pre_g": gains_of(STAGES, w, "pre"),
        "post_g": gains_of(STAGES, w, "post"),
        "p_t": w["p"][:, 0].transpose(0, 2, 1),
    }
    arrays.update(mixer_arrays(w))
    arrays = {n: np.ascontiguousarray(v) for n, v in arrays.items()}
    nc = _bacc.Bacc("TRN2", target_bir_lowering=False, num_devices=1)
    aps = {n: nc.dram_tensor(n, v.shape, mybir.dt.from_np(v.dtype), kind="ExternalInput").ap()
           for n, v in arrays.items()}
    out = nc.dram_tensor("out", (SEQ, D), mybir.dt.float32, kind="ExternalOutput").ap()
    hybrid_trunk(nc, STAGES, aps, out)
    r = _run(nc, [arrays], core_ids=[0])
    return r.results[0]["out"].reshape(1, SEQ, D)
```

```python
from contextlib import ExitStack

import numpy as np

import concourse.bass as bass
from concourse import mybir

D = 1024
SEQ = 256
P = 128
D_FF = 2816
PLE = 256
BANK = 512
UNIT = 2048
RING = 3
KT = D // P
EPS = 1e-6
LN_EPS = 1e-5
CHUNK = 512
FULL = D_FF // CHUNK
FFN_UNITS = 33
GM_W = 1024
SSD_IN = 1024
CONV_CH = 1536
HEADS = 16
NOPE, ROPE, VD = 128, 64, 128
Q_LORA, KV_LORA = 256, 128
SCALE = float((NOPE + ROPE) ** -0.5)
ROPE_BASE = 10000.0
NEG = -1.0e30

STAGES = [("ffn", 0), ("hyb", 0), ("ffn", 1), ("ple", 0), ("ffn", 2), ("mla", 0), ("ffn", 3), ("ple", 1)]
N_UNITS = {"ffn": FFN_UNITS, "hyb": 26, "ple": 5, "mla": 15}


def hybrid_trunk(nc, stages, a, out):
    f32, f32r, bf16, i32 = mybir.dt.float32, mybir.dt.float32r, mybir.dt.bfloat16, mybir.dt.int32
    ALU = mybir.AluOpType
    ACT = mybir.ActivationFunctionType

    first = {}
    n_units = 0
    for s, (kind, _) in enumerate(stages):
        first[s] = n_units
        n_units += N_UNITS[kind]
    NS = len(stages)

    ctx = ExitStack()
    with ctx:
        base = 16512
        at = [base]

        def place(name, shape, dt=f32, offset=None):
            size = int(np.prod(shape[1:])) * (2 if dt == bf16 else 4)
            if offset is None:
                offset = at[0]
                at[0] += (size + 31) // 32 * 32
            return nc.alloc_sbuf_tensor_at(name, shape, dt, offset=offset)

        raw = place("raw", [P, RING, UNIT])
        WH = place("WH", [P, RING, UNIT], f32r)
        WL = place("WL", [P, RING, UNIT], f32r)
        x_at = at[0]
        XH = place("XH", [P, KT, SEQ], f32r)
        XL = place("XL", [P, KT, SEQ], f32r)
        c_at = at[0]
        CH = place("CH", [P, 16, SEQ], f32r)
        CL = place("CL", [P, 16, SEQ], f32r)
        h = place("h", [P, 2, D])
        PG = place("PG", [P, D])
        QG = place("QG", [P, D])
        hn_at = at[0]
        hn = place("hn", [P, 2, D])
        junk = place("junk", [P, 2, D])
        ident = place("ident", [P, P])
        zeros = place("zeros", [P, BANK], bf16)
        stat = place("stat", [P, 128])
        nhalf = place("nhalf", [P, 8])
        tri = place("tri", [P, P])
        cmask = place("cmask", [P, 2 * P])
        cosT = place("cosT", [P, 2, ROPE // 2])
        sinT = place("sinT", [P, 2, ROPE // 2])
        mark = place("mark", [P, 8])
        s_at = at[0]
        end = 229344

        sg = place("sg", [P, 2, CHUNK], offset=s_at)
        act_h = place("act_h", [P, 2, CHUNK], offset=s_at + 4096)
        HH = place("HH", [P, 4, SEQ], f32r, offset=c_at)
        HL = place("HL", [P, 4, SEQ], f32r, offset=c_at + 4096)
        TH = place("TH", [P, 2, SEQ], f32r, offset=s_at + 8192)
        TL = place("TL", [P, 2, SEQ], f32r, offset=s_at + 8192 + 2048)
        gsb = place("gsb", [P, 2, D], offset=s_at + 8192)
        p_raw = place("p_raw", [P, 2, SEQ], offset=c_at + 8192)
        p_hi = place("p_hi", [P, 2, SEQ], f32r, offset=c_at + 8192 + 2048)
        p_lo = place("p_lo", [P, 2, SEQ], f32r, offset=c_at + 8192 + 4096)

        PS = ctx.enter_context(nc.psum_tensor("PS", [P, 8, BANK], f32))
        A, B, C, T = 0, 1, 2, 3

        def acc(t):
            return PS[:, 4 + 2 * t:6 + 2 * t, :]

        sems = {}

        def sem(name):
            if name not in sems:
                sems[name] = ctx.enter_context(nc.semaphore(name))
            return sems[name]

        for name in ("raw0", "raw1", "raw2", "w_hi", "w_lo", "w_used", "x_loaded0", "x_loaded1", "consts", "pg", "qg",
                     "out_done", "ple_done", "post_sq", "post_y", "post_rs", "w_lo_pool", "w_lo_half", "h_new", "pre_sq", "pre_rs", "hn_done",
                     "x_tr", "x_hi", "x_lo", "gate", "silu", "up", "acted", "h_tr", "h_hi", "h_lo",
                     "act_chain", "dve_chain", "pool_chain", "stored"):
            sem(name)

        chains = {"dve_chain": 0, "pool_chain": 0}

        def link(eng, name, ins):
            chains[name] += 1
            ins.then_inc(sem(name), 1)
            eng.wait_ge(sem(name), chains[name])

        def unit_at(n, k, step):
            return n if k is None else k * step + n

        def load_unit(sp, n, k=None, step=0):
            if n >= RING:
                sp.wait_ge(sem("w_hi"), unit_at(n - RING + 1, k, step))
                sp.wait_ge(sem("w_lo"), unit_at(n - RING + 1, k, step))
            if k is None:
                src = a["stream"][n, :, :]
            else:
                src = a["stream"][bass.ds(k * step + n, 1), :, :].rearrange("a p n -> (a p) n")
            sp.dma_start(raw[:, n % RING, :], src).then_inc(sem(f"raw{n % RING}"), 16)

        def split_hi(act, n, k=None, step=0):
            if n >= n_units:
                return
            rounds = 16 * (n // RING + 1)
            act.wait_ge(sem(f"raw{n % RING}"), rounds if k is None else k * (16 * step // RING) + rounds)
            if n >= RING:
                act.wait_ge(sem("w_used"), unit_at(n - RING + 1, k, step))
            act.activation(WH[:, n % RING, :], raw[:, n % RING, :], ACT.Copy).then_inc(sem("w_hi"), 1)

        def split_lo(dve, n, k=None, step=0):
            if n >= n_units:
                return
            dve.wait_ge(sem("w_hi"), unit_at(n + 1, k, step))
            dve.tensor_tensor(WL[:, n % RING, :], raw[:, n % RING, :], WH[:, n % RING, :],
                              ALU.subtract).then_inc(sem("w_lo"), 1)

        def split_lo_half(eng, n, part):
            eng.wait_ge(sem("w_hi"), n + 1)
            cols = slice(part * UNIT // 2, (part + 1) * UNIT // 2)
            return eng.tensor_tensor(WL[:, n % RING, cols], raw[:, n % RING, cols], WH[:, n % RING, cols], ALU.subtract)

        def splitter(eng, split):
            done = [0]

            def split_to(n):
                while done[0] <= n:
                    split(eng, done[0])
                    done[0] += 1
            return done, split_to

        def whole(tile, n):
            return tile[:, n % RING, :]

        def product(pe, out_ap, xh, xl, wh, wl, start, stop):
            pe.matmul(out_ap, xh, wh, start=start, stop=False)
            pe.matmul(out_ap, xl, wh, start=False, stop=False)
            return pe.matmul(out_ap, xh, wl, start=False, stop=stop)

        def tok(t):
            return slice(t * P, (t + 1) * P)

        by_pool = {first[s] + 1: s for s in range(1, NS)}

        def split_done(pe, n, k=None, step=0):
            if k is None and n in by_pool:
                pe.wait_ge(sem("w_lo_pool"), 2 * by_pool[n])
                pe.wait_ge(sem("w_lo_half"), by_pool[n])
            else:
                pe.wait_ge(sem("w_lo"), unit_at(n + 1, k, step))

        def lagged(units):
            units = list(units)
            order = [(units[0], 0)]
            for j in range(1, len(units)):
                order += [(units[j], 0), (units[j - 1], 1)]
            return order + [(units[-1], 1)]

        def wide(pe, n, t, bank, xh, xl, kt, start, stop, done=None, k=None, step=0, middle=None):
            split_done(pe, n, k, step)
            wh = whole(WH, n).rearrange("p (k n) -> p k n", k=2)
            wl = whole(WL, n).rearrange("p (k n) -> p k n", k=2)
            for c in range(2):
                if c and middle is not None:
                    middle()
                for q in range(2):
                    ins = product(pe, PS[:, bank + c, :], xh[:, kt + q, tok(t)], xl[:, kt + q, tok(t)],
                                  wh[:, q, c * BANK:(c + 1) * BANK], wl[:, q, c * BANK:(c + 1) * BANK],
                                  start and q == 0, stop and q == 1)
                if (t, c) == (1, 1):
                    ins.then_inc(sem("w_used"), 1)
                elif done:
                    ins.then_inc(sem(done), 1)

        def col(s, t, what):
            c = (2 * s + t) * 8 + what
            return stat[:, c:c + 1]

        SQ, RS = 0, 1
        POST_RS, POST_SQ = 2, 3

        def post_factor(s):
            return 0.5 if stages[s][0] == "ffn" else 1.0

        def half(a_):
            return slice(a_ * BANK, (a_ + 1) * BANK)

        def source(s, t, b):
            n = 2 * t + b
            if stages[s][0] == "ple":
                return gsb[:, t, half(b)], sem("ple_done"), 4 * sum(k == "ple" for k, _ in stages[:s]) + n + 1
            if n == 3:
                return PS[:, 7, :], sem("w_used"), first[s] + N_UNITS[stages[s][0]]
            return PS[:, 4 + n, :], sem("out_done"), 3 * sum(k != "ple" for k, _ in stages[:s]) + n + 1

        def post_square(act, s, t):
            for b in range(2):
                if stages[s][0] == "ple":
                    ple_sigmoid(act, s, t, b)
            for b in range(2):
                src, ready, value = source(s, t, b)
                act.wait_ge(ready, value)
                act.activation(junk[:, t, half(b)], src, ACT.Square, scale=1.0 / 32 / post_factor(s),
                               accum_out=col(s, t, POST_SQ + b)).then_inc(sem("post_sq"), 1)

        def h_ready(eng, s, t, b=1):
            if s:
                eng.wait_ge(sem("h_new"), 4 * (s - 1) + 2 * t + b + 1)
            else:
                eng.wait_ge(sem(f"x_loaded{t}"), 16)

        def pre_square(act, s, t):
            h_ready(act, s, t)
            act.activation(junk[:, t, :], h[:, t, :], ACT.Square, scale=1.0 / 32, accum_out=col(s, t, SQ))\
               .then_inc(sem("pre_sq"), 1)

        def inverse_rms(pool, s, t):
            pool.wait_ge(sem("pre_sq"), 2 * s + t + 1)
            link(pool, "pool_chain", pool.tensor_scalar(col(s, t, RS), col(s, t, SQ), 1.0, EPS, ALU.mult, ALU.add))
            pool.tensor_tensor(col(s, t, RS), col(s, t, RS), nhalf[:, 0:1], ALU.pow).then_inc(sem("pre_rs"), 1)

        def gained(dve, s, t, b):
            src, ready, value = source(s, t, b)
            dve.wait_ge(ready, value)
            dve.wait_ge(sem("post_sq"), 4 * s + 2 * t + b + 1)
            if (t, b) == (0, 0):
                dve.wait_ge(sem("pg"), 16 * (s + 1))
            dve.tensor_tensor(hn[:, t, half(b)], src, PG[:, half(b)], ALU.mult).then_inc(sem("post_y"), 1)

        def post_inverse_rms(pool, s, t):
            pool.wait_ge(sem("post_sq"), 4 * s + 2 * t + 2)
            link(pool, "pool_chain", pool.tensor_scalar(col(s, t, POST_RS), col(s, t, POST_SQ), col(s, t, POST_SQ + 1),
                                                        EPS / post_factor(s) ** 2, ALU.add, ALU.add))
            pool.tensor_tensor(col(s, t, POST_RS), col(s, t, POST_RS), nhalf[:, 0:1], ALU.pow)\
                .then_inc(sem("post_rs"), 1)

        def update_h(dve, s, t, b):
            dve.wait_ge(sem("post_y"), 4 * s + 2 * t + b + 1)
            dve.scalar_tensor_tensor(h[:, t, half(b)], hn[:, t, half(b)], col(s, t, POST_RS), h[:, t, half(b)],
                                     ALU.mult, ALU.add).then_inc(sem("h_new"), 1)

        def behind(dve, s, t):
            if s >= 0:
                if stages[s][0] == "ple":
                    ple_product(dve, s, t, 0)
                    ple_product(dve, s, t, 1)
                for b in range(2):
                    gained(dve, s, t, b)
                dve.wait_ge(sem("post_rs"), 2 * s + t + 1)
                if t == 1 and s + 1 < NS:
                    dve.wait_ge(sem("w_lo_pool"), 2 * (s + 1))
                    dve.memset(mark[:, :], 0.0).then_inc(sem("w_lo"), 1)
            for b in range(2):
                if s >= 0:
                    update_h(dve, s, t, b)
                if s + 1 < NS:
                    normed(dve, s + 1, t, b)

        def normed(dve, s, t, b):
            h_ready(dve, s, t, b)
            if (t, b) == (0, 0):
                dve.wait_ge(sem("qg"), 16 * (s + 1))
            dve.tensor_tensor(hn[:, t, half(b)], h[:, t, half(b)], QG[:, half(b)], ALU.mult)\
               .then_inc(sem("hn_done"), 1)

        def x_bank(s, t, a_):
            return (2 * t if t == 0 or stages[s][0] != "ffn" else 4) + a_

        def transpose_x(pe, s, t, halves=(0, 1)):
            for a_ in halves:
                pe.wait_ge(sem("hn_done"), 4 * s + 2 * t + a_ + 1)
                for q in range(4):
                    kt = 4 * a_ + q
                    ins = pe.transpose(PS[:, x_bank(s, t, a_), q * P:(q + 1) * P], hn[:, t, kt * P:(kt + 1) * P],
                                       ident[:, :])
                ins.then_inc(sem("x_tr"), 1)

        def next_x(pe, s):
            if s + 1 < NS:
                return lambda: transpose_x(pe, s + 1, 0)

        def x_there(pe, s, t, a_):
            pe.wait_ge(sem("x_lo"), 4 * s + 2 * t + a_ + 1)

        def x_half(tile, t, a_):
            return tile[:, 4 * a_:4 * a_ + 4, tok(t)]

        def x_psum(s, t, a_):
            return PS[:, x_bank(s, t, a_), :].rearrange("p (k n) -> p k n", n=P)

        def x_high(act, s, t, halves=(0, 1)):
            for a_ in halves:
                act.wait_ge(sem("x_tr"), 4 * s + 2 * t + a_ + 1)
                act.activation(x_half(XH, t, a_), x_psum(s, t, a_), ACT.Copy).then_inc(sem("x_hi"), 1)

        def x_low(dve, s, t):
            for a_ in range(2):
                dve.wait_ge(sem("x_hi"), 4 * s + 2 * t + a_ + 1)
                dve.tensor_tensor(x_half(XL, t, a_), x_psum(s, t, a_), x_half(XH, t, a_), ALU.subtract)\
                   .then_inc(sem("x_lo"), 1)

        def load_table(act, func):
            act.activation(mark[:, 4:5], nhalf[:, 0:1], func)

        def boundary_act(act, s, split_to):
            m = first[s] if s < NS else n_units
            if s:
                post_square(act, s - 1, 0)
            if s == NS:
                post_square(act, s - 1, 1)
                return
            if s:
                split_to(m + 1)
            x_high(act, s, 0)
            split_to(m + 1)
            if s:
                post_square(act, s - 1, 1)
            pre_square(act, s, 0)
            split_to(m + 3 if stages[s][0] == "ple" else m + 2)
            if stages[s][0] == "mla":
                return
            x_high(act, s, 1)
            pre_square(act, s, 1)
            if stages[s][0] == "ffn":
                if s == 0:
                    act.wait_ge(sem("consts"), 1)
                load_table(act, ACT.Silu)

        def boundary_dve(dve, s, done, split_to):
            m = first[s] if s < NS else n_units
            behind(dve, s - 1, 0)
            if s == NS:
                behind(dve, s - 1, 1)
                return
            if s:
                dve.wait_ge(sem("w_lo_pool"), 2 * s - 1)
                split_lo_half(dve, m, 1).then_inc(sem("w_lo"), 1)
                done[0] = m + 1
            split_to(m)
            x_low(dve, s, 0)
            if s:
                split_lo_half(dve, m + 1, 1).then_inc(sem("w_lo_half"), 1)
                done[0] = m + 2
            else:
                split_to(m + 1)
            behind(dve, s - 1, 1)
            x_low(dve, s, 1)
            if stages[s][0] != "mla":
                split_to(m + 2)

        def boundary_pool(pool, s):
            if s:
                post_inverse_rms(pool, s - 1, 0)
                if s < NS:
                    for n in (first[s], first[s] + 1):
                        split_lo_half(pool, n, 0).then_inc(sem("w_lo_pool"), 1)
                post_inverse_rms(pool, s - 1, 1)
            if s == NS:
                return
            for t in range(1 if stages[s][0] == "mla" else 2):
                inverse_rms(pool, s, t)

        def load_gains(pool, s):
            if s:
                pool.wait_ge(sem("post_y"), 4 * s)
            pool.dma_start(PG[:, :], a["post_g"][s, :].partition_broadcast(P)).then_inc(sem("pg"), 16)
            if s + 1 < NS:
                pool.wait_ge(sem("hn_done"), 4 * s + 4)
                pool.dma_start(QG[:, :], a["pre_g"][s + 1, :].partition_broadcast(P)).then_inc(sem("qg"), 16)

        def ffn_chunk_pe(pe, f, s, g, c, k=None, half=False):
            def n2(t):
                v = 12 * f + 2 * c + t + 1
                return v if k is None else k * 2 + v

            def n1(d=0):
                v = 6 * f + c + 1 - d
                return v if k is None else k + v

            start = c == 0 and k is None
            width = CHUNK // 2 if half else CHUNK
            units = 1 if half else 2
            per = KT // units
            pairs = [(j, t) for j in range(2 * units) for t in range(2)]
            for j, t in lagged(range(4)) if start else pairs:
                up, part = j // units, j % units
                if start and (j, t) == (0, 1):
                    transpose_x(pe, s, 1, (1,))
                n = g + j
                split_done(pe, n, k, 6)
                wh = whole(WH, n).rearrange("p (k n) -> p k n", k=per)
                wl = whole(WL, n).rearrange("p (k n) -> p k n", k=per)
                if start and not up:
                    x_there(pe, s, t, part)
                if up and part == 0 and t == 0 and not start:
                    pe.wait_ge(sem("h_lo"), n1(1))
                if up and part == 0 and t == 1:
                    pe.wait_ge(sem("silu"), n2(0))
                bank = (C, A)[t] if up else (A, B)[t]
                for q in range(per):
                    if start and (j, t, q) == (1, 0, per - 1):
                        transpose_x(pe, s, 1, (0,))
                    kt = part * per + q
                    ins = product(pe, PS[:, bank, 0:width], XH[:, kt, tok(t)], XL[:, kt, tok(t)],
                                  wh[:, q, :], wl[:, q, :], kt == 0, kt == KT - 1)
                if t == 1:
                    ins.then_inc(sem("w_used"), 1)
                elif part == units - 1:
                    ins.then_inc(sem("up" if up else "gate"), 1)
            return n2, n1

        def ffn_down_pe(pe, g, j, t, k=None):
            wide(pe, g + j, t, 4 + 2 * t, HH, HL, 2 * j, False, False, None, k, 6)

        def ffn_transpose_pe(pe, n2, kts=4):
            for t in range(2):
                pe.wait_ge(sem("acted"), n2(t))
            for q in range(kts):
                for t in range(2):
                    ins = pe.transpose(PS[:, C + q // 2, (q % 2) * SEQ + t * P:(q % 2) * SEQ + (t + 1) * P],
                                       act_h[:, t, q * P:(q + 1) * P], ident[:, :])
            ins.then_inc(sem("h_tr"), 1)

        def ffn_pe(pe, s):
            f, u = stages[s][1], first[s]
            n2, n1 = ffn_chunk_pe(pe, f, s, u, 0)
            for b in range(4, 8):
                pe.matmul(PS[:, b, :], zeros[:, 0:P], zeros[:, :], start=True, stop=False)
            ffn_transpose_pe(pe, n2)
            with pe.Fori(0, FULL - 1) as k:
                n2, n1 = ffn_chunk_pe(pe, f, s, u + 4, 1, k)
                for j in range(2):
                    for t in range(2):
                        ffn_down_pe(pe, u + 8, j, t, k)
                ffn_transpose_pe(pe, n2)
            g = u + 4 + 6 * (FULL - 1)
            n2, n1 = ffn_chunk_pe(pe, f, s, g, FULL, half=True)
            ffn_down_pe(pe, g + 2, 0, 0)
            ffn_down_pe(pe, g + 2, 1, 0)
            ffn_transpose_pe(pe, n2, 2)
            ffn_down_pe(pe, g + 2, 0, 1)
            pe.wait_ge(sem("h_lo"), n1())
            wide(pe, g + 4, 0, 4, TH, TL, 0, False, True, "out_done")
            ffn_down_pe(pe, g + 2, 1, 1)
            wide(pe, g + 4, 1, 6, TH, TL, 0, False, True, "out_done", middle=next_x(pe, s))

        def ffn_product_done(eng, name, f, c, t, n, k):
            if t == 0:
                eng.wait_ge(sem(name), unit_at(6 * f + c + 1, k, 1))
            else:
                eng.wait_ge(sem("w_used"), unit_at(n + 1, k, 6))

        def ffn_silu(act, s, f, c, n, k=None, width=CHUNK):
            for t in range(2):
                v = 12 * f + 2 * c + t + 1
                ffn_product_done(act, "gate", f, c, t, n, k)
                if c == 0:
                    act.wait_ge(sem("pre_rs"), 2 * s + t + 1)
                if v > 2:
                    act.wait_ge(sem("acted"), v - 2 if k is None else k * 2 + (v - 2))
                act.activation(sg[:, t, 0:width], PS[:, (A, B)[t], 0:width], ACT.Silu, scale=col(s, t, RS))\
                   .then_inc(sem("silu"), 1)

        def h_bank(kts):
            return PS[:, C:C + (kts + 1) // 2, :]

        def h_tile(tile, kts):
            return tile[:, 0:kts, :].rearrange("p (a k) n -> p a (k n)", k=2)

        def ffn_high(act, f, c, k=None, kts=4, high=HH):
            v = 6 * f + c + 1
            act.wait_ge(sem("h_tr"), v if k is None else k + v)
            act.activation(h_tile(high, kts), h_bank(kts), ACT.Copy).then_inc(sem("h_hi"), 1)

        def ffn_low(dve, f, c, k=None, kts=4, high=HH, low=HL):
            v = 6 * f + c + 1
            dve.wait_ge(sem("h_hi"), v if k is None else k + v)
            dve.tensor_tensor(h_tile(low, kts), h_bank(kts), h_tile(high, kts), ALU.subtract)\
               .then_inc(sem("h_lo"), 1)

        def ffn_mult(dve, s, f, c, n, k=None, width=CHUNK):
            for t in range(2):
                ffn_product_done(dve, "up", f, c, t, n, k)
                if c == 0:
                    dve.wait_ge(sem("silu"), 12 * f + t + 1)
                if t == 0 and 6 * f + c > 0:
                    w = 6 * f + c
                    dve.wait_ge(sem("h_tr"), w if k is None else k + w)
                dve.scalar_tensor_tensor(act_h[:, t, 0:width], PS[:, (C, A)[t], 0:width], col(s, t, RS),
                                         sg[:, t, 0:width], ALU.mult, ALU.mult).then_inc(sem("acted"), 1)

        def ffn_act(act, s, done, split_to):
            f, u = stages[s][1], first[s]
            split_to(u + 3)
            ffn_silu(act, s, f, 0, u + 1)
            if s == 0:
                prelude_act(act)
            split_to(u + 5)
            ffn_high(act, f, 0)
            with act.Fori(0, FULL - 1) as k:
                g = u + 4
                split_hi(act, g + 2, k, 6)
                split_hi(act, g + 3, k, 6)
                ffn_silu(act, s, f, 1, g + 1, k)
                for j in range(4, 8):
                    split_hi(act, g + j, k, 6)
                ffn_high(act, f, 1, k)
            g = u + 4 + 6 * (FULL - 1)
            done[0] = g + 2
            split_to(g + 2)
            ffn_silu(act, s, f, FULL, g, width=CHUNK // 2)
            split_to(g + 4)
            if s + 1 < NS and stages[s + 1][0] == "ple":
                act.wait_ge(sem("p_loaded"), 16 * (stages[s + 1][1] + 1))
                act.activation(p_hi[:, :, :], p_raw[:, :, :], ACT.Copy).then_inc(sem("p_hi"), 1)
            ffn_high(act, f, FULL, kts=2, high=TH)
            split_to(g + 5)

        def ffn_dve(dve, s, done, split_to):
            f, u = stages[s][1], first[s]
            if s == 0:
                prelude_dve(dve)
            split_to(u + 4)
            ffn_mult(dve, s, f, 0, u + 3)
            split_to(u + 5)
            ffn_low(dve, f, 0)
            if s == 0:
                prelude_dve_end(dve)
            with dve.Fori(0, FULL - 1) as k:
                g = u + 4
                for j in range(2, 7):
                    split_lo(dve, g + j, k, 6)
                ffn_mult(dve, s, f, 1, g + 3, k)
                split_lo(dve, g + 7, k, 6)
                ffn_low(dve, f, 1, k)
            g = u + 4 + 6 * (FULL - 1)
            done[0] = g + 2
            split_to(g + 4)
            ffn_mult(dve, s, f, FULL, g + 1, width=CHUNK // 2)
            if s + 1 < NS and stages[s + 1][0] == "ple":
                dve.wait_ge(sem("p_hi"), stages[s + 1][1] + 1)
                dve.tensor_tensor(p_lo[:, :, :], p_raw[:, :, :], p_hi[:, :, :], ALU.subtract)\
                   .then_inc(sem("p_lo"), 1)
            ffn_low(dve, f, FULL, kts=2, high=TH, low=TL)

        def ffn_pool(pool, s):
            if s + 1 < NS and stages[s + 1][0] == "hyb":
                hyb_early(pool)
            if s + 1 < NS and stages[s + 1][0] == "mla":
                h_ready(pool, s, 1)
                mla_early(pool)
            if s + 1 < NS and stages[s + 1][0] == "ple":
                h_ready(pool, s, 1)
                pool.dma_start(p_raw[:, :, :], a["p_t"][stages[s + 1][1]].rearrange("(k p) n -> p k n", p=P))\
                    .then_inc(sem("p_loaded"), 16)

        def ple_pe(pe, s):
            i, u = stages[s][1], first[s]
            pe.wait_ge(sem("p_lo"), i + 1)
            for t in range(2):
                pe.wait_ge(sem("post_sq"), 4 * (s - 1) + 2 * t + 2)
                pe.wait_ge(sem("post_y"), 4 * (s - 1) + 2 * t + 2)
                wide(pe, u, t, 4 + 2 * t, p_hi, p_lo, 0, True, True)
            for j, t in [(0, 0), (0, 1), (1, 0), (2, 0), (3, 0), (1, 1), (2, 1), (3, 1)]:
                if j == 0:
                    x_there(pe, s, t, 1)
                wide(pe, u + 1 + j, t, 2 * t, XH, XL, 2 * j, j == 0, j == 3, "ple_gate" if j == 3 else None,
                     middle=(lambda: transpose_x(pe, s, 1)) if (j, t) == (0, 0) else None)

        def ple_sigmoid(act, s, t, b):
            i, n = stages[s][1], 2 * t + b
            if n < 3:
                act.wait_ge(sem("ple_gate"), 3 * i + n + 1)
            else:
                act.wait_ge(sem("w_used"), first[s] + 5)
            act.wait_ge(sem("pre_rs"), 2 * s + t + 1)
            act.activation(gsb[:, t, half(b)], PS[:, n, :], ACT.Sigmoid, scale=col(s, t, RS)).then_inc(sem("ple_sig"), 1)

        def ple_product(dve, s, t, b):
            n = 2 * t + b
            dve.wait_ge(sem("ple_sig"), 4 * stages[s][1] + n + 1)
            dve.tensor_tensor(gsb[:, t, half(b)], PS[:, 4 + n, :], gsb[:, t, half(b)], ALU.mult)\
               .then_inc(sem("ple_done"), 1)

        def ple_act(act, s, done, split_to):
            split_to(first[s] + 4)
            load_table(act, ACT.Sigmoid)

        def ple_dve(dve, s, done, split_to):
            split_to(first[s] + 4)

        for name in ("p_loaded", "p_hi", "p_lo", "ple_gate", "ple_sig"):
            sem(name)

        XBC, Z, V, UU = (0, 1, 2), (3, 4), (5, 6), (7, 8)
        P0, P1, P2, CT = 0, 4, 6, 2
        PAIR = [P0, P1, P2, P0, P2, P0, P1, P2, P0]
        NCH = CONV_CH // P
        GH = 8
        STATE = 128

        def pair(b):
            return PS[:, b:b + 2, :]

        def flat_pair(b):
            return pair(b).rearrange("p a n -> p (a n)")

        o = s_at
        cx = place("cx", [P, NCH, SEQ + 3], offset=o); o += NCH * (SEQ + 3) * 4 + 16
        xs = place("xs", [P, 2, SSD_IN], offset=o); o += 8192
        xd = place("xd", [P, 2, SSD_IN], offset=o); o += 8192
        zs = place("zs", [P, 2, SSD_IN], offset=o); o += 8192
        Eg = place("Eg", [P, 2, GH, P], offset=o); o += 8192
        cbm = place("cbm", [P, 4, P], offset=o); o += 2048
        sm_at = o
        sm = place("sm", [P, 512], offset=o); o += 2048
        Btok = place("Btok", [P, 2 * STATE], offset=o); o += 1024
        assert o <= end, o
        vt = hn
        gm_g = place("gm_g", [P, GM_W], offset=c_at)
        gm_b = place("gm_b", [P, GM_W], offset=c_at + 4096)
        dt_w = place("dt_w", [P, KT, HEADS], offset=c_at + 16384)
        dt_hi = place("dt_hi", [P, KT, HEADS], f32r, offset=c_at + 16384 + 512)
        dt_lo = place("dt_lo", [P, KT, HEADS], f32r, offset=c_at + 16384 + 1024)
        dtT = place("dtT", [HEADS, SEQ], offset=c_at + 16384 + 1536)
        wsT = place("wsT", [P, 8, P], offset=c_at + 16384 + 4096)
        ca = place("ca", [P, 4, SEQ], offset=c_at + 8192)
        xde = place("xde", [P, SSD_IN], offset=c_at + 12288)
        ug = place("ug", [P, 2, 2, CHUNK], offset=c_at + 16384 + 8192)
        xt = place("xt", [P, 2, CHUNK], offset=c_at + 16384 + 12288)
        stT = place("stT", [P, 2, BANK], offset=x_at + 8192)
        yo = place("yo", [P, SSD_IN], offset=x_at + 12288)
        ng = place("ng", [P, SSD_IN], offset=x_at + 4096)

        def smc(lo, n):
            return sm[:, lo:lo + n]
        CW, CB, BS = smc(0, 48), smc(48, 12), smc(60, 8)
        DV, DTB, ALOG = smc(68, 16), smc(84, 16), smc(100, 16)
        X0 = sm[:, 116:148]
        NA, EX, S1, S2, PO, DT, DA = (smc(148 + 32 * i, 32) for i in range(7))
        ACS = smc(372, 48)
        DTE, EA, NEGA = smc(420, 16), smc(436, 16), smc(452, 16)
        BN = Eg[:, 1, 0:1, 0:96].rearrange("p a b -> p (a b)")
        MV = smc(468, 16)
        RV = smc(484, 8)
        GQ = smc(492, 8)

        for name in ("hy_small", "hy_dtw", "hy_gm", "hy_ws", "hy_wsm", "hy_ng", "hy_ev", "hy_trx", "hy_cx", "hy_pad",
                     "hy_ca", "hy_conv", "hy_dth", "hy_dtl", "hy_dtp", "hy_dtc", "hy_dtt", "hy_dtv", "hy_na", "hy_ex", "hy_al",
                     "hy_da", "hy_acs", "hy_acv", "hy_dea", "hy_dte", "hy_back", "hy_xs", "hy_xd", "hy_bc",
                     "hy_bt", "hy_cbm", "hy_abc", "hy_seg", "hy_exp", "hy_G", "hy_mv", "hy_skip", "hy_rv", "hy_vn", "hy_v", "hy_t0",
                     "hy_mix", "hy_mixv", "hy_ya", "hy_trya", "hy_yahi", "hy_yalo", "hy_yd", "hy_st", "hy_stv",
                     "hy_yo", "hy_yoff", "hy_y", "hy_ysq", "hy_yrs", "hy_yn", "hy_try", "hy_yhi", "hy_ylo"):
            sem(name)

        def heads(ap, n=HEADS):
            return ap.rearrange("p (h q) -> p h q", h=n)

        def per_head(ap, n, width):
            return ap.unsqueeze(2).broadcast_to([P, n, width])

        def gemm_free(pe, idx):
            before = {3: 1, 4: 3, 5: 4, 7: 5, 8: 6}
            if idx in before:
                pe.wait_ge(sem("hy_ev"), before[idx])
            if idx == 6:
                pe.wait_ge(sem("hy_dtv"), 1)

        def hyb_pe(pe, s):
            u = first[s]

            def gemm(idx, parts=(0, 1)):
                if parts[0] == 0:
                    gemm_free(pe, idx)
                order = lagged(range(2)) if idx == 0 else [(j, t) for j in parts for t in range(2)]
                for j, t in order:
                    if idx == 0:
                        if (j, t) == (0, 1):
                            transpose_x(pe, s, 1, (1,))
                        x_there(pe, s, t, j)
                    n = u + 2 * idx + j
                    split_done(pe, n)
                    wh = whole(WH, n).rearrange("p (k n) -> p k n", k=4)
                    wl = whole(WL, n).rearrange("p (k n) -> p k n", k=4)
                    for q in range(4):
                        if (idx, j, t, q) == (0, 1, 0, 3):
                            transpose_x(pe, s, 1, (0,))
                        kt = 4 * j + q
                        ins = product(pe, PS[:, PAIR[idx] + t, :], XH[:, kt, tok(t)], XL[:, kt, tok(t)],
                                      wh[:, q, :], wl[:, q, :], kt == 0, kt == KT - 1)
                    if t == 1:
                        ins.then_inc(sem("w_used"), 1)

            def transpose_conv_input(j):
                pe.wait_ge(sem("hy_ev"), j + 1)
                if j:
                    pe.wait_ge(sem("hy_cx"), j)
                for q in range(4):
                    for t in range(2):
                        ins = pe.transpose(PS[:, CT + q // 2, (q % 2) * SEQ + t * P:(q % 2) * SEQ + (t + 1) * P],
                                           xt[:, t, q * P:(q + 1) * P], ident[:, :])
                ins.then_inc(sem("hy_trx"), 1)

            def back(t):
                if t == 0:
                    pe.wait_ge(sem("hy_conv"), 2)
                    pe.wait_ge(sem("hy_acv"), 1)
                else:
                    pe.wait_ge(sem("hy_xd"), 1)
                for q in range(8):
                    ins = pe.transpose(PS[:, CT + q // 4, (q % 4) * P:(q % 4 + 1) * P],
                                       cx[:, q, 3 + t * P:3 + (t + 1) * P], ident[:, :])
                ins.then_inc(sem("hy_back"), 1)

            def cumulated(t, g):
                n = 2 * t + g
                if n == 0:
                    pe.wait_ge(sem("hy_cbm"), 1)
                    pe.wait_ge(sem("hy_bt"), 1)
                elif n == 2:
                    pe.wait_ge(sem("hy_yalo"), 2)
                else:
                    pe.wait_ge(sem("hy_seg"), n)
                for r in range(GH):
                    c = t * HEADS + g * GH + r
                    ins = pe.matmul(PS[:, CT + r // 4, (r % 4) * P:(r % 4 + 1) * P],
                                    DA[:, c:c + 1].broadcast_to([P, P]), tri[:, :], start=True, stop=True)
                ins.then_inc(sem("hy_abc"), 1)

            def mix(c):
                b = (P1, P2)[c]
                if c == 0:
                    pe.wait_ge(sem("hy_wsm"), 1)
                    pe.wait_ge(sem("hy_ev"), 7)
                else:
                    pe.wait_ge(sem("hy_ev"), 8)
                pe.wait_ge(sem("hy_v"), c + 1)
                for r in range(8):
                    ins = pe.matmul(PS[:, b + r // 4, (r % 4) * P:(r % 4 + 1) * P], wsT[:, r, :],
                                    vt[:, c, r * P:(r + 1) * P], start=True, stop=True)
                ins.then_inc(sem("hy_mix"), 1)

            def diagonal(t, g):
                pe.wait_ge(sem("hy_G"), 2 * t + g + 1)
                if g == 0:
                    if t == 0:
                        pe.wait_ge(sem("hy_ev"), 9)
                        pe.wait_ge(sem("hy_xd"), 2)
                    else:
                        pe.wait_ge(sem("hy_y"), 1)
                for r in range(GH):
                    ins = pe.matmul(PS[:, P0 + g, r * 64:(r + 1) * 64], Eg[:, g, r, :],
                                    xd[:, t, (g * GH + r) * 64:(g * GH + r + 1) * 64], start=True, stop=True)
                ins.then_inc(sem("hy_yd"), 1)

            def transpose_out(src, t, done):
                for q in range(8):
                    ins = pe.transpose(PS[:, CT + q // 4, (q % 4) * P:(q % 4 + 1) * P],
                                       src[:, t, q * P:(q + 1) * P], ident[:, :])
                ins.then_inc(sem(done), 1)

            def out_unit(j, t):
                if j == 0:
                    pe.wait_ge(sem("hy_mixv"), t + 1)
                    pe.wait_ge(sem("hy_yalo"), t + 1)
                if j == 4:
                    pe.wait_ge(sem("hy_ylo"), t + 1)
                wide(pe, u + 18 + j, t, 4 + 2 * t, CH, CL, 2 * j, j == 0, j == 7, "out_done" if j == 7 else None,
                     middle=next_x(pe, s) if (j, t) == (7, 1) else None)

            gemm(0)
            gemm(1)
            transpose_conv_input(0)
            gemm(2)
            transpose_conv_input(1)
            gemm(3)
            transpose_conv_input(2)
            pe.wait_ge(sem("hy_dtl"), 1)
            pe.wait_ge(sem("hy_ev"), 2)
            for kt in range(KT):
                ins = product(pe, PS[0:HEADS, P1, 0:SEQ], dt_hi[:, kt, :], dt_lo[:, kt, :], XH[:, kt, :], XL[:, kt, :],
                              kt == 0, kt == KT - 1)
            ins.then_inc(sem("hy_dtp"), 1)
            gemm(4, (0,))
            pe.wait_ge(sem("hy_dtc"), 1)
            for t in range(2):
                ins = pe.transpose(PS[:, P1, t * HEADS:(t + 1) * HEADS], dtT[:, tok(t)], ident[0:HEADS, 0:HEADS])
            ins.then_inc(sem("hy_dtt"), 1)
            gemm(4, (1,))
            gemm(5)
            pe.wait_ge(sem("hy_da"), 1)
            pe.wait_ge(sem("hy_cx"), 3)
            pe.matmul(PS[:, C, 0:32], tri[:, :], DA, start=True, stop=True)
            pe.matmul(PS[:, C, 32:48], tri[:, P - 1:P].broadcast_to([P, P]), DA[:, 0:HEADS], start=True, stop=True)\
              .then_inc(sem("hy_acs"), 1)
            gemm(6, (0,))
            back(0)
            gemm(6, (1,))
            gemm(7, (0,))
            back(1)
            gemm(7, (1,))
            pe.wait_ge(sem("hy_xd"), 2)
            pe.wait_ge(sem("hy_conv"), 3)
            for g in range(2):
                pe.transpose(PS[:, C, g * P:(g + 1) * P], cx[:, 8 + g, 3:3 + P], ident[:, :])
            for t in range(2):
                for g in range(2):
                    ins = pe.matmul(PS[:, T, (2 * t + g) * P:(2 * t + g + 1) * P], cx[:, 8 + g, 3 + t * P:3 + (t + 1) * P],
                                    cx[:, 10 + g, 3 + t * P:3 + (t + 1) * P], start=True, stop=True)
            ins.then_inc(sem("hy_bc"), 1)
            gemm(8, (0,))
            cumulated(0, 0)
            gemm(8, (1,))
            mix(0)
            cumulated(0, 1)
            mix(1)

            def transpose_ya(t):
                pe.wait_ge(sem("hy_ya"), t + 1)
                if t == 0:
                    pe.wait_ge(sem("hy_seg"), 2)
                else:
                    pe.wait_ge(sem("hy_yalo"), 1)
                transpose_out(vt, t, "hy_trya")

            def transpose_y(t):
                pe.wait_ge(sem("hy_yn"), t + 1)
                pe.wait_ge(sem("hy_yoff" if t == 0 else "hy_ylo"), 1)
                transpose_out(xs, t, "hy_try")

            transpose_ya(0)
            diagonal(0, 0)
            out_unit(0, 0)
            diagonal(0, 1)
            transpose_ya(1)
            out_unit(1, 0)
            out_unit(0, 1)
            cumulated(1, 0)
            out_unit(1, 1)
            cumulated(1, 1)
            out_unit(2, 0)
            diagonal(1, 0)
            pe.wait_ge(sem("hy_seg"), 4)
            for g in range(2):
                ins = pe.matmul(PS[:, CT + g, :], Btok[:, g * P:(g + 1) * P], xde[:, g * BANK:(g + 1) * BANK],
                                start=True, stop=True)
            ins.then_inc(sem("hy_st"), 1)
            diagonal(1, 1)
            pe.wait_ge(sem("hy_stv"), 1)
            for g in range(2):
                ins = pe.matmul(PS[:, CT + g, :], cx[:, 10 + g, 3 + P:3 + 2 * P], stT[:, g, :], start=True, stop=True)
            ins.then_inc(sem("hy_yo"), 1)
            out_unit(2, 1)
            transpose_y(0)
            out_unit(3, 0)
            out_unit(3, 1)
            transpose_y(1)
            for j, t in lagged(range(4, 8)):
                out_unit(j, t)

        def hyb_act(act, s, done, split_to):
            u = first[s]

            def evacuate(idx):
                act.wait_ge(sem("w_used"), u + 2 * idx + 2)
                if idx in XBC:
                    if idx:
                        act.wait_ge(sem("hy_trx"), idx)
                    dst, f = xt[:, :, :], ACT.Copy
                elif idx in Z:
                    dst, f = zs[:, :, (idx - 3) * BANK:(idx - 2) * BANK], ACT.Silu
                elif idx in V:
                    dst, f = vt[:, :, (idx - 5) * BANK:(idx - 4) * BANK], ACT.Gelu_apprx_tanh
                else:
                    if idx == 8:
                        act.wait_ge(sem("hy_trx"), 3)
                    dst, f = ug[:, idx - 7, :, :], ACT.Gelu_apprx_tanh
                if idx == 0:
                    act.wait_ge(sem("pre_rs"), 2 * s + 2)
                for t in range(2):
                    ins = act.activation(dst[:, t, :], PS[:, PAIR[idx] + t, :], f, scale=col(s, t, RS))
                ins.then_inc(sem("hy_ev"), 1)

            def first_tap(j):
                act.wait_ge(sem("hy_cx"), j + 1)
                if j == 0:
                    act.wait_ge(sem("hy_pad"), 1)
                else:
                    act.wait_ge(sem("hy_conv"), j)
                for q in range(4):
                    c = 4 * j + q
                    ins = act.activation(ca[:, q, :], cx[:, c, 0:SEQ], ACT.Identity, bias=CB[:, c:c + 1],
                                         scale=CW[:, 4 * c:4 * c + 1])
                ins.then_inc(sem("hy_t0"), 1)

            def conv_silu(j):
                act.wait_ge(sem("hy_ca"), j + 1)
                act.activation(cx[:, 4 * j:4 * j + 4, 3:3 + SEQ], ca[:, :, :], ACT.Silu).then_inc(sem("hy_conv"), 1)

            def decay(n):
                act.wait_ge(sem("hy_seg"), n + 1)
                act.activation(Eg[:, n % 2, :, :], Eg[:, n % 2, :, :], ACT.Exp).then_inc(sem("hy_exp"), 1)

            def copy_xs(t):
                act.wait_ge(sem("hy_back"), t + 1)
                act.activation(xs[:, t, :], flat_pair(CT), ACT.Copy).then_inc(sem("hy_xs"), 1)

            def out_high(t, base, tr, hi):
                act.wait_ge(sem(tr), t + 1)
                act.activation(CH[:, base:base + 8, tok(t)],
                               pair(CT).rearrange("p a (k n) -> p (a k) n", n=P), ACT.Copy).then_inc(sem(hi), 1)

            split_to(u + 2)
            act.wait_ge(sem("hy_dtw"), 16)
            act.activation(dt_hi[:, :, :], dt_w[:, :, :], ACT.Copy).then_inc(sem("hy_dth"), 1)
            act.wait_ge(sem("hy_small"), 32)
            act.activation(NEGA, ALOG, ACT.Exp).then_inc(sem("hy_al"), 1)
            split_to(u + 3)
            evacuate(0)
            split_to(u + 5)
            evacuate(1)
            split_to(u + 6)
            first_tap(0)
            split_to(u + 7)
            evacuate(2)
            split_to(u + 8)
            conv_silu(0)
            first_tap(1)
            split_to(u + 9)
            evacuate(3)
            split_to(u + 10)
            conv_silu(1)
            first_tap(2)
            act.wait_ge(sem("hy_na"), 1)
            act.activation(EX, NA, ACT.Exp).then_inc(sem("hy_ex"), 1)
            split_to(u + 11)
            evacuate(4)
            split_to(u + 12)
            split_to(u + 13)
            conv_silu(2)
            evacuate(5)
            act.wait_ge(sem("hy_dea"), 1)
            act.activation(DTE, DTE, ACT.Exp)
            act.activation(EA, ACS[:, HEADS:2 * HEADS], ACT.Exp).then_inc(sem("hy_dte"), 1)
            split_to(u + 14)
            copy_xs(0)
            split_to(u + 15)
            evacuate(6)
            split_to(u + 16)
            copy_xs(1)
            split_to(u + 17)
            evacuate(7)
            act.wait_ge(sem("hy_bc"), 1)
            act.activation(Btok[:, :], PS[:, C, 0:2 * P], ACT.Copy).then_inc(sem("hy_bt"), 1)
            split_to(u + 19)
            evacuate(8)
            decay(0)
            split_to(u + 20)

            def squares(t):
                act.wait_ge(sem("hy_y"), 2 * t + 2)
                for g in range(2):
                    act.activation(junk[:, t, g * BANK:(g + 1) * BANK], xs[:, t, g * BANK:(g + 1) * BANK], ACT.Square,
                                   accum_out=GQ[:, 2 * t + g:2 * t + g + 1]).then_inc(sem("hy_ysq"), 1)

            out_high(0, 0, "hy_trya", "hy_yahi")
            decay(1)
            out_high(1, 0, "hy_trya", "hy_yahi")
            squares(0)
            split_to(u + 21)
            decay(2)
            decay(3)
            split_to(u + 22)
            act.wait_ge(sem("hy_st"), 1)
            act.activation(stT[:, :, :], pair(CT), ACT.Copy).then_inc(sem("hy_stv"), 1)
            out_high(0, 8, "hy_try", "hy_yhi")
            squares(1)
            split_to(u + 24)
            out_high(1, 8, "hy_try", "hy_yhi")
            split_to(u + 26)

        def hyb_dve(dve, s, done, split_to):
            u = first[s]

            def chain(ins):
                link(dve, "dve_chain", ins)

            def conv_input(j):
                dve.wait_ge(sem("hy_trx"), j + 1)
                dve.tensor_copy(cx[:, 4 * j:4 * j + 4, 3:3 + SEQ], PS[:, CT:CT + 2, :]
                                .rearrange("p a (k n) -> p (a k) n", n=SEQ)).then_inc(sem("hy_cx"), 1)

            def taps(j, which):
                if which[0] == 1:
                    dve.wait_ge(sem("hy_t0"), j + 1)
                    dve.wait_ge(sem("hy_cx"), j + 1)
                    dve.wait_ge(sem("hy_pad"), 1)
                for tap in which:
                    for q in range(4):
                        c = 4 * j + q
                        ins = dve.scalar_tensor_tensor(ca[:, q, :], cx[:, c, tap:tap + SEQ], CW[:, 4 * c + tap:4 * c + tap + 1],
                                                       ca[:, q, :], ALU.mult, ALU.add)
                    if tap < 3:
                        chain(ins)
                    else:
                        ins.then_inc(sem("hy_ca"), 1)

            def segment(t, g):
                n = 2 * t + g
                dve.wait_ge(sem("hy_abc"), n + 1)
                if n == 1:
                    dve.wait_ge(sem("hy_mv"), 2)
                if n >= 2:
                    dve.wait_ge(sem("hy_yd"), n - 1)
                c = t * HEADS + g * GH
                chain(dve.tensor_tensor(Eg[:, g, :, :], flat_pair(CT).rearrange("p (h l) -> p h l", h=GH),
                                        per_head(ACS[:, c:c + GH], GH, P), ALU.subtract))
                dve.tensor_scalar(Eg[:, g, :, :], Eg[:, g, :, :], 0.0, None, ALU.min).then_inc(sem("hy_seg"), 1)

            def weigh(t, g):
                n = 2 * t + g
                dve.wait_ge(sem("hy_exp"), n + 1)
                dve.tensor_tensor(Eg[:, g, :, :], Eg[:, g, :, :],
                                  cbm[:, n, :].unsqueeze(1).broadcast_to([P, GH, P]), ALU.mult)\
                   .then_inc(sem("hy_G"), 1)

            def times_dt(t):
                dve.wait_ge(sem("hy_xs"), t + 1)
                dve.tensor_tensor(heads(xd[:, t, :]), heads(flat_pair(CT)),
                                  per_head(DT[:, t * HEADS:(t + 1) * HEADS], HEADS, 64), ALU.mult)\
                   .then_inc(sem("hy_xd"), 1)

            def head_statistics(c):
                for r in range(8):
                    ins = dve.bn_stats(BN[:, 6 * r:6 * r + 6], vt[:, c, r * P:(r + 1) * P])
                chain(ins)
                for r in range(8):
                    ins = dve.bn_aggr(MV[:, 2 * r:2 * r + 2], BN[:, 6 * r:6 * r + 6])
                ins.then_inc(sem("hy_mv"), 1)

            def normalise(c):
                dve.wait_ge(sem("hy_mv"), c + 1)
                dve.wait_ge(sem("hy_rv"), c + 1)
                for r in range(8):
                    v = vt[:, c, r * P:(r + 1) * P]
                    ins = dve.tensor_scalar(v, v, MV[:, 2 * r:2 * r + 1], RV[:, r:r + 1], ALU.subtract, ALU.mult)
                ins.then_inc(sem("hy_vn"), 1)
                dve.wait_ge(sem("hy_vn"), c + 1)

            def gate_v(c):
                dve.wait_ge(sem("hy_mix"), c + 1)
                b = (P1, P2)[c]
                dve.tensor_tensor(heads(vt[:, c, :], 8), heads(flat_pair(b), 8), per_head(BS, 8, P), ALU.add)\
                   .then_inc(sem("hy_mixv"), 1)
                dve.wait_ge(sem("hy_mixv"), c + 1)
                dve.wait_ge(sem("hy_ev"), 9)
                v = vt[:, c, :].rearrange("p (a n) -> p a n", a=2)
                dve.tensor_tensor(v, v, ug[:, :, c, :], ALU.mult).then_inc(sem("hy_ya"), 1)

            def out_low(t, base, hi, lo):
                dve.wait_ge(sem(hi), t + 1)
                dve.tensor_tensor(CL[:, base:base + 8, tok(t)], pair(CT).rearrange("p a (k n) -> p (a k) n", n=P),
                                  CH[:, base:base + 8, tok(t)], ALU.subtract).then_inc(sem(lo), 1)

            def gated(t):
                dve.wait_ge(sem("hy_yd"), 2 * t + 2)
                dve.wait_ge(sem("hy_skip"), t + 1)
                dve.tensor_tensor(xs[:, t, :], flat_pair(P0), xs[:, t, :], ALU.add).then_inc(sem("hy_y"), 1)
                if t:
                    dve.wait_ge(sem("hy_y"), 3)
                    chain(dve.tensor_tensor(xs[:, t, :], xs[:, t, :], yo[:, :], ALU.add))
                else:
                    dve.wait_ge(sem("hy_y"), 1)
                dve.tensor_tensor(xs[:, t, :], xs[:, t, :], zs[:, t, :], ALU.mult).then_inc(sem("hy_y"), 1)

            split_to(u + 2)
            dve.wait_ge(sem("hy_dth"), 1)
            dve.tensor_tensor(dt_lo[:, :, :], dt_w[:, :, :], dt_hi[:, :, :], ALU.subtract).then_inc(sem("hy_dtl"), 1)
            split_to(u + 6)
            conv_input(0)
            taps(0, (1,))
            split_to(u + 7)
            taps(0, (2, 3))
            split_to(u + 8)
            conv_input(1)
            taps(1, (1,))
            split_to(u + 9)
            taps(1, (2, 3))
            dve.wait_ge(sem("hy_dtp"), 1)
            dve.tensor_copy(dtT[:, :], PS[0:HEADS, P1, 0:SEQ]).then_inc(sem("hy_dtc"), 1)
            split_to(u + 10)
            conv_input(2)
            taps(2, (1,))
            dve.wait_ge(sem("hy_dtt"), 1)
            dve.wait_ge(sem("pre_rs"), 2 * s + 2)
            for t in range(2):
                hs = slice(t * HEADS, (t + 1) * HEADS)
                ins = dve.scalar_tensor_tensor(X0[:, hs], PS[:, P1, hs], col(s, t, RS), DTB, ALU.mult, ALU.add)
            ins.then_inc(sem("hy_dtv"), 1)
            dve.wait_ge(sem("hy_dtv"), 1)
            dve.scalar_tensor_tensor(NA, X0, -1.0, X0, ALU.mult, ALU.min).then_inc(sem("hy_na"), 1)
            split_to(u + 11)
            dve.wait_ge(sem("hy_ex"), 1)
            chain(dve.tensor_scalar(S1, EX, 2.0, None, ALU.add))
            chain(dve.reciprocal(S1, S1))
            chain(dve.tensor_tensor(S1, S1, EX, ALU.mult))
            chain(dve.tensor_tensor(S2, S1, S1, ALU.mult))
            terms = [2.0 / (2 * i + 1) for i in range(9)]
            chain(dve.tensor_scalar(PO, S2, terms[8], None, ALU.mult))
            for c in terms[7:0:-1]:
                chain(dve.scalar_tensor_tensor(PO, PO, c, S2, ALU.add, ALU.mult))
            chain(dve.scalar_tensor_tensor(PO, PO, terms[0], S1, ALU.add, ALU.mult))
            chain(dve.scalar_tensor_tensor(DT, X0, 0.0, PO, ALU.max, ALU.add))
            dve.wait_ge(sem("hy_al"), 1)
            dve.scalar_tensor_tensor(DA.rearrange("p (t h) -> p t h", t=2), DT.rearrange("p (t h) -> p t h", t=2), -1.0,
                                     NEGA.unsqueeze(1).broadcast_to([P, 2, HEADS]), ALU.mult, ALU.mult)\
               .then_inc(sem("hy_da"), 1)
            split_to(u + 12)
            taps(2, (2, 3))
            dve.wait_ge(sem("hy_acs"), 1)
            dve.tensor_copy(ACS, PS[:, C, 0:48]).then_inc(sem("hy_acv"), 1)
            dve.wait_ge(sem("hy_acv"), 1)
            dve.tensor_tensor(DTE, ACS[:, 32:48], ACS[:, 0:HEADS], ALU.subtract).then_inc(sem("hy_dea"), 1)
            split_to(u + 13)
            split_to(u + 14)
            times_dt(0)
            dve.wait_ge(sem("hy_xd"), 1)
            dve.wait_ge(sem("hy_dte"), 1)
            dve.tensor_tensor(heads(xde[:, :]), heads(xd[:, 0, :]), per_head(DTE, HEADS, 64), ALU.mult)
            split_to(u + 15)
            split_to(u + 16)
            times_dt(1)
            dve.wait_ge(sem("hy_ev"), 7)
            head_statistics(0)
            split_to(u + 17)
            dve.wait_ge(sem("hy_bc"), 1)
            dve.tensor_tensor(cbm[:, :, :], PS[:, T, :].rearrange("p (n l) -> p n l", l=P),
                              tri[:, :].unsqueeze(1).broadcast_to([P, 4, P]), ALU.mult).then_inc(sem("hy_cbm"), 1)
            normalise(0)
            head_statistics(1)
            segment(0, 0)
            normalise(1)
            gate_v(0)
            segment(0, 1)
            weigh(0, 0)
            split_to(u + 18)
            out_low(0, 0, "hy_yahi", "hy_yalo")
            weigh(0, 1)
            gate_v(1)
            split_to(u + 19)
            out_low(1, 0, "hy_yahi", "hy_yalo")
            gated(0)
            split_to(u + 20)
            segment(1, 0)
            split_to(u + 21)
            weigh(1, 0)
            segment(1, 1)
            weigh(1, 1)

            def normalise_y(t):
                if t == 0:
                    dve.wait_ge(sem("hy_ng"), 16)
                dve.wait_ge(sem("hy_yrs"), t + 1)
                for g in range(2):
                    y = xs[:, t, g * BANK:(g + 1) * BANK]
                    ins = dve.scalar_tensor_tensor(y, y, GQ[:, 4 + 2 * t + g:5 + 2 * t + g], ng[:, g * BANK:(g + 1) * BANK],
                                                   ALU.mult, ALU.mult)
                ins.then_inc(sem("hy_yn"), 1)

            split_to(u + 22)
            normalise_y(0)
            dve.wait_ge(sem("hy_yo"), 1)
            dve.tensor_tensor(heads(yo[:, :]), heads(flat_pair(CT)), per_head(EA, HEADS, 64), ALU.mult)\
               .then_inc(sem("hy_yoff"), 1)
            dve.wait_ge(sem("hy_yoff"), 1)
            gated(1)
            out_low(0, 8, "hy_yhi", "hy_ylo")
            normalise_y(1)
            split_to(u + 23)
            split_to(u + 24)
            out_low(1, 8, "hy_yhi", "hy_ylo")
            split_to(u + 25)

        def hyb_early(pool):
            pool.dma_start(dt_w[:, :, :], a["dt_w"]).then_inc(sem("hy_dtw"), 16)
            pool.dma_start(sm[:, 0:68], a["hy_cols"]).then_inc(sem("hy_small"), 16)
            pool.dma_start(sm[:, 68:116], a["hy_rows"].partition_broadcast(P)).then_inc(sem("hy_small"), 16)
            pool.dma_start(wsT[:, :, :], a["gm_w"]).then_inc(sem("hy_ws"), 16)
            pool.wait_ge(sem("hy_ws"), 16)
            pool.tensor_tensor(wsT[:, :, :], wsT[:, :, :], tri[:, :].unsqueeze(1).broadcast_to([P, 8, P]), ALU.mult)\
                .then_inc(sem("hy_wsm"), 1)

        def hyb_pool(pool, s):
            if s == 0:
                hyb_early(pool)
            pool.memset(cx[:, :, 0:3], 0.0).then_inc(sem("hy_pad"), 1)
            pool.dma_start(gm_g[:, :], a["gm_g"].partition_broadcast(P)).then_inc(sem("hy_gm"), 16)
            pool.dma_start(gm_b[:, :], a["gm_b"].partition_broadcast(P)).then_inc(sem("hy_gm"), 16)
            for t in range(2):
                pool.wait_ge(sem("hy_xs"), t + 1)
                pool.tensor_tensor(heads(xs[:, t, :]), heads(xs[:, t, :]), per_head(DV, HEADS, 64), ALU.mult)\
                    .then_inc(sem("hy_skip"), 1)
            for c in range(2):
                pool.wait_ge(sem("hy_mv"), c + 1)
                if c:
                    pool.wait_ge(sem("hy_vn"), 1)
                link(pool, "pool_chain", pool.tensor_scalar(RV, MV.rearrange("p (h q) -> p h q", q=2)[:, :, 1], LN_EPS, None,
                                                            ALU.add))
                pool.tensor_tensor(RV, RV, nhalf[:, :], ALU.pow).then_inc(sem("hy_rv"), 1)
                if c == 0:
                    pool.wait_ge(sem("hy_gm"), 32)
                pool.wait_ge(sem("hy_vn"), c + 1)
                link(pool, "pool_chain", pool.tensor_tensor(vt[:, c, :], vt[:, c, :], gm_g[:, :], ALU.mult))
                pool.tensor_tensor(vt[:, c, :], vt[:, c, :], gm_b[:, :], ALU.add).then_inc(sem("hy_v"), 1)
            pool.wait_ge(sem("w_used"), first[s] + 18)
            pool.dma_start(ng[:, :], a["ssd_g"].partition_broadcast(P)).then_inc(sem("hy_ng"), 16)
            for t in range(2):
                pool.wait_ge(sem("hy_ysq"), 2 * t + 2)
                ms, rs = GQ[:, 2 * t:2 * t + 2], GQ[:, 4 + 2 * t:6 + 2 * t]
                link(pool, "pool_chain", pool.tensor_scalar(rs, ms, 1.0 / 512, EPS, ALU.mult, ALU.add))
                pool.tensor_tensor(rs, rs, nhalf[:, 0:2], ALU.pow).then_inc(sem("hy_yrs"), 1)


        HALF = ROPE // 2
        kT = place("kT", [P, HEADS, SEQ], offset=x_at)
        o = s_at
        qT = place("qT", [P, HEADS, SEQ], offset=o); o += 16384
        vv = place("vv", [P, 2, HEADS * VD], offset=o); o += 16384
        qrT = place("qrT", [P, 8, SEQ], offset=o); o += 8192
        krT = place("krT", [P, SEQ], offset=o); o += 1024
        pr = place("pr", [P, 2, 3 * P], offset=o); o += 3072
        pT = place("pT", [P, 2, 3 * P], offset=o); o += 3072
        msm = place("msm", [P, 256], offset=o); o += 1024
        assert o <= end, o
        qr = hn
        cn = place("cn", [P, 2, BANK], offset=c_at)
        cTH = place("cTH", [P, 3, SEQ], f32r, offset=c_at + 4096)
        cTL = place("cTL", [P, 3, SEQ], f32r, offset=c_at + 4096 + 3072)
        cg = place("cg", [P, Q_LORA + KV_LORA], offset=c_at + 10240)
        ra = place("ra", [P, HEADS, HALF], offset=c_at + 12288)
        rb = place("rb", [P, HEADS, HALF], offset=c_at + 14336)
        rc = place("rc", [P, HEADS, HALF], offset=c_at + 16384)
        rd = place("rd", [P, HEADS, HALF], offset=c_at + 18432)

        LSQ, LRS = msm[:, 0:4], msm[:, 4:8]
        NMX, SUM = msm[:, 8:72], msm[:, 72:136]
        MAXS = msm[:, 136:200]

        for name in ("ml_in", "ml_half", "ml_cg", "ml_sq", "ml_rs", "ml_cn", "ml_tr", "ml_chi", "ml_clo", "ml_krT", "ml_pa",
                     "ml_pv", "ml_S", "ml_mx", "ml_nm", "ml_exp", "ml_P", "ml_PT", "ml_PTe", "ml_O", "ml_Ohi", "ml_Olo",
                     "ml_qr", "ml_qrt", "rope_pos", "rope_arg", "rope_sin", "rope_done", "ml_X", "ml_XA", "ml_XD"):
            sem(name)

        PA, PB, PC, PD = (4, 5), (6, 7), (0, 1), (2, 3)
        ROPE0, V00, V01, ROPE1, V10, V11, K0, K1, K2, K3, Q0, Q1, R0, R1, Q2, Q3 = range(16)
        PIECES = [(PA, "turn", None), (PB, "act", None), (PC, "act", None), (PD, "turn", 2), (PB, "act", None),
                  (PC, "act", 3), (PA, "act", None), (PB, "dve", None), (PC, "act", None), (PD, "dve", 4),
                  (PA, "act", None), (PB, "dve", 5), (PC, "act", None), (PD, "dve", None), (PA, "act", None),
                  (PB, "dve", 6)]
        DONE = {"turn": "ml_qr", "act": "ml_XA", "dve": "ml_XD"}

        def piece_view(n):
            lo = PIECES[n][0][0]
            return PS[:, lo:lo + 2, :]

        def piece_emptied(pe, n):
            for m in range(n - 1, -1, -1):
                if PIECES[m][0] == PIECES[n][0]:
                    who = PIECES[m][1]
                    pe.wait_ge(sem(DONE[who]), sum(PIECES[i][1] == who for i in range(m + 1)))
                    return

        def piece_ready(eng, s, n):
            if PIECES[n][2] is None:
                eng.wait_ge(sem("ml_X"), sum(PIECES[i][2] is None for i in range(n + 1)))
            else:
                eng.wait_ge(sem("w_used"), first[s] + PIECES[n][2] + 1)

        def piece_filled(ins, n):
            ins.then_inc(sem("ml_X" if PIECES[n][2] is None else "w_used"), 1)

        def mla_pe(pe, s):
            u = first[s]

            def transpose_latents(t):
                pe.wait_ge(sem("ml_cn"), t + 1)
                for q in range(4):
                    ins = pe.transpose(PS[:, 2 * t + 1, q * P:(q + 1) * P], cn[:, t, q * P:(q + 1) * P], ident[:, :])
                ins.then_inc(sem("ml_tr"), 1)

            for j, t in lagged(range(2)):
                if (j, t) == (0, 1):
                    transpose_x(pe, s, 1, (1,))
                split_done(pe, u + j)
                wh = whole(WH, u + j).rearrange("p (k n) -> p k n", k=4)
                wl = whole(WL, u + j).rearrange("p (k n) -> p k n", k=4)
                x_there(pe, s, t, j)
                for q in range(4):
                    if (j, t, q) == (1, 0, 3):
                        transpose_x(pe, s, 1, (0,))
                    if (j, t, q) == (1, 1, 3):
                        transpose_latents(0)
                    kt = 4 * j + q
                    ins = product(pe, PS[:, 2 * t, 0:448], XH[:, kt, tok(t)], XL[:, kt, tok(t)],
                                  wh[:, q, 0:448], wl[:, q, 0:448], kt == 0, kt == KT - 1)
                if t == 1:
                    ins.then_inc(sem("w_used"), 1)
                elif j == 1:
                    ins.then_inc(sem("ml_in"), 1)
            def rope_queries(t):
                n = (ROPE0, ROPE1)[t]
                pe.wait_ge(sem("ml_krT"), t + 1)
                split_done(pe, u + 2)
                wh = whole(WH, u + 2).rearrange("p (k n) -> p k n", k=2)
                wl = whole(WL, u + 2).rearrange("p (k n) -> p k n", k=2)
                for c in range(2):
                    for q in range(2):
                        ins = product(pe, PS[:, PIECES[n][0][c], :], cTH[:, q, tok(t)], cTL[:, q, tok(t)],
                                      wh[:, q, c * BANK:(c + 1) * BANK], wl[:, q, c * BANK:(c + 1) * BANK],
                                      q == 0, q == 1)
                piece_filled(ins, n)

            def values(t, part):
                n = ((V00, V01), (V10, V11))[t][part]
                piece_emptied(pe, n)
                split_done(pe, u + 3)
                for c in range(2):
                    cols = slice((2 * part + c) * BANK, (2 * part + c + 1) * BANK)
                    ins = product(pe, PS[:, PIECES[n][0][c], :], cTH[:, 2, tok(t)], cTL[:, 2, tok(t)],
                                  whole(WH, u + 3)[:, cols], whole(WL, u + 3)[:, cols], True, True)
                piece_filled(ins, n)

            def turned(n, unit, kts, h0, base):
                piece_emptied(pe, n)
                split_done(pe, unit)
                wh = whole(WH, unit).rearrange("p (k n) -> p k n", k=kts)
                wl = whole(WL, unit).rearrange("p (k n) -> p k n", k=kts)
                for r in range(4):
                    out_ap = PS[:, PIECES[n][0][r // 2], (r % 2) * SEQ:(r % 2 + 1) * SEQ]
                    w = slice((h0 + r) * P, (h0 + r + 1) * P)
                    for q in range(kts):
                        ins = product(pe, out_ap, wh[:, q, w], wl[:, q, w], cTH[:, base + q, :], cTL[:, base + q, :],
                                      q == 0, q == kts - 1)
                piece_filled(ins, n)

            def transpose_ropes(part):
                n = (R0, R1)[part]
                piece_emptied(pe, n)
                for r in range(4):
                    for t in range(2):
                        w = (4 * part + r) * P
                        ins = pe.transpose(PS[:, PIECES[n][0][r // 2], (r % 2) * SEQ + t * P:(r % 2) * SEQ + (t + 1) * P],
                                           qr[:, t, w:w + P], ident[:, :])
                piece_filled(ins, n)

            rope_queries(0)
            values(0, 0)
            transpose_latents(1)
            values(0, 1)
            rope_queries(1)
            values(1, 0)
            values(1, 1)
            for i in range(4):
                turned(K0 + i, u + 4, 1, 4 * i, 2)
            turned(Q0, u + 5, 2, 0, 0)
            turned(Q1, u + 5, 2, 4, 0)
            transpose_ropes(0)
            transpose_ropes(1)
            turned(Q2, u + 6, 2, 0, 0)

            def scores(hd):
                if hd >= 2:
                    pe.wait_ge(sem("ml_mx"), hd - 1)
                lo = (hd % 2) * 64
                for t in range(2):
                    n = (t + 1) * P
                    dst = PS[:, hd % 2, t * P:t * P + n]
                    pe.matmul(dst, qT[:, hd, tok(t)], kT[:, hd, 0:n], start=True, stop=False)
                    ins = pe.matmul(dst, qrT[lo:lo + 64, hd // 2, tok(t)], krT[lo:lo + 64, 0:n], start=False, stop=True)
                ins.then_inc(sem("ml_S"), 1)

            def transpose_probabilities(hd):
                pe.wait_ge(sem("ml_P"), hd + 1)
                if hd:
                    pe.wait_ge(sem("ml_PTe"), hd)
                for q in range(3):
                    ins = pe.transpose(PS[:, C, q * P:(q + 1) * P], pr[:, hd % 2, q * P:(q + 1) * P], ident[:, :])
                ins.then_inc(sem("ml_PT"), 1)

            def weighted_values(hd):
                pe.wait_ge(sem("ml_PTe"), hd + 1)
                if hd % 2 == 0 and hd:
                    pe.wait_ge(sem("ml_Olo"), hd // 2)
                lo = (hd % 2) * SEQ
                w = slice(hd * VD, (hd + 1) * VD)
                pe.matmul(PS[:, T, lo:lo + SEQ], vv[:, 0, w], pT[:, hd % 2, 0:SEQ], start=True, stop=False)
                ins = pe.matmul(PS[:, T, lo + P:lo + SEQ], vv[:, 1, w], pT[:, hd % 2, SEQ:3 * P], start=False, stop=True)
                ins.then_inc(sem("ml_O"), 1)

            def out_unit(j, t):
                pe.wait_ge(sem("ml_Olo"), j + 1)
                wide(pe, u + 7 + j, t, 4 + 2 * t, CH, CL, 2 * j, j == 0, j == 7, "out_done" if j == 7 else None,
                     middle=next_x(pe, s) if (j, t) == (7, 1) else None)

            def wait_emptied(upto):
                pe.wait_ge(sem("ml_XA"), sum(who == "act" for _, who, _ in PIECES[:upto + 1]))
                pe.wait_ge(sem("ml_XD"), sum(who == "dve" for _, who, _ in PIECES[:upto + 1]))

            wait_emptied(R0)
            scores(0)
            scores(1)
            turned(Q3, u + 6, 2, 4, 0)
            wait_emptied(R1)
            for j in range(8):
                if j == 1:
                    wait_emptied(Q3)
                transpose_probabilities(2 * j)
                if j < 7:
                    scores(2 * j + 2)
                if j:
                    out_unit(j - 1, 0)
                transpose_probabilities(2 * j + 1)
                if j < 7:
                    scores(2 * j + 3)
                weighted_values(2 * j)
                if j == 7:
                    weighted_values(2 * j + 1)
                if j > 1:
                    out_unit(j - 2, 1)
                if j < 7:
                    weighted_values(2 * j + 1)
            out_unit(7, 0)
            out_unit(6, 1)
            out_unit(7, 1)

        def empty(n, op):
            def four(tile, h0):
                return tile[:, h0:h0 + 4, :].rearrange("p (a h) n -> p a (h n)", a=2)
            if n in (V00, V01, V10, V11):
                t, part = n // V10, n % 2 == (0 if n < V10 else 1)
                dst = vv[:, t, part * 1024:(part + 1) * 1024].rearrange("p (a n) -> p a n", a=2)
            elif n < Q0:
                dst = four(kT, 4 * (n - K0))
            elif n in (R0, R1):
                dst = four(qrT, 4 * (n - R0))
            else:
                dst = four(qT, 4 * (Q0, Q1, Q2, Q3).index(n))
            return op(dst, piece_view(n))

        def mla_act(act, s, done, split_to):
            u = first[s]
            split_to(u + 2)

            def latent_squares(t):
                if t == 0:
                    act.wait_ge(sem("ml_in"), 1)
                else:
                    act.wait_ge(sem("w_used"), u + 2)
                act.wait_ge(sem("pre_rs"), 2 * s + t + 1)
                act.activation(junk[:, t, 0:Q_LORA], PS[:, 2 * t, 0:Q_LORA], ACT.Square, scale=col(s, t, RS),
                               accum_out=LSQ[:, t:t + 1])
                act.activation(junk[:, t, Q_LORA:Q_LORA + KV_LORA], PS[:, 2 * t, Q_LORA:Q_LORA + KV_LORA], ACT.Square,
                               scale=col(s, t, RS), accum_out=LSQ[:, 2 + t:3 + t]).then_inc(sem("ml_sq"), 1)

            def latents_high(t):
                act.wait_ge(sem("ml_tr"), t + 1)
                act.activation(cTH[:, :, tok(t)], PS[:, 2 * t + 1, 0:384].rearrange("p (k n) -> p k n", n=P), ACT.Copy)\
                   .then_inc(sem("ml_chi"), 1)

            def take(n):
                piece_ready(act, s, n)
                empty(n, lambda dst, src: act.activation(dst, src, ACT.Copy)).then_inc(sem("ml_XA"), 1)

            x_high(act, s, 1, (0,))
            latent_squares(0)
            x_high(act, s, 1, (1,))
            pre_square(act, s, 1)
            split_to(u + 3)
            latents_high(0)
            latent_squares(1)
            split_to(u + 4)
            take(V00)
            latents_high(1)
            take(V01)
            split_to(u + 5)
            take(V10)
            take(V11)
            take(K0)
            split_to(u + 6)
            take(K2)
            split_to(u + 7)
            take(Q0)
            take(R0)
            take(Q2)
            load_table(act, ACT.Exp)
            split_to(u + 8)

            def exponentials(hd):
                act.wait_ge(sem("ml_nm"), hd + 1)
                for t in range(2):
                    p = pr[:, hd % 2, t * P:t * P + (t + 1) * P]
                    c = 2 * hd + t
                    ins = act.activation(p, p, ACT.Exp, bias=NMX[:, c:c + 1], scale=SCALE, accum_out=SUM[:, c:c + 1])
                ins.then_inc(sem("ml_exp"), 1)

            def copy_pT(hd):
                act.wait_ge(sem("ml_PT"), hd + 1)
                if hd >= 2:
                    act.wait_ge(sem("ml_O"), hd - 1)
                act.activation(pT[:, hd % 2, :], PS[:, C, 0:3 * P], ACT.Copy).then_inc(sem("ml_PTe"), 1)

            exponentials(0)
            exponentials(1)
            for j in range(8):
                copy_pT(2 * j)
                if j < 7:
                    exponentials(2 * j + 2)
                split_to(max(u + 7 + j, u + 9))
                copy_pT(2 * j + 1)
                if j < 7:
                    exponentials(2 * j + 3)
                act.wait_ge(sem("ml_O"), 2 * j + 2)
                act.activation(CH[:, 2 * j:2 * j + 2, :], PS[:, T, :].rearrange("p (k n) -> p k n", n=SEQ), ACT.Copy)\
                   .then_inc(sem("ml_Ohi"), 1)
            split_to(u + 15)

        def mla_dve(dve, s, done, split_to):
            u = first[s]

            def rotate(x, y, t, n, tmp):
                c = cosT[:, t, :].unsqueeze(1).broadcast_to([P, n, HALF])
                sn = sinT[:, t, :].unsqueeze(1).broadcast_to([P, n, HALF])
                w, x_, y_, z_ = (m[:, 0:n, :] for m in tmp)
                if n == 1:
                    x0, x1, y0, y1 = x[:, :, 0, :], x[:, :, 1, :], y[:, :, 0, :], y[:, :, 1, :]
                else:
                    def two(v):
                        return v.rearrange("p (b n) h -> p b n h", b=2)
                    c, sn, w, x_, y_, z_ = (two(v) for v in (c, sn, w, x_, y_, z_))
                    x0, x1, y0, y1 = x[:, :, :, 0, :], x[:, :, :, 1, :], y[:, :, :, 0, :], y[:, :, :, 1, :]
                dve.tensor_tensor(w, x0, c, ALU.mult)
                dve.tensor_tensor(x_, x1, sn, ALU.mult)
                dve.tensor_tensor(y_, x1, c, ALU.mult)
                link(dve, "dve_chain", dve.tensor_tensor(z_, x0, sn, ALU.mult))
                dve.tensor_tensor(y0, w, x_, ALU.subtract)
                return dve.tensor_tensor(y1, y_, z_, ALU.add)

            tmp = (ra, rb, rc, rd)
            def latents(t):
                dve.wait_ge(sem("ml_rs"), t + 1)
                q, kv = slice(0, Q_LORA), slice(Q_LORA, Q_LORA + KV_LORA)
                dve.scalar_tensor_tensor(cn[:, t, q], PS[:, 2 * t, q], LRS[:, t:t + 1], cg[:, q], ALU.mult, ALU.mult)
                dve.scalar_tensor_tensor(cn[:, t, kv], PS[:, 2 * t, kv], LRS[:, 2 + t:3 + t], cg[:, kv], ALU.mult, ALU.mult)
                kr = ra[:, 2 + 2 * t:4 + 2 * t, :]
                link(dve, "dve_chain", rotate(PS[:, 2 * t, 384:448].rearrange("p (n a h) -> p n a h", n=1, a=2),
                                              kr.unsqueeze(1), t, 1, tmp))
                for twice in range(2):
                    lo = 384 + 64 * twice
                    ins = dve.tensor_scalar(cn[:, t, lo:lo + 64], kr.rearrange("p a h -> p (a h)"), col(s, t, RS), None,
                                            ALU.mult)
                ins.then_inc(sem("ml_cn"), 1)

            def latents_low(t):
                dve.wait_ge(sem("ml_chi"), t + 1)
                dve.tensor_tensor(cTL[:, :, tok(t)], PS[:, 2 * t + 1, 0:384].rearrange("p (k n) -> p k n", n=P),
                                  cTH[:, :, tok(t)], ALU.subtract)
                dve.tensor_copy(krT[:, tok(t)], PS[:, 2 * t + 1, 384:512]).then_inc(sem("ml_krT"), 1)

            def turn(t):
                n = (ROPE0, ROPE1)[t]
                piece_ready(dve, s, n)
                rotate(piece_view(n).rearrange("p b (n a h) -> p b n a h", a=2, h=HALF),
                       qr[:, t, :].rearrange("p (b n a h) -> p b n a h", b=2, a=2, h=HALF), t, HEADS, tmp)\
                    .then_inc(sem("ml_qr"), 1)
                dve.wait_ge(sem("ml_qr"), t + 1)

            def take(n):
                piece_ready(dve, s, n)
                empty(n, dve.tensor_copy).then_inc(sem("ml_XD"), 1)

            def maxima(hd):
                dve.wait_ge(sem("ml_S"), hd + 1)
                if hd >= 2:
                    dve.wait_ge(sem("ml_PT"), hd - 1)
                for t in range(2):
                    c = 2 * hd + t
                    n = (t + 1) * P
                    ins = dve.tensor_tensor_reduce(out=pr[:, hd % 2, t * P:t * P + n], in0=PS[:, hd % 2, t * P:t * P + n],
                                                   in1=cmask[:, 2 * P - n:2 * P], scale=1.0, scalar=-3.0e38, op0=ALU.add,
                                                   op1=ALU.max, accum_out=MAXS[:, c:c + 1])
                ins.then_inc(sem("ml_mx"), 1)
                dve.wait_ge(sem("ml_mx"), hd + 1)
                dve.tensor_scalar(NMX[:, 2 * hd:2 * hd + 2], MAXS[:, 2 * hd:2 * hd + 2], -SCALE, None, ALU.mult)\
                   .then_inc(sem("ml_nm"), 1)

            def normalise(hd):
                dve.wait_ge(sem("ml_exp"), hd + 1)
                r = SUM[:, 2 * hd:2 * hd + 2]
                link(dve, "dve_chain", dve.reciprocal(r, r))
                for t in range(2):
                    p = pr[:, hd % 2, t * P:t * P + (t + 1) * P]
                    c = 2 * hd + t
                    ins = dve.tensor_scalar(p, p, SUM[:, c:c + 1], None, ALU.mult)
                ins.then_inc(sem("ml_P"), 1)

            dve.wait_ge(sem("ml_cg"), 32)
            latents(0)
            dve.wait_ge(sem("ml_half"), 1)
            split_lo_half(dve, u + 2, 1).then_inc(sem("w_lo"), 1)
            done[0] = u + 3
            latents_low(0)
            split_to(u + 3)
            latents(1)
            split_to(u + 4)
            latents_low(1)
            turn(0)
            turn(1)
            split_to(u + 5)
            take(K1)
            take(K3)
            split_to(u + 6)
            take(Q1)
            split_to(u + 7)
            take(R1)
            maxima(0)
            maxima(1)
            normalise(0)
            normalise(1)
            take(Q3)
            for j in range(8):
                if j < 7:
                    maxima(2 * j + 2)
                    normalise(2 * j + 2)
                split_to(max(u + 7 + j, min(u + 8 + j, u + 9)))
                if j < 7:
                    maxima(2 * j + 3)
                    normalise(2 * j + 3)
                dve.wait_ge(sem("ml_Ohi"), j + 1)
                dve.tensor_tensor(CL[:, 2 * j:2 * j + 2, :], PS[:, T, :].rearrange("p (k n) -> p k n", n=SEQ),
                                  CH[:, 2 * j:2 * j + 2, :], ALU.subtract).then_inc(sem("ml_Olo"), 1)
            split_to(u + 14)

        def mla_early(pool):
            pool.dma_start(cg[:, 0:Q_LORA], a["q_g"].partition_broadcast(P)).then_inc(sem("ml_cg"), 16)
            pool.dma_start(cg[:, Q_LORA:Q_LORA + KV_LORA], a["kv_g"].partition_broadcast(P)).then_inc(sem("ml_cg"), 16)

        def mla_pool(pool, s):
            for t in range(2):
                pool.wait_ge(sem("ml_sq"), t + 1)
                pool.tensor_scalar(LRS[:, t:t + 1], LSQ[:, t:t + 1], 1.0 / Q_LORA, EPS, ALU.mult, ALU.add)
                link(pool, "pool_chain", pool.tensor_scalar(LRS[:, 2 + t:3 + t], LSQ[:, 2 + t:3 + t], 1.0 / KV_LORA, EPS,
                                                            ALU.mult, ALU.add))
                both = LRS[:, t:t + 3:2]
                link(pool, "pool_chain", pool.tensor_tensor(both, both, nhalf[:, 0:2], ALU.pow))
                pool.tensor_scalar(both, both, col(s, t, RS), None, ALU.mult).then_inc(sem("ml_rs"), 1)
                if t == 0:
                    split_lo_half(pool, first[s] + 2, 0).then_inc(sem("ml_half"), 1)
                    inverse_rms(pool, s, 1)

        r_at = s_at + 16384
        rp = place("rp", [P, 2], i32, offset=r_at)
        rf = place("rf", [P, 2], offset=r_at + 32)
        inv = place("inv", [P, HALF], offset=r_at + 64)
        ang = place("ang", [P, 2, HALF], offset=r_at + 256)
        turns = place("turns", [P, 2, HALF], offset=r_at + 512)
        sh = place("sh", [P, 2, HALF], offset=r_at + 768)
        parts, rest = [], 2 * np.pi
        for bits in (8, 8, 8):
            unit = 2.0 ** (np.floor(np.log2(rest)) - bits + 1)
            parts.append(float(np.floor(rest / unit) * unit))
            rest -= parts[-1]
        parts.append(float(rest))
        MAGIC = 1.5 * 2.0 ** 23
        LIMIT = 3.1415925

        def prelude_pool(pool):
            if not has_mla:
                return
            pool.dma_start(rp[:, :], a["positions"]).then_inc(sem("rope_pos"), 16)
            pool.dma_start(inv[:, :], a["inv"].partition_broadcast(P)).then_inc(sem("rope_pos"), 16)

        def prelude_act(act):
            if not has_mla:
                return
            act.wait_ge(sem("rope_arg"), 1)
            act.activation(sinT[:, :, :], ang[:, :, :], ACT.Sin)
            act.activation(sh[:, :, :], ang[:, :, :], ACT.Sin, scale=0.5).then_inc(sem("rope_sin"), 1)

        def prelude_dve(dve):
            if not has_mla:
                return

            def chain(ins):
                link(dve, "dve_chain", ins)

            dve.wait_ge(sem("rope_pos"), 32)
            chain(dve.tensor_copy(rf[:, :], rp[:, :]))
            for t in range(2):
                ins = dve.tensor_scalar(ang[:, t, :], inv[:, :], rf[:, t:t + 1], None, ALU.mult)
            chain(ins)
            chain(dve.tensor_scalar(turns[:, :, :], ang[:, :, :], float(1 / (2 * np.pi)), MAGIC, ALU.mult, ALU.add))
            chain(dve.tensor_scalar(turns[:, :, :], turns[:, :, :], MAGIC, None, ALU.subtract))
            for part in parts:
                chain(dve.scalar_tensor_tensor(ang[:, :, :], turns[:, :, :], -part, ang[:, :, :], ALU.mult, ALU.add))
            dve.tensor_scalar(ang[:, :, :], ang[:, :, :], LIMIT, -LIMIT, ALU.min, ALU.max).then_inc(sem("rope_arg"), 1)

        def prelude_dve_end(dve):
            if not has_mla:
                return
            dve.wait_ge(sem("rope_sin"), 1)
            link(dve, "dve_chain", dve.tensor_tensor(sh[:, :, :], sh[:, :, :], sh[:, :, :], ALU.mult))
            dve.tensor_scalar(cosT[:, :, :], sh[:, :, :], -2.0, 1.0, ALU.mult, ALU.add).then_inc(sem("rope_done"), 1)

        has_mla = any(kind == "mla" for kind, _ in stages)
        PES = {"ffn": ffn_pe, "ple": ple_pe, "hyb": hyb_pe, "mla": mla_pe}
        ACTS = {"ffn": ffn_act, "ple": ple_act, "hyb": hyb_act, "mla": mla_act}
        DVES = {"ffn": ffn_dve, "ple": ple_dve, "hyb": hyb_dve, "mla": mla_dve}
        POOL = {"ffn": ffn_pool, "ple": lambda pool, s: None, "hyb": hyb_pool, "mla": mla_pool}

        block = ctx.enter_context(nc.Block())

        @block.sync
        def _(sp):
            sp.dma_start(h[:, 0, :], a["x"][tok(0), :]).then_inc(sem("x_loaded0"), 16)
            load_unit(sp, 0)
            load_unit(sp, 1)
            sp.dma_start(h[:, 1, :], a["x"][tok(1), :]).then_inc(sem("x_loaded1"), 16)
            for n in range(2, 2 * RING):
                load_unit(sp, n)
            rounds = (n_units - 2 * RING) // RING
            with sp.Fori(0, rounds) as k:
                for j in range(RING):
                    load_unit(sp, 2 * RING + j, k, RING)
            for n in range((2 + rounds) * RING, n_units):
                load_unit(sp, n)
            for t in range(2):
                for b in range(2):
                    h_ready(sp, NS, t, b)
                    sp.dma_start(out[tok(t), half(b)], h[:, t, half(b)]).then_inc(sem("stored"), 16)
            sp.wait_ge(sem("stored"), 64)

        @block.gpsimd
        def _(pool):
            pool.dma_start(QG[:, :], a["pre_g"][0, :].partition_broadcast(P)).then_inc(sem("qg"), 16)
            pool.memset(ident[:, :], 0.0)
            pool.memset(tri[:, :], 1.0)
            pool.memset(cmask[:, :], 0.0)
            pool.memset(zeros[:, :], 0.0)
            link(pool, "pool_chain", pool.memset(nhalf[:, :], -0.5))
            pool.affine_select(out=ident[:, :], in_=ident[:, :], compare_op=ALU.not_equal, fill=1.0, base=0,
                               pattern=[[-1, P]], channel_multiplier=1)
            pool.affine_select(out=tri[:, :], in_=tri[:, :], compare_op=ALU.is_ge, fill=0.0, base=0,
                               pattern=[[1, P]], channel_multiplier=-1)
            pool.affine_select(out=cmask[:, P:2 * P], in_=cmask[:, P:2 * P], compare_op=ALU.is_ge, fill=NEG,
                               base=0, pattern=[[-1, P]], channel_multiplier=1).then_inc(sem("consts"), 1)
            prelude_pool(pool)
            for s, (kind, _) in enumerate(stages):
                boundary_pool(pool, s)
                if kind != "mla":
                    load_gains(pool, s)
                POOL[kind](pool, s)
                if kind == "mla":
                    load_gains(pool, s)
            boundary_pool(pool, NS)

        @block.scalar
        def _(act):
            done, split_to = splitter(act, split_hi)
            split_to(0)
            for s, (kind, _) in enumerate(stages):
                boundary_act(act, s, split_to)
                ACTS[kind](act, s, done, split_to)
            boundary_act(act, NS, split_to)

        @block.vector
        def _(dve):
            done, split_to = splitter(dve, split_lo)
            for s, (kind, _) in enumerate(stages):
                boundary_dve(dve, s, done, split_to)
                DVES[kind](dve, s, done, split_to)
            boundary_dve(dve, NS, done, split_to)

        def idle_products(pe, n):
            for _ in range(n):
                pe.matmul(PS[:, 7, :], zeros[:, 0:P], zeros[:, :], start=True, stop=True)

        @block.tensor
        def _(pe):
            pe.wait_ge(sem("consts"), 1)
            idle_products(pe, 16)
            for s, (kind, _) in enumerate(stages):
                if s == 0 or stages[s - 1][0] == "ple":
                    transpose_x(pe, s, 0)
                if s == 0:
                    idle_products(pe, 4)
                PES[kind](pe, s)


def units_of(w, kts, cols):
    K, N = w.shape
    v = w.reshape(K // (kts * P), kts, P, N // cols, cols)
    return v.transpose(3, 0, 2, 1, 4).reshape(-1, P, kts * cols)


def ffn_units(w_in, w_down):
    gate, up = w_in[:, :D_FF], w_in[:, D_FF:]
    whole = FULL * CHUNK
    out, down = [], units_of(w_down, 2, D)
    for c in range(FULL):
        for w in (gate, up):
            out.append(units_of(w[:, c * CHUNK:(c + 1) * CHUNK], 4, CHUNK))
        if c:
            out.append(down[2 * (c - 1):2 * c])
    for w in (gate, up):
        out.append(units_of(w[:, whole:], 8, CHUNK // 2))
    out += [down[2 * (FULL - 1):2 * FULL], down[2 * FULL:]]
    return out


def hybrid_units(w_in, w_out):
    u, v = w_in[:, :GM_W], w_in[:, GM_W:2 * GM_W]
    z = w_in[:, 2 * GM_W:2 * GM_W + SSD_IN]
    xbc = w_in[:, 2 * GM_W + SSD_IN:2 * GM_W + SSD_IN + CONV_CH]
    return [units_of(c, 4, CHUNK) for c in (xbc, z, v, u)] + [units_of(w_out, 2, D)]


def mla_units(w_in, w_uq, w_ukv, w_out):
    pad = np.zeros((D, BANK - w_in.shape[1]), w_in.dtype)
    q = w_uq.reshape(Q_LORA, HEADS, NOPE + ROPE)
    kv = w_ukv.reshape(KV_LORA, HEADS, NOPE + VD)
    return [units_of(np.concatenate([w_in, pad], axis=1), 4, BANK),
            units_of(q[:, :, NOPE:].reshape(Q_LORA, HEADS * ROPE), 2, D),
            units_of(kv[:, :, NOPE:].reshape(KV_LORA, HEADS * VD), 1, UNIT),
            units_of(kv[:, :, :NOPE].reshape(KV_LORA, HEADS * NOPE), 1, UNIT),
            units_of(q[:, :, :NOPE].reshape(Q_LORA, HEADS * NOPE), 2, D),
            units_of(w_out, 2, D)]


def mixer_arrays(w):
    dt_w = w["hyb_w_in"][0][:, 2 * GM_W + SSD_IN + CONV_CH:]
    conv_w = w["ssd_conv_w"][0].T.reshape(CONV_CH // P, P, 4).transpose(1, 0, 2).reshape(P, -1)
    conv_b = w["ssd_conv_b"][0].reshape(CONV_CH // P, P).T
    inv = np.float32(1.0) / np.float32(ROPE_BASE) ** (np.arange(0, ROPE, 2, dtype=np.float32) / np.float32(ROPE))
    return {
        "dt_w": dt_w.reshape(KT, P, HEADS).transpose(1, 0, 2),
        "hy_cols": np.concatenate([conv_w, conv_b, w["gm_b_s"][0].T], axis=1),
        "hy_rows": np.concatenate([w["ssd_d"][0], w["ssd_dt_bias"][0], w["ssd_a_log"][0]]),
        "gm_w": w["gm_w_s"][0].transpose(2, 0, 1),
        "gm_g": w["gm_ln_g"][0],
        "gm_b": w["gm_ln_b"][0],
        "ssd_g": w["ssd_norm_g"][0],
        "q_g": w["mla_q_norm_g"][0],
        "kv_g": w["mla_kv_norm_g"][0],
        "positions": w["positions"][0].reshape(2, P).T,
        "inv": inv,
    }


def stream_of(stages, w):
    out = []
    for kind, i in stages:
        if kind == "ffn":
            name = "ffn1" if i % 2 == 0 else "ffn2"
            out += ffn_units(w[name + "_w_in"][i // 2], w[name + "_w_down"][i // 2])
        elif kind == "ple":
            out.append(units_of(w["ple_w_proj"][i], 2, D))
            out.append(units_of(w["ple_w_gate"][i], 2, D))
        elif kind == "hyb":
            out += hybrid_units(w["hyb_w_in"][0], w["hyb_w_out"][0])
        else:
            out += mla_units(w["mla_w_in"][0], w["mla_w_uq"][0], w["mla_w_ukv"][0], w["mla_w_out"][0])
    return np.concatenate(out, axis=0)


def gains_of(stages, w, side):
    out = []
    for n, (kind, i) in enumerate(stages):
        name = {"ffn": "ffn1" if i % 2 == 0 else "ffn2", "ple": "ple", "hyb": "mix", "mla": "mix"}[kind]
        layer = i // 2 if kind == "ffn" else 1 if kind == "mla" else i
        out.append(w[f"{name}_{side}_g"][layer])
    return np.stack(out)


def kernel(**inputs):
    import concourse.bacc as _bacc
    from concourse.bass_utils import run_bass_kernel_spmd as _run

    w = {n: np.asarray(v) for n, v in inputs.items()}
    arrays = {
        "x": w["x"][0],
        "stream": stream_of(STAGES, w),
        "pre_g": gains_of(STAGES, w, "pre"),
        "post_g": gains_of(STAGES, w, "post"),
        "p_t": w["p"][:, 0].transpose(0, 2, 1),
    }
    arrays.update(mixer_arrays(w))
    arrays = {n: np.ascontiguousarray(v) for n, v in arrays.items()}
    nc = _bacc.Bacc("TRN2", target_bir_lowering=False, num_devices=1)
    aps = {n: nc.dram_tensor(n, v.shape, mybir.dt.from_np(v.dtype), kind="ExternalInput").ap()
           for n, v in arrays.items()}
    out = nc.dram_tensor("out", (SEQ, D), mybir.dt.float32, kind="ExternalOutput").ap()
    hybrid_trunk(nc, STAGES, aps, out)
    r = _run(nc, [arrays], core_ids=[0])
    return r.results[0]["out"].reshape(1, SEQ, D)
```
